# Optimizing a Trainium2 kernel written in Bass

```python
import math
import jax, jax.numpy as jnp
from jax import lax
import numpy as np
import jax
import jax.numpy as jnp

D_MODEL = 1024
BATCH = 1
SEQ = 256
DEPTH = 2

N_EVEN = (DEPTH + 1) // 2
N_ODD = DEPTH // 2
CONV_WIDTH = 4
NORM_EPS = 1e-6
LRU_WIDTH = D_MODEL
LRU_BLOCKS = 16
LRU_BLOCK = LRU_WIDTH // LRU_BLOCKS
LRU_C = 8.0
SSD_WIDTH = D_MODEL
SSD_HEAD_DIM = 64
SSD_HEADS = SSD_WIDTH // SSD_HEAD_DIM
SSD_GROUPS = 2
SSD_STATE = 128
SSD_CHUNK = 128
SSD_CONV_CH = SSD_WIDTH + 2 * SSD_GROUPS * SSD_STATE
REC_IN = 2 * LRU_WIDTH + SSD_WIDTH + SSD_CONV_CH + SSD_HEADS
REC_OUT = LRU_WIDTH + SSD_WIDTH
ATT_HEADS = 16
ATT_HEAD_DIM = D_MODEL // ATT_HEADS
ATT_WIDTH = ATT_HEADS * ATT_HEAD_DIM
ROPE_DIM = ATT_HEAD_DIM // 4
ROPE_THETA = 500000.0
DILATED_PATTERNS = ((128, 1), (512, 4), (2048, 16))
FFN_HIDDEN = -(-8 * D_MODEL // (3 * 256)) * 256


def rmsnorm(x, g):
    x32 = x.astype(jnp.float32)
    y = x32 * lax.rsqrt(jnp.mean(x32 * x32, axis=-1, keepdims=True) + NORM_EPS)
    return (y * g.astype(jnp.float32)).astype(x.dtype)

def causal_dwconv(x, w, b):
    k = w.shape[0]
    l = x.shape[1]
    xp = jnp.pad(x, ((0, 0), (k - 1, 0), (0, 0)))
    y = b
    for j in range(k):
        y = y + xp[:, j:j + l] * w[j]
    return y

def rg_lru(xc, w_r, b_r, w_i, b_i, lam):
    b, l, w = xc.shape
    xb = xc.reshape(b, l, LRU_BLOCKS, LRU_BLOCK)
    r = jax.nn.sigmoid(jnp.einsum('blhi,hij->blhj', xb, w_r).reshape(b, l, w) + b_r)
    i = jax.nn.sigmoid(jnp.einsum('blhi,hij->blhj', xb, w_i).reshape(b, l, w) + b_i)
    log_a = -LRU_C * r * jax.nn.softplus(-lam)
    a = jnp.exp(log_a)
    u = jnp.sqrt(-jnp.expm1(2.0 * log_a)) * (i * xc)

    def combine(e1, e2):
        a1, h1 = e1
        a2, h2 = e2
        return a1 * a2, a2 * h1 + h2

    _, h = lax.associative_scan(combine, (a, u), axis=1)
    return h

def ssd_chunked(xs, dt, a, bm, cm):
    b, l, nh, p = xs.shape
    g, n = bm.shape[2], bm.shape[3]
    r = nh // g
    c = l // SSD_CHUNK
    t = SSD_CHUNK
    xdt = (xs * dt[..., None]).reshape(b, c, t, g, r, p)
    adt = (dt * a).reshape(b, c, t, g, r)
    bc = bm.reshape(b, c, t, g, n)
    cc = cm.reshape(b, c, t, g, n)
    cs = jnp.cumsum(adt, axis=2)
    seg = cs[:, :, :, None] - cs[:, :, None, :]
    causal = (jnp.arange(t)[:, None] >= jnp.arange(t)[None, :])[:, :, None, None]
    decay = jnp.exp(jnp.where(causal, seg, -jnp.inf))
    cb = jnp.einsum('bclgn,bcsgn->bclsg', cc, bc)
    y_diag = jnp.einsum('bclsgr,bcsgrp->bclgrp', cb[..., None] * decay, xdt)
    decay_to_end = jnp.exp(cs[:, :, -1:] - cs)
    states = jnp.einsum('bcsgn,bcsgrp->bcgrpn', bc, xdt * decay_to_end[..., None])
    chunk_decay = jnp.exp(cs[:, :, -1])

    def step(carry, inp):
        s_c, d_c = inp
        return carry * d_c[..., None, None] + s_c, carry

    init = jnp.zeros((b, g, r, p, n), jnp.float32)
    _, prev = lax.scan(step, init, (jnp.moveaxis(states, 1, 0), jnp.moveaxis(chunk_decay, 1, 0)))
    prev = jnp.moveaxis(prev, 0, 1)
    y_off = jnp.einsum('bclgn,bcgrpn->bclgrp', cc, prev) * jnp.exp(cs)[..., None]
    return (y_diag + y_off).reshape(b, l, nh, p)

def recurrent_layer(x, norm_g, w_in, lru_conv_w, lru_conv_b, lru_w_r, lru_b_r, lru_w_i, lru_b_i,
                    lru_lambda, ssd_conv_w, ssd_conv_b, ssd_dt_bias, ssd_a_log, ssd_d, ssd_norm, w_out):
    f32 = jnp.float32
    b, l, _ = x.shape
    h = rmsnorm(x, norm_g)
    proj = h @ w_in
    s1 = LRU_WIDTH
    s2 = 2 * LRU_WIDTH
    s3 = s2 + SSD_WIDTH
    s4 = s3 + SSD_CONV_CH
    lru_x, lru_gate, z, xbc, dt_raw = jnp.split(proj, [s1, s2, s3, s4], axis=-1)
    xc = causal_dwconv(lru_x, lru_conv_w, lru_conv_b).astype(f32)
    h_lru = rg_lru(xc, lru_w_r.astype(f32), lru_b_r.astype(f32), lru_w_i.astype(f32),
                   lru_b_i.astype(f32), lru_lambda.astype(f32))
    out_a = h_lru * jax.nn.gelu(lru_gate.astype(f32))
    xbc = jax.nn.silu(causal_dwconv(xbc, ssd_conv_w, ssd_conv_b).astype(f32))
    xs, bm, cm = jnp.split(xbc, [SSD_WIDTH, SSD_WIDTH + SSD_GROUPS * SSD_STATE], axis=-1)
    xs = xs.reshape(b, l, SSD_HEADS, SSD_HEAD_DIM)
    bm = bm.reshape(b, l, SSD_GROUPS, SSD_STATE)
    cm = cm.reshape(b, l, SSD_GROUPS, SSD_STATE)
    dt = jax.nn.softplus(dt_raw.astype(f32) + ssd_dt_bias.astype(f32))
    a = -jnp.exp(ssd_a_log.astype(f32))
    y = ssd_chunked(xs, dt, a, bm, cm) + ssd_d.astype(f32)[:, None] * xs
    y = y.reshape(b, l, SSD_WIDTH) * jax.nn.silu(z.astype(f32))
    y = y.reshape(b, l, SSD_GROUPS, SSD_WIDTH // SSD_GROUPS)
    y = y * lax.rsqrt(jnp.mean(y * y, axis=-1, keepdims=True) + NORM_EPS)
    out_b = y.reshape(b, l, SSD_WIDTH) * ssd_norm.astype(f32)
    mixed = jnp.concatenate([out_a, out_b], axis=-1).astype(x.dtype)
    return x + mixed @ w_out

def partial_rope(x, pos):
    half = ROPE_DIM // 2
    inv = ROPE_THETA ** (-2.0 * jnp.arange(half, dtype=jnp.float32) / ROPE_DIM)
    ang = pos[:, None] * inv[None, :]
    cos = jnp.cos(ang)[None, :, None, :]
    sin = jnp.sin(ang)[None, :, None, :]
    x1 = x[..., :half].astype(jnp.float32)
    x2 = x[..., half:ROPE_DIM].astype(jnp.float32)
    rot = jnp.concatenate([x1 * cos - x2 * sin, x2 * cos + x1 * sin], axis=-1)
    return jnp.concatenate([rot.astype(x.dtype), x[..., ROPE_DIM:]], axis=-1)

def dilated_window_attention(q, k, v, window, dilation):
    b, l, h, e = q.shape
    span = window // dilation
    u = l // dilation
    nblk = -(-u // span)
    up = nblk * span

    def to_strided(t):
        t = t.reshape(b, u, dilation, h, e).transpose(0, 2, 1, 3, 4).reshape(b * dilation, u, h, e)
        t = jnp.pad(t, ((0, 0), (0, up - u), (0, 0), (0, 0)))
        return t.reshape(b * dilation, nblk, span, h, e)

    def with_prev(t):
        prev = jnp.pad(t[:, :-1], ((0, 0), (1, 0), (0, 0), (0, 0), (0, 0)))
        return jnp.concatenate([prev, t], axis=2)

    def from_strided(t):
        tail = t.shape[3:]
        t = t.reshape((b, dilation, up) + tail)[:, :, :u]
        return jnp.swapaxes(t, 1, 2).reshape((b, l) + tail)

    qb = to_strided(q)
    kc = with_prev(to_strided(k))
    vc = with_prev(to_strided(v))
    s = jnp.einsum('bnqhe,bnkhe->bnhqk', qb, kc).astype(jnp.float32)
    qi = jnp.arange(span)[:, None]
    kj = jnp.arange(2 * span)[None, :]
    band = (kj >= qi) & (kj <= qi + span)
    valid = band[None] & ((jnp.arange(nblk)[:, None, None] > 0) | (kj[None] >= span))
    s = jnp.where(valid[None, :, None], s, -jnp.inf)
    m = jnp.max(s, axis=-1)
    p = jnp.exp(s - m[..., None])
    den = jnp.sum(p, axis=-1)
    o = jnp.einsum('bnhqk,bnkhe->bnqhe', p, vc.astype(jnp.float32))
    den_q = jnp.swapaxes(den, 2, 3)
    o = o / den_q[..., None]
    return from_strided(o), from_strided(jnp.swapaxes(m, 2, 3)), from_strided(den_q)

def attention_layer(x, norm_g, w_qkv, q_norm, k_norm, w_out):
    b, l, _ = x.shape
    h = rmsnorm(x, norm_g)
    qkv = (h @ w_qkv).reshape(b, l, 3, ATT_HEADS, ATT_HEAD_DIM)
    pos = jnp.arange(l, dtype=jnp.float32)
    q = partial_rope(rmsnorm(qkv[:, :, 0], q_norm), pos) * (ATT_HEAD_DIM ** -0.5)
    k = partial_rope(rmsnorm(qkv[:, :, 1], k_norm), pos)
    v = qkv[:, :, 2]
    outs, maxes, dens = [], [], []
    for window, dilation in DILATED_PATTERNS:
        o_i, m_i, d_i = dilated_window_attention(q, k, v, window, dilation)
        outs.append(o_i)
        maxes.append(m_i)
        dens.append(d_i)
    m_all = jnp.stack(maxes)
    wts = jnp.stack(dens) * jnp.exp(m_all - jnp.max(m_all, axis=0, keepdims=True))
    o = jnp.sum(wts[..., None] * jnp.stack(outs), axis=0) / jnp.sum(wts, axis=0)[..., None]
    o = o.astype(x.dtype).reshape(b, l, ATT_WIDTH)
    return x + o @ w_out

def swiglu_layer(x, norm_g, w_gate_up, w_down):
    h = rmsnorm(x, norm_g)
    g, u = jnp.split(h @ w_gate_up, 2, axis=-1)
    return x + (jax.nn.silu(g) * u) @ w_down

def first_inputs(seed: int = 0) -> dict:
    key = jax.random.key(seed)
    ks = iter(jax.random.split(key, 32))
    f32 = jnp.float32
    ne, no = N_EVEN, N_ODD

    def nrm(shape, scale):
        return jax.random.normal(next(ks), shape, f32) * scale

    def gain(shape):
        return 1.0 + 0.02 * jax.random.normal(next(ks), shape, f32)

    lam_base = jax.random.uniform(next(ks), (ne, LRU_WIDTH), f32, 0.9, 0.999)
    sig = lam_base ** (1.0 / LRU_C)
    lru_lambda = jnp.log(sig) - jnp.log1p(-sig)
    dt0 = jnp.exp(jax.random.uniform(next(ks), (ne, SSD_HEADS), f32, math.log(1e-3), math.log(1e-1)))
    ssd_dt_bias = dt0 + jnp.log(-jnp.expm1(-dt0))
    ssd_a_log = jnp.log(jax.random.uniform(next(ks), (ne, SSD_HEADS), f32, 1.0, 16.0))
    inputs = {}
    inputs['x'] = nrm((BATCH, SEQ, D_MODEL), 1.0)
    inputs['rec_norm'] = gain((ne, D_MODEL))
    inputs['rec_w_in'] = nrm((ne, D_MODEL, REC_IN), D_MODEL ** -0.5)
    inputs['lru_conv_w'] = nrm((ne, CONV_WIDTH, LRU_WIDTH), CONV_WIDTH ** -0.5)
    inputs['lru_conv_b'] = nrm((ne, LRU_WIDTH), 0.02)
    inputs['lru_w_r'] = nrm((ne, LRU_BLOCKS, LRU_BLOCK, LRU_BLOCK), LRU_BLOCK ** -0.5)
    inputs['lru_b_r'] = nrm((ne, LRU_WIDTH), 0.02)
    inputs['lru_w_i'] = nrm((ne, LRU_BLOCKS, LRU_BLOCK, LRU_BLOCK), LRU_BLOCK ** -0.5)
    inputs['lru_b_i'] = nrm((ne, LRU_WIDTH), 0.02)
    inputs['lru_lambda'] = lru_lambda
    inputs['ssd_conv_w'] = nrm((ne, CONV_WIDTH, SSD_CONV_CH), CONV_WIDTH ** -0.5)
    inputs['ssd_conv_b'] = nrm((ne, SSD_CONV_CH), 0.02)
    inputs['ssd_dt_bias'] = ssd_dt_bias
    inputs['ssd_a_log'] = ssd_a_log
    inputs['ssd_d'] = 1.0 + 0.1 * jax.random.normal(next(ks), (ne, SSD_HEADS), f32)
    inputs['ssd_norm'] = gain((ne, SSD_WIDTH))
    inputs['rec_w_out'] = nrm((ne, REC_OUT, D_MODEL), REC_OUT ** -0.5)
    inputs['att_norm'] = gain((no, D_MODEL))
    inputs['att_w_qkv'] = nrm((no, D_MODEL, 3 * ATT_WIDTH), D_MODEL ** -0.5)
    inputs['att_q_norm'] = gain((no, ATT_HEAD_DIM))
    inputs['att_k_norm'] = gain((no, ATT_HEAD_DIM))
    inputs['att_w_out'] = nrm((no, ATT_WIDTH, D_MODEL), ATT_WIDTH ** -0.5)
    inputs['ffn_norm'] = gain((DEPTH, D_MODEL))
    inputs['ffn_w_gate_up'] = nrm((DEPTH, D_MODEL, 2 * FFN_HIDDEN), D_MODEL ** -0.5)
    inputs['ffn_w_down'] = nrm((DEPTH, FFN_HIDDEN, D_MODEL), FFN_HIDDEN ** -0.5)
    return inputs

def first_block(x, rec_norm, rec_w_in, lru_conv_w, lru_conv_b, lru_w_r, lru_b_r, lru_w_i, lru_b_i,
              lru_lambda, ssd_conv_w, ssd_conv_b, ssd_dt_bias, ssd_a_log, ssd_d, ssd_norm, rec_w_out,
              att_norm, att_w_qkv, att_q_norm, att_k_norm, att_w_out,
              ffn_norm, ffn_w_gate_up, ffn_w_down):
    for layer in range(DEPTH):
        i = layer // 2
        if layer % 2 == 0:
            x = recurrent_layer(x, rec_norm[i], rec_w_in[i], lru_conv_w[i], lru_conv_b[i],
                                lru_w_r[i], lru_b_r[i], lru_w_i[i], lru_b_i[i], lru_lambda[i],
                                ssd_conv_w[i], ssd_conv_b[i], ssd_dt_bias[i], ssd_a_log[i],
                                ssd_d[i], ssd_norm[i], rec_w_out[i])
        else:
            x = attention_layer(x, att_norm[i], att_w_qkv[i], att_q_norm[i], att_k_norm[i],
                                att_w_out[i])
        x = swiglu_layer(x, ffn_norm[layer], ffn_w_gate_up[layer], ffn_w_down[layer])
    return x


CHUNK = 64
Q_BLOCK = 128

MLA_HEADS = 8
MLA_Q_LORA = 512
MLA_KV_LORA = 256
MLA_NOPE = 128
MLA_ROPE = 64
MLA_V = 128
MLA_WIDTH = MLA_HEADS * MLA_V
ROPE_BASE = 10000.0

RWKV_HEAD = 64
RWKV_HEADS = D_MODEL // RWKV_HEAD
RWKV_WIDTH = RWKV_HEADS * RWKV_HEAD
RWKV_DECAY_LORA = 64
RWKV_AAA_LORA = 64
RWKV_SHIFT_COLS = 3 * RWKV_WIDTH + RWKV_DECAY_LORA + RWKV_AAA_LORA
RWKV_GN_EPS = 64e-5

GLA_HEADS = 4
GLA_KEY_WIDTH = D_MODEL // 2
GLA_WIDTH = D_MODEL
GLA_DK = GLA_KEY_WIDTH // GLA_HEADS
GLA_DV = GLA_WIDTH // GLA_HEADS
GLA_GATE_LORA = 16
GLA_GATE_NORM = 16.0

IN_SIZES = (
    MLA_Q_LORA, MLA_KV_LORA, MLA_ROPE, MLA_WIDTH,
    RWKV_SHIFT_COLS, RWKV_WIDTH,
    GLA_KEY_WIDTH, GLA_KEY_WIDTH, GLA_WIDTH, GLA_GATE_LORA, GLA_WIDTH,
    D_MODEL, D_MODEL, D_MODEL,
)
N_IN = sum(IN_SIZES)


def _split(p, sizes):
    outs = []
    start = 0
    for size in sizes:
        outs.append(p[..., start:start + size])
        start += size
    return outs

def _rms_norm(x, gain, eps=NORM_EPS):
    xf = x.astype(jnp.float32)
    y = xf * lax.rsqrt(jnp.mean(xf * xf, axis=-1, keepdims=True) + eps)
    return (y * gain.astype(jnp.float32)).astype(x.dtype)

def _rope_tables(positions):
    inv_freq = ROPE_BASE ** (-jnp.arange(0, MLA_ROPE, 2, dtype=jnp.float32) / MLA_ROPE)
    ang = positions.astype(jnp.float32)[..., None] * inv_freq
    ang = jnp.concatenate([ang, ang], axis=-1)
    return jnp.cos(ang), jnp.sin(ang)

def _apply_rope(x, cos, sin):
    xf = x.astype(jnp.float32)
    half = xf.shape[-1] // 2
    rot = jnp.concatenate([-xf[..., half:], xf[..., :half]], axis=-1)
    return (xf * cos + rot * sin).astype(x.dtype)

def _chunk_causal_attention(q_nope, q_rope, k_nope, k_rope, v):
    b, s, h, _ = q_nope.shape
    n_blocks = s // Q_BLOCK
    scale = (MLA_NOPE + MLA_ROPE) ** -0.5
    key_chunk = jnp.arange(s) // CHUNK

    def block(args):
        qn, qr, blk = args
        scores = (jnp.einsum('bqhd,bkhd->bhqk', qn, k_nope, preferred_element_type=jnp.float32)
                  + jnp.einsum('bqhr,bkr->bhqk', qr, k_rope, preferred_element_type=jnp.float32))
        q_chunk = (blk * Q_BLOCK + jnp.arange(Q_BLOCK)) // CHUNK
        allowed = key_chunk[None, :] <= q_chunk[:, None]
        scores = jnp.where(allowed, scores * scale, -jnp.inf)
        probs = jax.nn.softmax(scores, axis=-1).astype(v.dtype)
        return jnp.einsum('bhqk,bkhv->bqhv', probs, v)

    qn_b = q_nope.reshape(b, n_blocks, Q_BLOCK, h, MLA_NOPE).transpose(1, 0, 2, 3, 4)
    qr_b = q_rope.reshape(b, n_blocks, Q_BLOCK, h, MLA_ROPE).transpose(1, 0, 2, 3, 4)
    out = lax.map(block, (qn_b, qr_b, jnp.arange(n_blocks)))
    return out.transpose(1, 0, 2, 3, 4).reshape(b, s, h, MLA_V)

def _mla_branch(c_q, c_kv, k_rope, z, cos, sin, q_norm, kv_norm, w_uq, w_ukv, w_o):
    b, s, _ = c_q.shape
    c_q = _rms_norm(c_q, q_norm)
    c_kv = _rms_norm(c_kv, kv_norm)
    q = (c_q @ w_uq).reshape(b, s, MLA_HEADS, MLA_NOPE + MLA_ROPE)
    kv = (c_kv @ w_ukv).reshape(b, s, MLA_HEADS, MLA_NOPE + MLA_V)
    q_nope, q_rope = q[..., :MLA_NOPE], q[..., MLA_NOPE:]
    k_nope, v = kv[..., :MLA_NOPE], kv[..., MLA_NOPE:]
    q_rope = _apply_rope(q_rope, cos[:, :, None, :], sin[:, :, None, :])
    k_rope = _apply_rope(k_rope, cos, sin)
    o = _chunk_causal_attention(q_nope, q_rope, k_nope, k_rope, v).reshape(b, s, MLA_WIDTH)
    return (o * jax.nn.silu(z)) @ w_o

def _rwkv7_branch(streams, z, mu, w0, w2, a0, a2, k_k, k_a, r_k, ln_w, ln_b, w_o):
    b, s, _ = streams.shape
    f32 = jnp.float32
    prev = jnp.pad(streams, ((0, 0), (1, 0), (0, 0)))[:, :-1]
    streams = streams + mu * (prev - streams)
    r, k, v, w_l, a_l = _split(streams, (RWKV_WIDTH, RWKV_WIDTH, RWKV_WIDTH,
                                         RWKV_DECAY_LORA, RWKV_AAA_LORA))
    w = -jax.nn.softplus(-(w0 + jnp.tanh(w_l) @ w2)) - 0.5
    decay = jnp.exp(-jnp.exp(w.astype(f32)))
    a = jax.nn.sigmoid(a0 + a_l @ a2)
    heads = lambda t: t.astype(f32).reshape(b, s, RWKV_HEADS, RWKV_HEAD)
    kk = heads(k * k_k)
    kk = kk / jnp.maximum(jnp.sqrt(jnp.sum(kk * kk, axis=-1, keepdims=True)), 1e-12)
    k = k * (1 + (a - 1) * k_a)
    r_h, k_h, v_h, w_h, a_h = heads(r), heads(k), heads(v), heads(decay), heads(a)

    def step(state, inp):
        r_t, w_t, k_t, v_t, kk_t, a_t = inp
        sa = jnp.einsum('bhvk,bhk->bhv', state, -kk_t)
        state = (state * w_t[:, :, None, :]
                 + sa[..., None] * (kk_t * a_t)[:, :, None, :]
                 + v_t[..., None] * k_t[:, :, None, :])
        return state, jnp.einsum('bhvk,bhk->bhv', state, r_t)

    to_steps = lambda t: t.transpose(1, 0, 2, 3)
    state0 = jnp.zeros((b, RWKV_HEADS, RWKV_HEAD, RWKV_HEAD), f32)
    _, y = lax.scan(step, state0, tuple(to_steps(t) for t in (r_h, w_h, k_h, v_h, kk, a_h)))
    y = y.transpose(1, 0, 2, 3)
    mean = jnp.mean(y, axis=-1, keepdims=True)
    var = jnp.mean(jnp.square(y - mean), axis=-1, keepdims=True)
    y = ((y - mean) * lax.rsqrt(var + RWKV_GN_EPS)).reshape(b, s, RWKV_WIDTH)
    y = y * ln_w.astype(f32) + ln_b.astype(f32)
    bonus = jnp.sum(r_h * k_h * r_k.astype(f32), axis=-1, keepdims=True) * v_h
    y = (y + bonus.reshape(b, s, RWKV_WIDTH)).astype(z.dtype)
    return (y * jax.nn.silu(z)) @ w_o

def _gla_branch(q, k, v, g_l, z, w2, g_bias, norm_g, w_o):
    b, s, _ = q.shape
    nc = s // CHUNK
    f32 = jnp.float32
    q = q.astype(f32).reshape(b, nc, CHUNK, GLA_HEADS, GLA_DK) * (GLA_DK ** -0.5)
    k = k.astype(f32).reshape(b, nc, CHUNK, GLA_HEADS, GLA_DK)
    v = v.astype(f32).reshape(b, nc, CHUNK, GLA_HEADS, GLA_DV)
    log_a = jax.nn.log_sigmoid((g_l @ w2 + g_bias).astype(f32)) / GLA_GATE_NORM
    cum = jnp.cumsum(log_a.reshape(b, nc, CHUNK, GLA_HEADS, GLA_DK), axis=2)
    cum_last = cum[:, :, -1:]
    q_dec = q * jnp.exp(cum)
    k_inv = k * jnp.exp(-cum)
    k_to_end = k * jnp.exp(cum_last - cum)
    attn = jnp.einsum('bnihd,bnjhd->bnhij', q_dec, k_inv)
    attn = jnp.where(jnp.tril(jnp.ones((CHUNK, CHUNK), bool)), attn, 0.0)
    o_intra = jnp.einsum('bnhij,bnjhv->bnihv', attn, v)

    def step(state, inp):
        q_c, k_c, v_c, d_c = inp
        o_c = jnp.einsum('bihd,bhdv->bihv', q_c, state)
        state = state * d_c[..., None] + jnp.einsum('bjhd,bjhv->bhdv', k_c, v_c)
        return state, o_c

    mv = lambda t: jnp.moveaxis(t, 1, 0)
    state0 = jnp.zeros((b, GLA_HEADS, GLA_DK, GLA_DV), f32)
    _, o_inter = lax.scan(step, state0, (mv(q_dec), mv(k_to_end), mv(v), mv(jnp.exp(cum_last[:, :, 0]))))
    o = o_intra + mv(o_inter)
    o = o * lax.rsqrt(jnp.mean(o * o, axis=-1, keepdims=True) + NORM_EPS) * norm_g.astype(f32)
    o = o.reshape(b, s, GLA_WIDTH).astype(z.dtype)
    return (o * jax.nn.silu(z)) @ w_o

def second_inputs(seed: int = 0) -> dict:
    key = jax.random.key(seed)
    ks = jax.random.split(key, 32)
    L = DEPTH
    f32 = jnp.float32
    nrm = lambda k, shape, sc: jax.random.normal(k, shape, f32) * sc
    gain = lambda k, shape: 1.0 + nrm(k, shape, 0.05)
    positions = (jax.random.randint(ks[2], (BATCH, 1), 0, 4096, dtype=jnp.int32)
                 + jnp.arange(SEQ, dtype=jnp.int32)[None, :])
    return {
        "x": nrm(ks[0], (BATCH, SEQ, D_MODEL), 1.0),
        "c": nrm(ks[1], (BATCH, D_MODEL), 1.0),
        "positions": positions,
        "ada_w": nrm(ks[3], (L, D_MODEL, 3 * D_MODEL), 0.5 * D_MODEL ** -0.5),
        "ada_b": nrm(ks[4], (L, 3 * D_MODEL), 0.02),
        "norm_pre": gain(ks[5], (L, D_MODEL)),
        "norm_post": gain(ks[6], (L, D_MODEL)),
        "w_in": nrm(ks[7], (L, D_MODEL, N_IN), D_MODEL ** -0.5),
        "rwkv_mu": jax.random.uniform(ks[8], (L, RWKV_SHIFT_COLS), f32),
        "mla_q_norm": gain(ks[9], (L, MLA_Q_LORA)),
        "mla_kv_norm": gain(ks[10], (L, MLA_KV_LORA)),
        "mla_w_uq": nrm(ks[11], (L, MLA_Q_LORA, MLA_HEADS * (MLA_NOPE + MLA_ROPE)), MLA_Q_LORA ** -0.5),
        "mla_w_ukv": nrm(ks[12], (L, MLA_KV_LORA, MLA_HEADS * (MLA_NOPE + MLA_V)), MLA_KV_LORA ** -0.5),
        "mla_w_o": nrm(ks[13], (L, MLA_WIDTH, D_MODEL), MLA_WIDTH ** -0.5),
        "rwkv_w0": jax.random.uniform(ks[14], (L, RWKV_WIDTH), f32, -6.0, -1.0),
        "rwkv_w2": nrm(ks[15], (L, RWKV_DECAY_LORA, RWKV_WIDTH), 0.1 * RWKV_DECAY_LORA ** -0.5),
        "rwkv_a0": nrm(ks[16], (L, RWKV_WIDTH), 0.1),
        "rwkv_a2": nrm(ks[17], (L, RWKV_AAA_LORA, RWKV_WIDTH), 0.1 * RWKV_AAA_LORA ** -0.5),
        "rwkv_k_k": 0.85 + nrm(ks[18], (L, RWKV_WIDTH), 0.05),
        "rwkv_k_a": gain(ks[19], (L, RWKV_WIDTH)),
        "rwkv_r_k": nrm(ks[20], (L, RWKV_HEADS, RWKV_HEAD), 0.1),
        "rwkv_ln_w": gain(ks[21], (L, RWKV_WIDTH)),
        "rwkv_ln_b": nrm(ks[22], (L, RWKV_WIDTH), 0.02),
        "rwkv_w_o": nrm(ks[23], (L, RWKV_WIDTH, D_MODEL), RWKV_WIDTH ** -0.5),
        "gla_w2": nrm(ks[24], (L, GLA_GATE_LORA, GLA_KEY_WIDTH), GLA_GATE_LORA ** -0.5),
        "gla_b": nrm(ks[25], (L, GLA_KEY_WIDTH), 0.1),
        "gla_norm": gain(ks[26], (L, GLA_DV)),
        "gla_w_o": nrm(ks[27], (L, GLA_WIDTH, D_MODEL), GLA_WIDTH ** -0.5),
        "w_out": nrm(ks[28], (L, D_MODEL, D_MODEL), D_MODEL ** -0.5),
    }

def second_block(x, c, positions, ada_w, ada_b, norm_pre, norm_post, w_in, rwkv_mu,
              mla_q_norm, mla_kv_norm, mla_w_uq, mla_w_ukv, mla_w_o,
              rwkv_w0, rwkv_w2, rwkv_a0, rwkv_a2, rwkv_k_k, rwkv_k_a, rwkv_r_k,
              rwkv_ln_w, rwkv_ln_b, rwkv_w_o,
              gla_w2, gla_b, gla_norm, gla_w_o, w_out):
    cos, sin = _rope_tables(positions)
    c_act = jax.nn.silu(c)
    for l in range(DEPTH):
        mod = c_act @ ada_w[l] + ada_b[l]
        shift, scale, gate = jnp.split(mod, 3, axis=-1)
        h = _rms_norm(x, norm_pre[l]) * (1 + scale[:, None, :]) + shift[:, None, :]
        p = h @ w_in[l]
        (m_cq, m_ckv, m_kr, m_z, r_streams, r_z,
         g_q, g_k, g_v, g_l, g_z, gate_a, gate_b, gate_c) = _split(p, IN_SIZES)
        o_mla = _mla_branch(m_cq, m_ckv, m_kr, m_z, cos, sin, mla_q_norm[l], mla_kv_norm[l],
                            mla_w_uq[l], mla_w_ukv[l], mla_w_o[l])
        o_rwkv = _rwkv7_branch(r_streams, r_z, rwkv_mu[l], rwkv_w0[l], rwkv_w2[l], rwkv_a0[l],
                               rwkv_a2[l], rwkv_k_k[l], rwkv_k_a[l], rwkv_r_k[l],
                               rwkv_ln_w[l], rwkv_ln_b[l], rwkv_w_o[l])
        o_gla = _gla_branch(g_q, g_k, g_v, g_l, g_z, gla_w2[l], gla_b[l], gla_norm[l], gla_w_o[l])
        merged = (jax.nn.sigmoid(gate_a) * o_mla + jax.nn.sigmoid(gate_b) * o_rwkv
                  + jax.nn.sigmoid(gate_c) * o_gla)
        y = merged @ w_out[l]
        x = x + gate[:, None, :] * _rms_norm(y, norm_post[l])
    return x


_first_inputs = second_inputs


def second_inputs(seed=0):
    import zlib

    import numpy as np

    out = dict(_first_inputs(seed))
    spreads = {}
    factors = {'mla_q_norm': 8.0,
     'mla_kv_norm': 8.0,
     'rwkv_w2': 8.0,
     'rwkv_a0': 3.801,
     'rwkv_a2': 3.673,
     'rwkv_ln_w': 3.604,
     'rwkv_ln_b': 8.0,
     'gla_b': 3.879,
     'gla_norm': 3.944}
    for name, (base, spread) in spreads.items():
        noise = np.random.default_rng([zlib.crc32(name.encode()), seed]).standard_normal(out[name].shape)
        drawn = base * np.exp(spread * noise) if base else spread * noise
        out[name] = jnp.asarray(drawn.astype(out[name].dtype))
    for name, factor in factors.items():
        out[name] = (out[name] * factor).astype(out[name].dtype)
    return out


_narrow_inputs = second_inputs


def second_inputs(seed=0):

    out = dict(_narrow_inputs(seed))
    wider = {'rwkv_w2': 3.26, 'rwkv_k_k': 3.05, 'rwkv_ln_w': 3.99, 'rwkv_ln_b': 5.1, 'gla_norm': 4.23}
    for name, times in wider.items():
        mean = out[name].mean()
        out[name] = (mean + times * (out[name] - mean)).astype(out[name].dtype)
    return out


def setup_inputs(seed=0):
    out = dict(first_inputs(seed))
    for name, value in second_inputs(seed + 1).items():
        if name != "x":
            out[name + "_2"] = value
    return out


def reference(
    x, rec_norm, rec_w_in, lru_conv_w, lru_conv_b, lru_w_r, lru_b_r, lru_w_i, lru_b_i,
    lru_lambda, ssd_conv_w, ssd_conv_b, ssd_dt_bias, ssd_a_log, ssd_d, ssd_norm, rec_w_out,
    att_norm, att_w_qkv, att_q_norm, att_k_norm, att_w_out, ffn_norm, ffn_w_gate_up, ffn_w_down,
    c_2, positions_2, ada_w_2, ada_b_2, norm_pre_2, norm_post_2, w_in_2, rwkv_mu_2,
    mla_q_norm_2, mla_kv_norm_2, mla_w_uq_2, mla_w_ukv_2, mla_w_o_2, rwkv_w0_2, rwkv_w2_2,
    rwkv_a0_2, rwkv_a2_2, rwkv_k_k_2, rwkv_k_a_2, rwkv_r_k_2, rwkv_ln_w_2, rwkv_ln_b_2,
    rwkv_w_o_2, gla_w2_2, gla_b_2, gla_norm_2, gla_w_o_2, w_out_2,
):
    x = first_block(
        x, rec_norm, rec_w_in, lru_conv_w, lru_conv_b, lru_w_r, lru_b_r, lru_w_i, lru_b_i,
        lru_lambda, ssd_conv_w, ssd_conv_b, ssd_dt_bias, ssd_a_log, ssd_d, ssd_norm, rec_w_out,
        att_norm, att_w_qkv, att_q_norm, att_k_norm, att_w_out, ffn_norm, ffn_w_gate_up,
        ffn_w_down,
    )
    return second_block(
        x, c_2, positions_2, ada_w_2, ada_b_2, norm_pre_2, norm_post_2, w_in_2, rwkv_mu_2,
        mla_q_norm_2, mla_kv_norm_2, mla_w_uq_2, mla_w_ukv_2, mla_w_o_2, rwkv_w0_2, rwkv_w2_2,
        rwkv_a0_2, rwkv_a2_2, rwkv_k_k_2, rwkv_k_a_2, rwkv_r_k_2, rwkv_ln_w_2, rwkv_ln_b_2,
        rwkv_w_o_2, gla_w2_2, gla_b_2, gla_norm_2, gla_w_o_2, w_out_2,
    )


_drawn_inputs = setup_inputs


def setup_inputs(seed=0):
    import zlib

    import numpy as np

    out = dict(_drawn_inputs(seed))
    spreads = {}
    factors = {'lru_b_r': 8.0,
     'lru_b_i': 8.0,
     'att_norm': 3.026,
     'att_q_norm': 5.515,
     'att_k_norm': 5.918,
     'norm_post_2': 3.047,
     'rwkv_k_a_2': 4.559,
     'rwkv_r_k_2': 4.173}
    for name, (base, spread) in spreads.items():
        noise = np.random.default_rng([zlib.crc32(name.encode()), seed]).standard_normal(out[name].shape)
        drawn = base * np.exp(spread * noise) if base else spread * noise
        out[name] = jnp.asarray(drawn.astype(out[name].dtype))
    for name, factor in factors.items():
        out[name] = (out[name] * factor).astype(out[name].dtype)
    return out
```

```python
from contextlib import ExitStack

import numpy as np

import concourse.bass as bass
from concourse import mybir

F32 = mybir.dt.float32
I32 = mybir.dt.int32
ALU = mybir.AluOpType
ACT = mybir.ActivationFunctionType
AX = mybir.AxisListType.X

P = 128
T = 256
TT = T // P
D = 1024
DK = D // P
COLS = 256
EPS = 1e-6
GN_EPS = 64e-5
FFN = 2816
CH = 64



def constants():
    p = np.arange(P)
    s, t = p[:, None], p[None, :]
    same = s // CH == t // CH
    parts = {}
    parts["ident"] = np.eye(P)
    parts["ones"] = np.ones((P, P))
    parts["ones64"] = same * 1.0
    parts["tri"] = (s <= t) * 1.0
    parts["half"] = np.stack([p < 64, p >= 64], 1) * 1.0
    parts["neg_strict"] = -1.0 * (same & (t < s))
    parts["before"] = same & (s < t)
    parts["upto"] = same & (s <= t)
    for n in range(6):
        b = 1 << n
        parts[f"level{n}"] = (s // (2 * b) == t // (2 * b)) & ((s // b) % 2 == 0) & ((t // b) % 2 == 1)
    tok = np.arange(T)
    parts["run"] = np.tile((tok % CH != 0) * 1.0, (P, 1))
    q = (np.arange(TT)[None, :, None] * P + p[:, None, None])
    k = tok[None, None, :]
    count = (k <= q) * ((k >= q - 128) * 1 + ((q - k) % 4 == 0) * 1 + ((q - k) % 16 == 0) * 1)
    parts["windows"] = np.where(count > 0, np.log(np.maximum(count, 1)), -1e30).reshape(P, -1)
    parts["chunks"] = np.where(k // CH <= q // CH, 0.0, -1e30).reshape(P, -1)
    half = 8
    inv = np.float32(500000.0) ** (np.float32(-2.0) * np.arange(half, dtype=np.float32) / np.float32(16))
    ang = (tok[:, None].astype(np.float32) * inv[None, :].astype(np.float32)).astype(np.float32).T
    e = p % 64
    cos = np.ones((P, T))
    sin = np.zeros((P, T))
    for i in range(P):
        if e[i] < 16:
            cos[i], sin[i] = np.cos(ang[e[i] % 8]), np.sin(ang[e[i] % 8])
    rot = np.zeros((P, P))
    for i in range(P):
        if e[i] < 8:
            rot[i + 8, i] = -1.0
        elif e[i] < 16:
            rot[i - 8, i] = 1.0
    parts["att_cos"], parts["att_sin"], parts["att_rot"] = cos, sin, rot
    rot = np.zeros((P, P))
    for i in range(P):
        if e[i] < 32:
            rot[i + 32, i] = -1.0
        else:
            rot[i - 32, i] = 1.0
    parts["mla_rot"] = rot
    freq = np.float32(10000.0) ** (-np.arange(0, 64, 2, dtype=np.float32) / np.float32(64))
    parts["mla_freq"] = np.tile(np.concatenate([freq, freq]), 2)[:, None]
    at, n = {}, 0
    for name, a in parts.items():
        at[name] = (n, n + a.shape[1])
        n += a.shape[1]
    return np.concatenate([np.asarray(a, np.float32) for a in parts.values()], 1), at


CONST, CONST_AT = constants()



def vector_rows():
    sizes = [("rec_norm", 8), ("lru_conv_w", 32), ("lru_conv_b", 8), ("lru_b_r", 8), ("lru_b_i", 8),
             ("lru_lambda", 8), ("ssd_conv_w", 48), ("ssd_conv_b", 12), ("ssd_norm", 8), ("att_norm", 8),
             ("ffn_norm", 16), ("att_q_norm", 1), ("att_k_norm", 1), ("c_2", 8)]
    for l in range(2):
        sizes += [(f"{n}_2/{l}", r) for n, r in (
            ("ada_b", 24), ("norm_pre", 8), ("norm_post", 8), ("rwkv_mu", 25), ("mla_q_norm", 4),
            ("mla_kv_norm", 2), ("rwkv_w0", 8), ("rwkv_a0", 8), ("rwkv_k_k", 8), ("rwkv_k_a", 8),
            ("rwkv_r_k", 8), ("rwkv_ln_w", 8), ("rwkv_ln_b", 8), ("gla_b", 4), ("gla_norm", 2))]
    at, pack, row = {}, 0, 0
    for name, n in sizes:
        if row + n > P:
            pack, row = pack + 1, 0
        at[name] = (pack, row, n)
        row += n
    return at, pack + 1


VEC_AT, PACKS = vector_rows()

SIZES = (("cq", 512), ("ckv", 256), ("kr", 64), ("mz", 1024), ("r", 1024), ("k", 1024), ("v", 1024),
         ("wl", 64), ("al", 64), ("rz", 1024), ("gq", 512), ("gk", 512), ("gv", 1024), ("gl", 16),
         ("gz", 1024), ("ga", 1024), ("gb", 1024), ("gc", 1024))
IN_AT = {}
_n = 0
for _name, _size in SIZES:
    IN_AT[_name] = _n
    _n += _size


class Count:

    def __init__(self, sem):
        self.sem, self.counts = sem, {}

    def due(self, eng, n=1):
        k = self.counts[id(eng)] = self.counts.get(id(eng), 0) + n
        return k


class Banks:

    def __init__(self, tiles, full, free):
        self.banks, self.filled, self.emptied = list(zip(tiles, full, free)), 0, 0

    def fill(self):
        tile, full, free = self.banks[self.filled % len(self.banks)]
        self.filled += 1
        return tile, free, full.sem

    def empty(self):
        self.emptied += 1
        return self.banks[(self.emptied - 1) % len(self.banks)]


def program(nc, A, out, stop=None):
    with ExitStack() as ctx:
        def sem(name):
            return Count(ctx.enter_context(nc.semaphore(name)))


        def flat(x):
            return x.rearrange("p a b -> p (a b)")

        AR = 53100
        arena = ctx.enter_context(nc.sbuf_tensor("arena", [P, AR], F32))
        psum = [ctx.enter_context(nc.psum_tensor(f"bank{i}", [P, 512], F32))[:, :] for i in range(8)]
        place = [0]

        def buf(*shape):
            n = int(np.prod(shape))
            at = place[0]
            place[0] += n
            assert place[0] <= AR, ("the arena is too small", place[0])
            v = arena[:, at:at + n]
            if len(shape) == 2:
                v = v.rearrange("p (a b) -> p a b", a=shape[0])
            if len(shape) == 3:
                v = v.rearrange("p (a b c) -> p a b c", a=shape[0], b=shape[1])
            return v

        cst = buf(CONST.shape[1])

        def const(name):
            return cst[:, CONST_AT[name][0]:CONST_AT[name][1]]

        ident, ones, ones64, half, tri = (const(n) for n in ("ident", "ones", "ones64", "half", "tri"))
        cols = buf(PACKS * P)

        def col(name, i=0, n=1):
            pack, row, _ = VEC_AT[name]
            at = pack * P + row + i
            return cols[:, at:at + n]

        X = buf(DK, T)
        H = buf(DK, T)
        STAT = buf(4, T)
        biases = buf(4)
        COS, SIN = buf(T), buf(T)
        base = place[0]

        def views(kt):
            return [buf(kt, COLS), buf(kt, COLS)]

        WIDE = views(FFN // P)
        first_base = place[0]
        LX, XB = buf(DK, T + 3), buf(12, T + 3)
        G, Z, XC, RG, IG = (buf(DK, T) for _ in range(5))
        XBC, MIX = buf(12, T), buf(16, T)
        BD = buf(2, DK, P)
        DT, DTB, DTC, DTD, DTE = (buf(TT, 16) for _ in range(5))
        AROW, CS = buf(3, 16), buf(TT, 16)
        LAM, LAMB, LAMC, LAMD, LAMX, DCOL, LAMA = (buf(8) for _ in range(7))
        LAST = buf(16)
        place[0] = first_base
        spare = buf(DK * (T + 3) + 12 * (T + 3))
        XTOK = spare[:, 0:TT * D].rearrange("p (a b) -> p a b", a=TT)
        XDTE = spare[:, TT * D:TT * D + D]
        BTOK = spare[:, 3 * D:3 * D + 2 * P].rearrange("p (a b) -> p a b", a=2)
        CBM = spare[:, 3 * D + 2 * P:3 * D + 4 * P].rearrange("p (a b) -> p a b", a=2)
        PREV = spare[:, 3 * D + 4 * P:4 * D + 4 * P].rearrange("p (a b) -> p a b", a=2)
        UU = XTOK.rearrange("p a b -> p (a b)").rearrange("p (k t) -> p k t", k=DK)
        heads16 = "p (h l) -> p h l"
        ADTRI = RG.rearrange("p a b -> p (a b)").rearrange(heads16, h=16)
        SEG = IG.rearrange("p a b -> p (a b)").rearrange(heads16, h=16)
        ECS = XC.rearrange("p a b -> p (a b)").rearrange(heads16, h=16)
        place[0] = first_base
        hidden, silu_g, SQF = buf(FFN // P, T), buf(2, T), buf(DK, T)
        place[0] = first_base
        Q, K, SQA, RS, O, ROT = (buf(DK, T) for _ in range(6))
        VT, KP = buf(TT, D), buf(16, T)
        SC, PR, PT = ([buf(TT, T) for _ in range(2)] for _ in range(3))
        MX, SM = [buf(TT) for _ in range(2)], [buf(TT) for _ in range(2)]
        place[0] = first_base
        PACK, XIN = buf(PACKS, P), buf(TT, D)

        place[0] = base
        SL = views(DK)
        M, GT = buf(DK, T), buf(DK, T)
        MOD, GPRE, GPOST, CA = buf(24), buf(8), buf(8), buf(8, 1)
        WL, GL = buf(T + 1), buf(T)
        second_base = place[0]
        CQ, CKV, KR, QR, KRP = buf(4, T), buf(2, T), buf(1, T), buf(4, T), buf(2, T)
        QN, KN, ZM, OM, SQM = (buf(DK, T) for _ in range(5))
        VM = buf(TT, D)
        ROTM = buf(4, T)
        MSC, MPR, MPT = ([buf(TT, T) for _ in range(2)] for _ in range(3))
        MMX, MSM = [buf(TT) for _ in range(2)], [buf(TT) for _ in range(2)]
        ANG = buf(4, T)
        place[0] = second_base
        GQ, GK, GE, GX, GY, GC, GD, KINV, KTE = (buf(4, T) for _ in range(9))
        GV, OG, GZ, SQG = buf(TT, D), buf(DK, T), buf(DK, T), buf(DK, T)
        G2 = buf(512)
        KTT = [buf(4, P) for _ in range(2)]
        AT = buf(4, P)
        GS = [None] + [buf(4, T) for _ in range(3)]
        EL = buf(16)
        place[0] = second_base
        raw = [buf(DK, T + 1) for _ in range(3)]
        R, KR_, V_ = buf(DK, T), buf(DK, T), buf(DK, T)
        tile_base = place[0]
        BDT, KDT = [buf(D), buf(D)], [buf(D), buf(D)]
        VTK, KKT = buf(D), buf(D)
        PAD = buf(8 * 4, P)
        AN, XT, XX, QQ, BT = (buf(16, P) for _ in range(5))
        ST = [buf(8, P), KKT.rearrange("p (a b) -> p a b", a=DK)]
        ECEND = buf(DK, 4)
        KAI = buf(8)
        assert place[0] <= AR
        place[0] = tile_base
        AA, SW, CC, W2 = buf(DK, T), buf(DK, T), buf(DK, T), buf(16, P)
        E1, E2, SQR = buf(DK, T), buf(DK, T), buf(DK, T)
        assert place[0] <= AR - 2200

        KKD, BDF, BONUS = (x[:, :, 0:T] for x in raw)
        BVT = UT = flat(AN)[:, 0:D]
        WT = flat(AN)[:, D:2 * D].rearrange("p (a b) -> p a b", a=DK)
        ZT = flat(BT)[:, 0:D]
        SQT, RST = (flat(x).rearrange("p (a b) -> p a b", a=DK) for x in (XT, XX))
        ZR = flat(PAD)[:, 0:DK * T].rearrange("p (a b) -> p a b", a=DK)
        TMP = [flat(PAD)[:, DK * T + n * 512:DK * T + n * 512 + 512].rearrange("p (a b) -> p a b", a=2) for n in range(2)]
        TMPG = [flat(GE)[:, n * 512:n * 512 + 512].rearrange("p (a b) -> p a b", a=2) for n in range(2)]

        landed = [sem("weights_landed_a"), sem("weights_landed_b")]
        product = [sem("half_product_a"), sem("half_product_b")]
        evicted = [sem("half_evicted_a"), sem("half_evicted_b")]
        vector_step, scalar_step = sem("vector_step_done"), sem("scalar_step_done")
        vbanks = Banks(psum[2:5], [sem(f"full_for_vector_{i}") for i in range(3)],
                       [sem(f"vector_emptied_{i}") for i in range(3)])
        abanks = Banks(psum[5:8], [sem(f"full_for_scalar_{i}") for i in range(3)],
                       [sem(f"scalar_emptied_{i}") for i in range(3)])
        a_exp = sem("a_exp")
        a_ready = sem("a_ready")
        angles_ready = sem("angles_ready")
        biases_set = sem("biases_set")
        branch_ready = sem("branch_ready")
        bv_ready = sem("bv_ready")
        condition_ready = sem("condition_ready")
        conv_fronts_zeroed = sem("conv_fronts_zeroed")
        cumulated = sem("cumulated")
        decay_in = sem("decay_in")
        decay_out = sem("decay_out")
        decay_steps = sem("decay_steps")
        decays = sem("decays")
        fronts_zeroed = sem("fronts_zeroed")
        gate_in = sem("gate_in")
        gate_out = sem("gate_out")
        gla_exps = sem("gla_exps")
        gla_operands = sem("gla_operands")
        gla_states = sem("gla_states")
        gla_sums = sem("gla_sums")
        head_normed = sem("head_normed")
        head_rms = sem("head_rms")
        head_squares = sem("head_squares")
        heads_out = sem("heads_out")
        hidden_ready = sem("hidden_ready")
        inputs_landed = sem("inputs_landed")
        inverse_ready = sem("inverse_ready")
        keys_ready = sem("keys_ready")
        level_operands = sem("level_operands")
        lora_gates = sem("lora_gates")
        lora_mixed = sem("lora_mixed")
        lora_ready = sem("lora_ready")
        lora_weights = sem("lora_weights")
        lora_zeroed = sem("lora_zeroed")
        lru_conv_done = sem("lru_conv_done")
        lru_functions = sem("lru_functions")
        lru_gates = sem("lru_gates")
        lru_root = sem("lru_root")
        lru_root_in = sem("lru_root_in")
        lru_weights_landed = sem("lru_weights_landed")
        lru_weights_zeroed = sem("lru_weights_zeroed")
        merge_ready = sem("merge_ready")
        merged = sem("merged")
        merged_rwkv = sem("merged_rwkv")
        normed = sem("normed")
        output_ready = sem("output_ready")
        output_written = sem("output_written")
        packs_zeroed = sem("packs_zeroed")
        positions_landed = sem("positions_landed")
        probs_ready = sem("probs_ready")
        probs_scaled = sem("probs_scaled")
        probs_turned = sem("probs_turned")
        rate_ready = sem("rate_ready")
        rms_ready = sem("rms_ready")
        rows_landed = sem("rows_landed")
        scores_ready = sem("scores_ready")
        second_begins = sem("second_begins")
        softplus_exp = sem("softplus_exp")
        softplus_in = sem("softplus_in")
        squares_ready = sem("squares_ready")
        ssd_conv_done = sem("ssd_conv_done")
        ssd_operand = sem("ssd_operand")
        state_operand = sem("state_operand")
        state_ready = sem("state_ready")
        tables_ready = sem("tables_ready")
        tile_operands = sem("tile_operands")
        token_major = sem("token_major")
        u_ready = sem("u_ready")
        w_ready = sem("w_ready")
        x_added = sem("x_added")
        x_ready = sem("x_ready")
        xbc_ready = sem("xbc_ready")

        pe, dve, act, sp = nc.tensor, nc.vector, nc.scalar, nc.sync
        block = ctx.enter_context(nc.Block())

        def along(c, a, b):
            return c.unsqueeze(2).to_broadcast([P, a, b])

        def over(c, a, b):
            return c.unsqueeze(1).to_broadcast([P, a, b])

        class Job:

            def __init__(self, n, kt, rhs, loads, slots, by_token=False, width=COLS, per=1):
                self.n, self.kt, self.rhs, self.loads, self.slots = n, kt, rhs, loads, slots
                self.by_token, self.width, self.per = by_token, width, per
                self.at = None

            def each(self, eng, body):
                at = self.at
                if self.n >= 4:
                    assert at % 2 == 0 and self.n % 2 == 0 and at >= 2
                    with eng.Fori(0, self.n // 2) as j:
                        for s in range(2):
                            body(j * 2 + s, s, j + at // 2, j)
                    return
                for i in range(self.n):
                    body(i, (at + i) % 2, (at + i) // 2, i // 2)

        def load(job):
            def body(i, s, rounds, turn):
                if not isinstance(rounds, int) or rounds > 0:
                    sp.wait_ge(product[s].sem, rounds)
                for to, frm in job.loads(i, job.slots[s]):
                    sp.dma_start(to, frm).then_inc(landed[s].sem, 16)

            job.each(sp, body)

        dmas = [0, 0]

        def multiply(job):
            n = job.rhs.shape[2]

            def body(i, s, rounds, turn):
                pe.wait_ge(landed[s].sem, turn * (16 * job.per) + 16 * (dmas[s] + job.per))
                if not isinstance(rounds, int) or rounds > 0:
                    pe.wait_ge(evicted[s].sem, rounds)
                w = job.slots[s]
                bank = psum[s].rearrange("p (a b) -> p a b", a=2)
                if job.by_token:
                    for t in range(TT):
                        for k in range(job.kt):
                            last = pe.matmul(bank[:, t, 0:job.width], job.rhs[:, k, t * P:t * P + P],
                                             w[:, k, 0:job.width], start=k == 0, stop=k == job.kt - 1)
                else:
                    for m in range(-(-job.width // P)):
                        c = min(P, job.width - m * P)
                        for k in range(job.kt):
                            last = pe.matmul(bank[0:c, m, 0:n], w[:, k, m * P:m * P + c], job.rhs[:, k, :],
                                             start=k == 0, stop=k == job.kt - 1)
                last.then_inc(product[s].sem, 1)

            job.each(pe, body)
            for i in range(job.n):
                dmas[(job.at + i) % 2] += job.per

        def evict(eng, job, step):
            def body(i, s, rounds, turn):
                eng.wait_ge(product[s].sem, rounds + 1)
                step(i, psum[s].rearrange("p (a b) -> p a b", a=2), evicted[s].sem, rounds)

            job.each(eng, body)

        def halves(s, job):
            return (job.at + job.n + 1 - s) // 2

        def column_loads(w, lo, c=COLS, step=COLS):
            v = w.rearrange("(k p) n -> p k n", p=P)
            kt = v.shape[1]

            def loads(i, slot):
                frm = v[:, :, lo + i * step:lo + i * step + c] if isinstance(i, int) else v[:, :, bass.ds(i * step + lo, c)]
                return [(slot[:, 0:kt, 0:c], frm)]
            return loads

        def two(dst, i, lo=0, n=T):
            if isinstance(i, int):
                return dst[:, 2 * i:2 * i + 2, lo:lo + n]
            return dst[:, bass.ds(i * 2, 2), lo:lo + n]

        def tokens(dst, i):
            if isinstance(i, int):
                return dst[:, :, i * COLS:(i + 1) * COLS]
            return dst[:, :, bass.ds(i * COLS, COLS)]

        def keep(dst, func, lo=0):
            return lambda i, bank, done, rounds: act.activation(two(dst, i, lo), bank, func).then_inc(done, 1)

        def keep_tokens(dst):
            return lambda i, bank, done, rounds: act.activation(tokens(dst, i), bank, ACT.Copy).then_inc(done, 1)

        def add_to_x(i, bank, done, rounds):
            dve.tensor_tensor(two(X, i), bank, two(X, i), ALU.add).then_inc(done, 1)

        def sums_pe(sq, nt, groups=1):
            pe.wait_ge(squares_ready.sem, squares_ready.due(pe))
            for g in range(groups):
                bank, free, done = abanks.fill()
                pe.wait_ge(free.sem, free.due(pe))
                for k in range(nt):
                    last = pe.matmul(bank[:, 0:T], ones, sq[:, g * nt + k, :], start=k == 0, stop=k == nt - 1)
                last.then_inc(done, 1)

        def rms_act(n, groups=1):
            for g in range(groups):
                bank, full, free = abanks.empty()
                act.wait_ge(full.sem, full.due(act))
                act.activation(STAT[:, g, :], bank[:, 0:T], ACT.Ln, bias=biases[:, 0:1], scale=1.0 / n)\
                   .then_inc(free.sem, 1)
                act.wait_ge(free.sem, free.due(act))
            act.activation(STAT[:, 0:groups, :], STAT[:, 0:groups, :], ACT.Exp, scale=-0.5)\
               .then_inc(rms_ready.sem, 1)
            act.wait_ge(rms_ready.sem, rms_ready.due(act))

        def norm_v(src, sq, nt, gain, dst, groups=1, shift=None):
            dve.tensor_tensor(sq, src, src, ALU.mult)\
               .then_inc(squares_ready.sem, 1)
            dve.wait_ge(squares_ready.sem, squares_ready.due(dve))
            dve.wait_ge(rms_ready.sem, rms_ready.due(dve))
            n = groups * nt
            for k in range(n):
                by = vector_step if shift or k < n - 1 else normed
                dve.scalar_tensor_tensor(dst[:, k, :], src[:, k, :], gain(k), STAT[:, k // nt, :], ALU.mult, ALU.mult)\
                   .then_inc(by.sem, 1)
                by_due = by.due(dve)
            dve.wait_ge(by.sem, by_due)
            if shift:
                for k in range(n):
                    by = vector_step if k < n - 1 else normed
                    dve.tensor_scalar(dst[:, k, :], dst[:, k, :], shift(k), None, ALU.add).then_inc(by.sem, 1)
                    by_due = by.due(dve)
                dve.wait_ge(by.sem, by_due)

        def head_sums_pe(sq, nt, banks, wait=True):
            if wait:
                pe.wait_ge(head_squares.sem, head_squares.due(pe))
            for k in range(0, nt, 2):
                bank, free, done = banks.fill()
                pe.wait_ge(free.sem, free.due(pe))
                pe.matmul(bank, ones64, flat(sq[:, k:k + 2, :]), start=True, stop=True).then_inc(done, 1)

        def turn_pe(pieces, banks):
            for i in range(0, len(pieces), 4):
                bank, free, done = banks.fill()
                pe.wait_ge(free.sem, free.due(pe))
                for n, x in enumerate(pieces[i:i + 4]):
                    last = pe.transpose(bank[:, n * P:n * P + P], x, ident)
                last.then_inc(done, 1)

        def softplus_v(x, a, b, c, dst):
            dve.scalar_tensor_tensor(a, x, -1.0, x, ALU.mult, ALU.min)\
               .then_inc(softplus_in.sem, 1)
            dve.wait_ge(softplus_in.sem, softplus_in.due(dve))
            dve.wait_ge(softplus_exp.sem, softplus_exp.due(dve))
            dve.tensor_scalar(b, a, 2.0, None, ALU.add)\
               .then_inc(vector_step.sem, 1)
            dve.wait_ge(vector_step.sem, vector_step.due(dve))
            dve.reciprocal(b, b)\
               .then_inc(vector_step.sem, 1)
            dve.wait_ge(vector_step.sem, vector_step.due(dve))
            dve.tensor_tensor(a, a, b, ALU.mult)\
               .then_inc(vector_step.sem, 1)
            dve.wait_ge(vector_step.sem, vector_step.due(dve))
            dve.tensor_tensor(b, a, a, ALU.mult)\
               .then_inc(vector_step.sem, 1)
            dve.wait_ge(vector_step.sem, vector_step.due(dve))
            dve.tensor_scalar(c, b, 1.0 / 17, None, ALU.mult)\
               .then_inc(vector_step.sem, 1)
            dve.wait_ge(vector_step.sem, vector_step.due(dve))
            for n in (15, 13, 11, 9, 7, 5, 3):
                dve.scalar_tensor_tensor(c, c, 1.0 / n, b, ALU.add, ALU.mult)\
                   .then_inc(vector_step.sem, 1)
                dve.wait_ge(vector_step.sem, vector_step.due(dve))
            dve.scalar_tensor_tensor(c, c, 1.0, a, ALU.add, ALU.mult)\
               .then_inc(vector_step.sem, 1)
            dve.wait_ge(vector_step.sem, vector_step.due(dve))
            dve.tensor_scalar(b, x, 0.0, None, ALU.max)\
               .then_inc(vector_step.sem, 1)
            dve.wait_ge(vector_step.sem, vector_step.due(dve))
            dve.scalar_tensor_tensor(dst, c, 2.0, b, ALU.mult, ALU.add)\
               .then_inc(vector_step.sem, 1)
            dve.wait_ge(vector_step.sem, vector_step.due(dve))

        def softplus_act(a):
            act.wait_ge(softplus_in.sem, softplus_in.due(act))
            act.activation(a, a, ACT.Exp)\
               .then_inc(softplus_exp.sem, 1)
            act.wait_ge(softplus_exp.sem, softplus_exp.due(act))

        w_in = A["rec_w_in"][0]
        dt_cols = w_in.rearrange("(k p) n -> p k n", p=P)
        rec_dt = Job(2, DK, H, lambda i, slot: [(slot[:, 0:DK, 0:8], dt_cols[:, :, 4608 + 8 * i:4616 + 8 * i])],
                     WIDE, by_token=True, width=8)
        rec_x = Job(4, DK, H, column_loads(w_in, 0), WIDE)
        rec_xbc = Job(6, DK, H, column_loads(w_in, 3 * D), WIDE)
        rec_gate = Job(4, DK, H, column_loads(w_in, D), WIDE)
        rec_z = Job(4, DK, H, column_loads(w_in, 2 * D), WIDE)
        rec_out = Job(4, 16, MIX, column_loads(A["rec_w_out"][0], 0), WIDE)
        att_q, att_k, att_v = (Job(4, DK, H, column_loads(A["att_w_qkv"][0], n * D), WIDE, by_token=n == 2) for n in range(3))
        att_out = Job(4, DK, O, column_loads(A["att_w_out"][0], 0), WIDE)

        def ffn_loads(l):
            up = A["ffn_w_gate_up"][l].rearrange("(k p) n -> p k n", p=P)

            def loads(i, slot):
                lo = 0 if slot is WIDE[0] else FFN - COLS // 2
                return [(slot[:, 0:DK, :], up[:, :, bass.ds(i * (COLS // 2) + lo, COLS)])]
            return loads

        ffn_up = [Job(2 * FFN // COLS, DK, H, ffn_loads(l), WIDE) for l in range(2)]
        ffn_down = [Job(4, FFN // P, hidden, column_loads(A["ffn_w_down"][l], 0), WIDE) for l in range(2)]
        first_jobs = [rec_dt, rec_x, rec_gate, rec_xbc, rec_z, rec_out, ffn_up[0], ffn_down[0],
                      att_q, att_k, att_v, att_out, ffn_up[1], ffn_down[1]]

        def second_jobs(l):
            w = A["w_in_2"][l]
            wv = w.rearrange("(k p) n -> p k n", p=P)
            uq = A["mla_w_uq_2"][l].rearrange("(k p) (h c) -> p k h c", p=P, c=192)
            ukv = A["mla_w_ukv_2"][l].rearrange("(k p) (h c) -> p k h c", p=P, c=256)

            def proj(name, n, rhs=H, **kw):
                return Job(n, DK, rhs, column_loads(w, IN_AT[name]), SL, **kw)

            def kr_loads(i, slot):
                frm = wv[:, :, IN_AT["kr"]:IN_AT["kr"] + 64]
                return [(slot[:, 0:DK, 0:64], frm), (slot[:, 0:DK, 64:128], frm)]

            def head_loads(v, kt, heads, lo, c):
                def loads(i, slot):
                    out = []
                    for k in range(kt):
                        to = slot[:, k, 0:heads * c].rearrange("p (h c) -> p h c", h=heads)
                        if isinstance(i, int):
                            out.append((to, v[:, k, i * heads:(i + 1) * heads, lo:lo + c]))
                        else:
                            out.append((to, v[:, k, bass.ds(i * heads, heads), lo:lo + c]))
                    return out
                return loads

            one = column_loads
            return {
                "ada": Job(12, DK, CA, column_loads(A["ada_w_2"][l], 0), SL),
                "cq": proj("cq", 2), "ckv": proj("ckv", 1),
                "kr": Job(1, DK, H, kr_loads, SL, width=128, per=2),
                "wl": Job(1, DK, H, one(w, IN_AT["wl"], 128), SL, width=128),
                "gl": Job(1, DK, H, one(w, IN_AT["gl"], 16), SL, width=16),
                "mz": proj("mz", 4), "ga": proj("ga", 4),
                "uqn": Job(4, 4, CQ, head_loads(uq, 4, 2, 0, 128), SL, per=4),
                "uqr": Job(2, 4, CQ, head_loads(uq, 4, 4, 128, 64), SL, per=4),
                "ukn": Job(4, 2, CKV, head_loads(ukv, 2, 2, 0, 128), SL, per=2),
                "ukv": Job(4, 2, CKV, head_loads(ukv, 2, 2, 128, 128), SL, per=2, by_token=True),
                "mo": Job(4, DK, OM, column_loads(A["mla_w_o_2"][l], 0), SL),
                "r": proj("r", 4), "k": proj("k", 4), "v": proj("v", 4),
                "rz": proj("rz", 4), "gb": proj("gb", 4),
                "ro": Job(4, DK, R, column_loads(A["rwkv_w_o_2"][l], 0), SL),
                "gq": proj("gq", 2), "gk": proj("gk", 2), "gv": proj("gv", 4, by_token=True),
                "gz": proj("gz", 4), "gc": proj("gc", 4),
                "go": Job(4, DK, OG, column_loads(A["gla_w_o_2"][l], 0), SL),
                "out": Job(4, DK, M, column_loads(A["w_out_2"][l], 0), SL),
            }

        second = [second_jobs(l) for l in range(2)]
        at = 0
        for j in first_jobs + [j for l in range(2) for j in second[l].values()]:
            j.at = at
            at += j.n

        def attend_pe(heads, score, value, turned):
            for i in range(heads + 2):
                if i < heads:
                    bank, free, done = vbanks.fill()
                    pe.wait_ge(free.sem, free.due(pe))
                    score(i, bank.rearrange("p (a b) -> p a b", a=TT)).then_inc(done, 1)
                if 1 <= i <= heads:
                    pe.wait_ge(probs_scaled.sem, probs_scaled.due(pe))
                    pr = turned[0][(i - 1) % 2]
                    bank, free, done = abanks.fill()
                    pe.wait_ge(free.sem, free.due(pe))
                    for s in range(TT):
                        for t in range(TT):
                            last = pe.transpose(bank[:, s * T + t * P:s * T + t * P + P], pr[:, t, s * P:s * P + P], ident)
                    last.then_inc(done, 1)
                if i >= 2:
                    pe.wait_ge(probs_turned.sem, probs_turned.due(pe))
                    bank, free, done = vbanks.fill()
                    pe.wait_ge(free.sem, free.due(pe))
                    for s in range(TT):
                        last = pe.matmul(bank[:, 0:T], value(i - 2, s), turned[1][i % 2][:, s, :], start=s == 0, stop=s == TT - 1)
                    last.then_inc(done, 1)

        def attend_v(heads, scale, mask, sc, pr, mx, sm, take):
            for i in range(heads + 2):
                if i < heads:
                    bank, full, free = vbanks.empty()
                    dve.wait_ge(full.sem, full.due(dve))
                    dve.scalar_tensor_tensor(flat(sc[i % 2]), bank, scale, mask, ALU.mult, ALU.add)\
                       .then_inc(free.sem, 1)
                    dve.wait_ge(free.sem, free.due(dve))
                    dve.reduce_max(mx[i % 2], sc[i % 2], axis=AX)\
                       .then_inc(vector_step.sem, 1)
                    dve.wait_ge(vector_step.sem, vector_step.due(dve))
                    dve.tensor_scalar(mx[i % 2], mx[i % 2], -1.0, None, ALU.mult)\
                       .then_inc(scores_ready.sem, 1)
                    dve.wait_ge(scores_ready.sem, scores_ready.due(dve))
                if 1 <= i <= heads:
                    dve.wait_ge(probs_ready.sem, probs_ready.due(dve))
                    n = (i - 1) % 2
                    dve.reciprocal(sm[n], sm[n])\
                       .then_inc(vector_step.sem, 1)
                    dve.wait_ge(vector_step.sem, vector_step.due(dve))
                    dve.tensor_tensor(pr[n], pr[n], along(sm[n], TT, T), ALU.mult)\
                       .then_inc(probs_scaled.sem, 1)
                    dve.wait_ge(probs_scaled.sem, probs_scaled.due(dve))
                if i >= 2:
                    bank, full, free = vbanks.empty()
                    dve.wait_ge(full.sem, full.due(dve))
                    take(i - 2, bank[:, 0:T], free)

        def attend_act(heads, sc, pr, pt, mx, sm):
            for i in range(heads + 1):
                if i < heads:
                    act.wait_ge(scores_ready.sem, scores_ready.due(act))
                    n = i % 2
                    for t in range(TT):
                        sig = probs_ready if t else scalar_step
                        act.activation(pr[n][:, t, :], sc[n][:, t, :], ACT.Exp, bias=mx[n][:, t:t + 1],
                            accum_out=sm[n][:, t:t + 1])\
                           .then_inc(sig.sem, 1)
                        act.wait_ge(sig.sem, sig.due(act))
                if i >= 1:
                    bank, full, free = abanks.empty()
                    act.wait_ge(full.sem, full.due(act))
                    act.activation(flat(pt[(i - 1) % 2]), bank, ACT.Copy)\
                       .then_inc(free.sem, 1)
                    act.wait_ge(free.sem, free.due(act))
                    act.nop().then_inc(probs_turned.sem, 1)

        n_inputs = 2 + len(VEC_AT) + 2

        def take_in_pe():
            pe.wait_ge(inputs_landed.sem, inputs_landed.due(pe, 16 * n_inputs))
            turn_pe([PACK[:, i, :] for i in range(PACKS)], vbanks)
            turn_pe([XIN[:, t, k * P:k * P + P] for k in range(DK) for t in range(TT)], vbanks)

        def lru_pe():
            pe.wait_ge(lru_conv_done.sem, lru_conv_done.due(pe))
            pe.wait_ge(lru_weights_landed.sem, lru_weights_landed.due(pe, 64))
            for k in range(DK):
                bank, free, done = abanks.fill()
                pe.wait_ge(free.sem, free.due(pe))
                pe.matmul(bank[:, 0:T], BD[:, 0, k, :], XC[:, k, :], start=True, stop=True)
                pe.matmul(bank[:, T:], BD[:, 1, k, :], XC[:, k, :], start=True, stop=True).then_inc(done, 1)

        def ssd_pe():
            for t in range(TT):
                here = slice(t * P, t * P + P)
                pe.wait_ge(decay_steps.sem, decay_steps.due(pe))
                bank, free, done = vbanks.fill()
                pe.wait_ge(free.sem, free.due(pe))
                pe.matmul(bank[:, 0:16], tri, DTB[:, t, :], start=True, stop=True).then_inc(done, 1)
                for h in range(0, 16, 4):
                    bank, free, done = vbanks.fill()
                    pe.wait_ge(free.sem, free.due(pe))
                    pe.matmul(bank, ones, flat(ADTRI[:, h:h + 4, :]), start=True, stop=True).then_inc(done, 1)
                if t == 0:
                    pe.wait_ge(xbc_ready.sem, xbc_ready.due(pe))
                bank, free, done = vbanks.fill()
                pe.wait_ge(free.sem, free.due(pe))
                for g in range(2):
                    last = pe.matmul(bank[:, g * P:g * P + P], XBC[:, 8 + g, here], XBC[:, 10 + g, here], start=True, stop=True)
                last.then_inc(done, 1)
                turn_pe([XBC[:, k, here] for k in range(DK)], vbanks)
                if t == 0:
                    turn_pe([XBC[:, 8 + g, here] for g in range(2)], vbanks)
                    pe.wait_ge(state_operand.sem, state_operand.due(pe))
                    for g in range(2):
                        bank, free, done = vbanks.fill()
                        pe.wait_ge(free.sem, free.due(pe))
                        pe.matmul(bank, BTOK[:, g, :], XDTE[:, g * 512:g * 512 + 512], start=True, stop=True).then_inc(done, 1)
                pe.wait_ge(ssd_operand.sem, ssd_operand.due(pe))
                for h in range(0, 16, 4):
                    bank, free, done = vbanks.fill()
                    pe.wait_ge(free.sem, free.due(pe))
                    for n in range(4):
                        e = (h + n) // 2
                        o = bank[:, n * P:n * P + P]
                        last = pe.matmul(o, XTOK[:, t, e * P:e * P + P], SEG[:, h + n, :], start=True, stop=t == 0)
                        if t:
                            last = pe.matmul(o, PREV[:, e // 4, (e % 4) * P:(e % 4) * P + P], ECS[:, h + n, :], start=False, stop=True)
                    last.then_inc(done, 1)

        def ffn_pe(l):
            sums_pe(SQF, DK)
            pe.wait_ge(normed.sem, normed.due(pe))
            multiply(ffn_up[l])
            pe.wait_ge(hidden_ready.sem, hidden_ready.due(pe))
            multiply(ffn_down[l])

        def att_pe():
            sums_pe(SQA, DK)
            pe.wait_ge(normed.sem, normed.due(pe))
            multiply(att_q)
            multiply(att_k)
            multiply(att_v)
            for x in (Q, K):
                head_sums_pe(SQA, DK, abanks)
                pe.wait_ge(head_normed.sem, head_normed.due(pe))
                for k in range(0, DK, 2):
                    bank, free, done = vbanks.fill()
                    pe.wait_ge(free.sem, free.due(pe))
                    pe.matmul(bank, const("att_rot"), flat(x[:, k:k + 2, :]), start=True, stop=True).then_inc(done, 1)
            pe.wait_ge(keys_ready.sem, keys_ready.due(pe))

            def score(h, bank):
                for t in range(TT):
                    last = pe.matmul(bank[:, t, :], Q[:, h // 2, t * P:t * P + P], KP[:, h, :], start=True, stop=True)
                return last

            pe.wait_ge(evicted[0].sem, halves(0, att_v))

            pe.wait_ge(evicted[1].sem, halves(1, att_v))
            attend_pe(16, score, lambda h, s: VT[:, s, (h // 2) * P:(h // 2) * P + P], (PR, PT))
            pe.wait_ge(heads_out.sem, heads_out.due(pe))
            multiply(att_out)

        def mla_pe(j):
            for n in ("cq", "ckv", "kr", "wl", "gl", "mz", "ga"):
                multiply(j[n])
            sums_pe(SQM, 4)
            pe.wait_ge(normed.sem, normed.due(pe))
            multiply(j["uqn"])
            multiply(j["uqr"])
            sums_pe(SQM, 2)
            pe.wait_ge(normed.sem, normed.due(pe))
            multiply(j["ukn"])
            multiply(j["ukv"])
            pe.wait_ge(evicted[0].sem, halves(0, j["ukv"]))
            pe.wait_ge(evicted[1].sem, halves(1, j["ukv"]))
            for x, nt in ((QR, 4), (KR, 1)):
                for k in range(0, nt, 2):
                    bank, free, done = vbanks.fill()
                    pe.wait_ge(free.sem, free.due(pe))
                    n = min(2, nt - k)
                    pe.matmul(bank[:, 0:n * T], const("mla_rot"), flat(x[:, k:k + n, :]), start=True, stop=True).then_inc(done, 1)
            pe.wait_ge(keys_ready.sem, keys_ready.due(pe))

            def score(h, bank):
                for t in range(TT):
                    here = slice(t * P, t * P + P)
                    pe.matmul(bank[:, t, :], QN[:, h, here], KN[:, h, :], start=True, stop=False)
                    last = pe.matmul(bank[:, t, :], QR[:, h // 2, here], KRP[:, h % 2, :], start=False, stop=True)
                return last

            attend_pe(8, score, lambda h, s: VM[:, s, h * P:h * P + P], (MPR, MPT))
            pe.wait_ge(heads_out.sem, heads_out.due(pe))
            multiply(j["mo"])

        def rwkv_pe(j):
            for n in ("r", "k", "v"):
                multiply(j[n])
            pe.wait_ge(lora_ready.sem, lora_ready.due(pe))
            pe.wait_ge(lora_weights.sem, lora_weights.due(pe, 32))
            for k in range(DK):
                bank, free, done = abanks.fill()
                pe.wait_ge(free.sem, free.due(pe))
                pe.matmul(bank[:, 0:T], flat(W2)[:, k * P:k * P + P], WL[:, 1:], start=True, stop=True)
                pe.matmul(bank[:, T:], flat(W2)[:, D + k * P:D + k * P + P], WL[:, 1:], start=True, stop=True).then_inc(done, 1)
            head_sums_pe(SQR, DK, abanks)
            head_sums_pe(SQR, DK, vbanks)
            for t in range(TT):
                pe.wait_ge(tile_operands.sem, tile_operands.due(pe))
                rd, kkd, kd, bd = (x[:, :, t * P:t * P + P] for x in (R, KKD, KR_, BDF))
                turn_pe([V_[:, k, t * P:t * P + P] for k in range(DK)], abanks)
                turn_pe([kkd[:, k, :] for k in range(DK)], abanks)
                turn_pe([kd[:, k, :] for k in range(DK)], abanks)
                turn_pe([bd[:, k, :] for k in range(DK)], abanks)
                for k in range(0, DK, 2):
                    bank, free, done = vbanks.fill()
                    pe.wait_ge(free.sem, free.due(pe))
                    for n in range(4):
                        last = pe.matmul(bank[:, n * P:n * P + P], PAD[:, (k + n // 2) * 4 + n % 2, :], bd[:, k + n // 2, :], start=True, stop=True)
                    last.then_inc(done, 1)
                for k in range(0, DK, 2):
                    bank, free, done = vbanks.fill()
                    pe.wait_ge(free.sem, free.due(pe))
                    for n in range(2):
                        last = pe.matmul(bank[:, n * T:n * T + T], kd[:, k + n, :], flat(PAD[:, (k + n) * 4:(k + n) * 4 + 2, :]), start=True, stop=True)
                    last.then_inc(done, 1)
                for h in range(0, 16, 4):
                    if h == 0:
                        pe.wait_ge(a_ready.sem, a_ready.due(pe))
                    turn_pe([AN[:, h + n, :] for n in range(4)], vbanks)
                for level in range(1, 6):
                    for h in range(0, 16, 4):
                        pe.wait_ge(inverse_ready.sem, inverse_ready.due(pe))
                        turn_pe([XT[:, h + n, :] for n in range(4)], abanks)
                    for h in range(0, 16, 4):
                        bank, free, done = abanks.fill()
                        pe.wait_ge(free.sem, free.due(pe))
                        for n in range(4):
                            last = pe.matmul(bank[:, n * P:n * P + P], AN[:, h + n, :], XT[:, h + n, :], start=True, stop=True)
                        last.then_inc(done, 1)
                    for h in range(0, 16, 4):
                        pe.wait_ge(level_operands.sem, level_operands.due(pe))
                        bank, free, done = vbanks.fill()
                        pe.wait_ge(free.sem, free.due(pe))
                        for n in range(4):
                            last = pe.matmul(bank[:, n * P:n * P + P], XX[:, h + n, :], QQ[:, h + n, :], start=True, stop=True)
                        last.then_inc(done, 1)
                pe.wait_ge(inverse_ready.sem, inverse_ready.due(pe, 4))
                pe.wait_ge(token_major.sem, token_major.due(pe))
                for h in range(0, 16, 8):
                    bank, free, done = vbanks.fill()
                    pe.wait_ge(free.sem, free.due(pe))
                    for n in range(8):
                        last = pe.matmul(bank[:, n * 64:n * 64 + 64], BT[:, h + n, :], VTK[:, (h + n) * 64:(h + n) * 64 + 64], start=True, stop=True)
                    last.then_inc(done, 1)
                for h in range(0, 16, 4):
                    bank, free, done = vbanks.fill()
                    pe.wait_ge(free.sem, free.due(pe))
                    for n in range(4):
                        e = (h + n) // 2
                        last = pe.matmul(bank[:, n * P:n * P + P], KKT[:, e * P:e * P + P], XT[:, h + n, :], start=True, stop=True)
                    last.then_inc(done, 1)
                pe.wait_ge(bv_ready.sem, bv_ready.due(pe))
                for h in range(0, 16, 8):
                    bank, free, done = vbanks.fill()
                    pe.wait_ge(free.sem, free.due(pe))
                    for n in range(8):
                        last = pe.matmul(bank[:, n * 64:n * 64 + 64], XT[:, h + n, :], BVT[:, (h + n) * 64:(h + n) * 64 + 64], start=True, stop=True)
                    last.then_inc(done, 1)
                for n, x in enumerate((bd, kd)):
                    for k in range(0, DK, 2):
                        bank, free, done = vbanks.fill()
                        pe.wait_ge(free.sem, free.due(pe))
                        for m in range(2):
                            last = pe.matmul(bank[:, m * T:m * T + T], x[:, k + m, :], flat(PAD[:, (k + m) * 4 + 2:(k + m) * 4 + 4, :]), start=True, stop=True)
                        last.then_inc(done, 1)
                pe.wait_ge(w_ready.sem, w_ready.due(pe))
                for c in range(2):
                    pe.wait_ge(state_ready.sem, state_ready.due(pe))
                    for k in range(0, DK, 4):
                        bank, free, done = vbanks.fill()
                        pe.wait_ge(free.sem, free.due(pe))
                        for n in range(4):
                            last = pe.matmul(bank[:, n * P:n * P + P], WT[:, k + n, :], ST[c][:, k + n, :], start=True, stop=True)
                        last.then_inc(done, 1)
                    pe.wait_ge(u_ready.sem, u_ready.due(pe))
                    if c == 1:
                        for h in range(0, 16, 4):
                            bank, free, done = vbanks.fill()
                            pe.wait_ge(free.sem, free.due(pe))
                            for n in range(4):
                                e, o = (h + n) // 2, bank[:, n * P:n * P + P]
                                at = slice(e * P, e * P + P)
                                pe.matmul(o, UT[:, at], XX[:, h + n, :], start=True, stop=False)
                                pe.matmul(o, VTK[:, at], QQ[:, h + n, :], start=False, stop=False)
                                pe.matmul(o[:, 0:CH], ST[0][:, e, :], rd[:, e, 0:CH], start=False, stop=False)
                                last = pe.matmul(o[:, CH:P], ST[1][:, e, :], rd[:, e, CH:P], start=False, stop=True)
                            last.then_inc(done, 1)
                    if (t, c) != (TT - 1, 1):
                        for k in range(0, DK, 4):
                            bank, free, done = vbanks.fill()
                            pe.wait_ge(free.sem, free.due(pe))
                            for n in range(4):
                                at = slice((k + n) * P, (k + n) * P + P)
                                pe.matmul(bank[:, n * P:n * P + P], BDT[c][:, at], UT[:, at], start=True, stop=False)
                                last = pe.matmul(bank[:, n * P:n * P + P], KDT[c][:, at], VTK[:, at], start=False, stop=True)
                            last.then_inc(done, 1)
            head_sums_pe(R, DK, vbanks)
            head_sums_pe(SQT, DK, abanks)
            for n in ("rz", "gb"):
                multiply(j[n])
            pe.wait_ge(branch_ready.sem, branch_ready.due(pe))
            multiply(j["ro"])

        def gla_pe(j):
            for n in ("gq", "gk", "gv"):
                multiply(j[n])
            pe.wait_ge(evicted[0].sem, halves(0, j["gv"]))
            pe.wait_ge(evicted[1].sem, halves(1, j["gv"]))
            pe.wait_ge(lora_weights.sem, lora_weights.due(pe, 16))
            for h in range(0, 4, 2):
                bank, free, done = vbanks.fill()
                pe.wait_ge(free.sem, free.due(pe))
                for n in range(2):
                    last = pe.matmul(bank[:, n * T:n * T + T], G2[0:16, (h + n) * P:(h + n) * P + P], GL[0:16, :], start=True, stop=True)
                last.then_inc(done, 1)
            pe.wait_ge(gla_operands.sem, gla_operands.due(pe))
            for t in range(TT):
                here = slice(t * P, t * P + P)
                turn_pe([KTE[:, h, here] for h in range(4)], abanks)
                bank, free, done = vbanks.fill()
                pe.wait_ge(free.sem, free.due(pe))
                for h in range(4):
                    last = pe.matmul(bank[:, h * P:h * P + P], KINV[:, h, here], GX[:, h, here], start=True, stop=True)
                last.then_inc(done, 1)
                pe.wait_ge(token_major.sem, token_major.due(pe))
                for c in range(2):
                    if (t, c) != (TT - 1, 1):
                        for h in range(0, 4, 2):
                            bank, free, done = vbanks.fill()
                            pe.wait_ge(free.sem, free.due(pe))
                            for n in range(2):
                                last = pe.matmul(bank[:, n * T:n * T + T], KTT[c][:, h + n, :], GV[:, t, (h + n) * T:(h + n) * T + T], start=True, stop=True)
                            last.then_inc(done, 1)
                pe.wait_ge(gla_states.sem, gla_states.due(pe))
                for h in range(0, 4, 2):
                    bank, free, done = vbanks.fill()
                    pe.wait_ge(free.sem, free.due(pe))
                    for n in range(4):
                        hh, v = h + n // 2, n % 2
                        o = bank[:, n * P:n * P + P]
                        last = pe.matmul(o, GV[:, t, hh * T + v * P:hh * T + v * P + P], AT[:, hh, :], start=True, stop=False)
                        for c in range(2):
                            g = 2 * t + c
                            if g:
                                last = pe.matmul(o[:, c * CH:c * CH + CH], GS[g][:, hh, v * P:v * P + P],
                                                 GX[:, hh, g * CH:g * CH + CH], start=False, stop=c == 1)
                    last.then_inc(done, 1)
            sums_pe(SQG, 2, 4)
            pe.wait_ge(normed.sem, normed.due(pe))
            for n in ("gz", "gc"):
                multiply(j[n])
            pe.wait_ge(branch_ready.sem, branch_ready.due(pe))
            multiply(j["go"])

        @block.tensor
        def _(_pe):
            take_in_pe()
            sums_pe(XC, DK)
            pe.wait_ge(normed.sem, normed.due(pe))
            for j in (rec_dt, rec_x, rec_gate, rec_xbc, rec_z):
                multiply(j)
            lru_pe()
            ssd_pe()
            sums_pe(UU, 4, 2)
            pe.wait_ge(normed.sem, normed.due(pe))
            multiply(rec_out)
            ffn_pe(0)
            att_pe()
            ffn_pe(1)
            for l in range(2):
                j = second[l]
                if l == 0:
                    pe.wait_ge(condition_ready.sem, condition_ready.due(pe))
                multiply(j["ada"])
                sums_pe(SQM, DK)
                pe.wait_ge(normed.sem, normed.due(pe))
                mla_pe(j)
                rwkv_pe(j)
                gla_pe(j)
                pe.wait_ge(merge_ready.sem, merge_ready.due(pe))
                multiply(j["out"])
                sums_pe(SQM, DK)
                pe.wait_ge(normed.sem, normed.due(pe))
            pe.wait_ge(x_ready.sem, x_ready.due(pe))
            turn_pe([X[:, k, t * P:t * P + P] for t in range(TT) for k in range(DK)], vbanks)

        def conv_v(src, nt, w, b, dst, by):
            for k in range(nt):
                dve.tensor_scalar(dst[:, k, :], src[:, k, 0:T], col(w, k), col(b, k), ALU.mult, ALU.add)\
                   .then_inc(vector_step.sem, 1)
                dve.wait_ge(vector_step.sem, vector_step.due(dve))
                for n in range(1, 4):
                    sig = by if (k, n) == (nt - 1, 3) else vector_step
                    dve.scalar_tensor_tensor(dst[:, k, :], src[:, k, n:n + T], col(w, n * nt + k),
                        dst[:, k, :], ALU.mult, ALU.add)\
                       .then_inc(sig.sem, 1)
                    dve.wait_ge(sig.sem, sig.due(dve))

        def halves_v(dst, bank, free):
            b = bank.rearrange("p (k e t) -> p k e t", k=2, e=2)
            dve.tensor_copy(dst[0:64], b[0:64, :, 0, :])\
               .then_inc(vector_step.sem, 1)
            dve.wait_ge(vector_step.sem, vector_step.due(dve))
            dve.tensor_copy(dst[64:128], b[64:128, :, 1, :])\
               .then_inc(free.sem, 1)
            dve.wait_ge(free.sem, free.due(dve))

        def take_in_v():
            dve.memset(flat(PACK), 0.0)\
               .then_inc(packs_zeroed.sem, 1)
            dve.wait_ge(packs_zeroed.sem, packs_zeroed.due(dve))
            dve.memset(biases[:, 0:1], EPS)\
               .then_inc(vector_step.sem, 1)
            dve.wait_ge(vector_step.sem, vector_step.due(dve))
            dve.memset(biases[:, 1:2], GN_EPS)\
               .then_inc(vector_step.sem, 1)
            dve.wait_ge(vector_step.sem, vector_step.due(dve))
            dve.memset(biases[:, 2:3], 1.0)\
               .then_inc(biases_set.sem, 1)
            dve.wait_ge(biases_set.sem, biases_set.due(dve))
            for i in range(0, PACKS, 4):
                bank, full, free = vbanks.empty()
                dve.wait_ge(full.sem, full.due(dve))
                n = min(4, PACKS - i)
                dve.tensor_copy(cols[:, i * P:(i + n) * P], bank[:, 0:n * P])\
                   .then_inc(free.sem, 1)
                dve.wait_ge(free.sem, free.due(dve))
            for k in range(0, DK, 2):
                bank, full, free = vbanks.empty()
                dve.wait_ge(full.sem, full.due(dve))
                dve.tensor_copy(flat(X[:, k:k + 2, :]), bank)\
                   .then_inc(free.sem, 1)
                dve.wait_ge(free.sem, free.due(dve))
            dve.memset(flat(BD.rearrange("p a b c -> p (a b) c")), 0.0)\
               .then_inc(lru_weights_zeroed.sem, 1)
            dve.wait_ge(lru_weights_zeroed.sem, lru_weights_zeroed.due(dve))
            dve.memset(LX[:, :, 0:3], 0.0)\
               .then_inc(vector_step.sem, 1)
            dve.wait_ge(vector_step.sem, vector_step.due(dve))
            dve.memset(XB[:, :, 0:3], 0.0)\
               .then_inc(conv_fronts_zeroed.sem, 1)
            dve.wait_ge(conv_fronts_zeroed.sem, conv_fronts_zeroed.due(dve))

        def rec_v():
            norm_v(X, XC, DK, lambda k: col("rec_norm", k), H)
            dve.tensor_scalar(LAMX, col("lru_lambda", 0, 8), -1.0, None, ALU.mult)\
               .then_inc(vector_step.sem, 1)
            dve.wait_ge(vector_step.sem, vector_step.due(dve))
            softplus_v(LAMX, LAMA, LAMB, LAMC, LAMD)
            dve.tensor_scalar(LAMD, LAMD, 8.0, None, ALU.mult)\
               .then_inc(vector_step.sem, 1)
            dve.wait_ge(vector_step.sem, vector_step.due(dve))
            dve.wait_ge(rows_landed.sem, rows_landed.due(dve, 48))
            dve.wait_ge(evicted[0].sem, halves(0, rec_dt))
            dve.wait_ge(evicted[1].sem, halves(1, rec_dt))
            dve.tensor_tensor(DT, DT, over(AROW[:, 0, :], TT, 16), ALU.add)\
               .then_inc(vector_step.sem, 1)
            dve.wait_ge(vector_step.sem, vector_step.due(dve))
            softplus_v(flat(DT), flat(DTB), flat(DTC), flat(DTD), flat(DT))
            dve.wait_ge(a_exp.sem, a_exp.due(dve))
            dve.scalar_tensor_tensor(DTB, DT, -1.0, over(AROW[:, 1, :], TT, 16), ALU.mult, ALU.mult)\
               .then_inc(vector_step.sem, 1)
            dve.wait_ge(vector_step.sem, vector_step.due(dve))
            dve.tensor_scalar(DCOL, AROW[:, 2, 0:16:2], half[:, 0:1], None, ALU.mult)\
               .then_inc(vector_step.sem, 1)
            dve.wait_ge(vector_step.sem, vector_step.due(dve))
            dve.scalar_tensor_tensor(DCOL, AROW[:, 2, 1:16:2], half[:, 1:2], DCOL, ALU.mult, ALU.add)\
               .then_inc(vector_step.sem, 1)
            dve.wait_ge(vector_step.sem, vector_step.due(dve))
            dve.wait_ge(evicted[0].sem, halves(0, rec_x))
            dve.wait_ge(evicted[1].sem, halves(1, rec_x))
            conv_v(LX, DK, "lru_conv_w", "lru_conv_b", XC, lru_conv_done)
            dve.wait_ge(evicted[0].sem, halves(0, rec_xbc))
            dve.wait_ge(evicted[1].sem, halves(1, rec_xbc))
            conv_v(XB, 12, "ssd_conv_w", "ssd_conv_b", XBC, ssd_conv_done)
            dve.wait_ge(lru_gates.sem, lru_gates.due(dve))
            dve.tensor_tensor(RG, RG, along(LAMD, DK, T), ALU.mult)\
               .then_inc(rate_ready.sem, 1)
            dve.wait_ge(rate_ready.sem, rate_ready.due(dve))
            dve.tensor_tensor(IG, IG, XC, ALU.mult)\
               .then_inc(vector_step.sem, 1)
            dve.wait_ge(vector_step.sem, vector_step.due(dve))
            dve.wait_ge(lru_functions.sem, lru_functions.due(dve))
            dve.tensor_tensor(UU, H, H, ALU.mult)\
               .then_inc(vector_step.sem, 1)
            dve.wait_ge(vector_step.sem, vector_step.due(dve))
            dve.scalar_tensor_tensor(flat(UU), flat(UU), 1.0, flat(RG), ALU.add, ALU.mult)\
               .then_inc(lru_root_in.sem, 1)
            dve.wait_ge(lru_root_in.sem, lru_root_in.due(dve))
            dve.wait_ge(lru_root.sem, lru_root.due(dve))
            dve.tensor_tensor(UU, UU, IG, ALU.mult)\
               .then_inc(vector_step.sem, 1)
            dve.wait_ge(vector_step.sem, vector_step.due(dve))
            for k in range(DK):
                dve.tensor_tensor_scan(RG[:, k, :], H[:, k, :], UU[:, k, :], 0.0, ALU.mult, ALU.add)\
                   .then_inc(vector_step.sem, 1)
                dve.wait_ge(vector_step.sem, vector_step.due(dve))
            dve.tensor_tensor(MIX[:, 0:DK, :], RG, G, ALU.mult)\
               .then_inc(vector_step.sem, 1)
            dve.wait_ge(vector_step.sem, vector_step.due(dve))
            ssd_v()
            dve.wait_ge(evicted[0].sem, halves(0, rec_z))
            dve.wait_ge(evicted[1].sem, halves(1, rec_z))
            dve.tensor_tensor(G, G, Z, ALU.mult)\
               .then_inc(vector_step.sem, 1)
            dve.wait_ge(vector_step.sem, vector_step.due(dve))
            norm_v(G, UU, 4, lambda k: col("ssd_norm", k), MIX[:, 8:16, :], 2)
            evict(dve, rec_out, add_to_x)

        def ssd_v():
            for t in range(TT):
                here = slice(t * P, t * P + P)
                dve.tensor_tensor(ADTRI, along(DTB[:, t, :], 16, P), over(tri, 16, P), ALU.mult)\
                   .then_inc(decay_steps.sem, 1)
                dve.wait_ge(decay_steps.sem, decay_steps.due(dve))
                bank, full, free = vbanks.empty()
                dve.wait_ge(full.sem, full.due(dve))
                dve.tensor_copy(CS[:, t, :], bank[:, 0:16])\
                   .then_inc(free.sem, 1)
                dve.wait_ge(free.sem, free.due(dve))
                for h in range(0, 16, 4):
                    bank, full, free = vbanks.empty()
                    dve.wait_ge(full.sem, full.due(dve))
                    b = bank.rearrange("p (h l) -> p h l", h=4)
                    if t == 0:
                        dve.tensor_copy(LAST[:, h:h + 4], b[:, :, P - 1])\
                           .then_inc(vector_step.sem, 1)
                        dve.wait_ge(vector_step.sem, vector_step.due(dve))
                    else:
                        dve.tensor_copy(ECS[:, h:h + 4, :], b)\
                           .then_inc(vector_step.sem, 1)
                        dve.wait_ge(vector_step.sem, vector_step.due(dve))
                    for n in range(4):
                        sig = free if n == 3 else vector_step
                        dve.tensor_scalar(SEG[:, h + n, :], b[:, n, :], CS[:, t, h + n:h + n + 1], 0.0,
                            ALU.subtract, ALU.min)\
                           .then_inc(sig.sem, 1)
                        dve.wait_ge(sig.sem, sig.due(dve))
                if t == 0:
                    dve.tensor_tensor(LAST, LAST, CS[:, 0, :], ALU.subtract)\
                       .then_inc(vector_step.sem, 1)
                    dve.wait_ge(vector_step.sem, vector_step.due(dve))
                dve.nop().then_inc(decay_in.sem, 1)
                bank, full, free = vbanks.empty()
                dve.wait_ge(full.sem, full.due(dve))
                dve.tensor_tensor(CBM, bank[:, 0:2 * P].rearrange("p (g l) -> p g l", g=2), over(tri, 2,
                    P), ALU.mult)\
                   .then_inc(free.sem, 1)
                dve.wait_ge(free.sem, free.due(dve))
                for k in range(0, DK, 4):
                    bank, full, free = vbanks.empty()
                    dve.wait_ge(full.sem, full.due(dve))
                    dve.tensor_tensor(XTOK[:, t, k * P:k * P + 512].rearrange("p (h c) -> p h c", h=8),
                        bank.rearrange("p (h c) -> p h c", h=8), along(DT[:, t, 2 * k:2 * k + 8], 8, 64), ALU.mult)\
                       .then_inc(free.sem, 1)
                    dve.wait_ge(free.sem, free.due(dve))
                dve.wait_ge(decay_out.sem, decay_out.due(dve))
                if t == 0:
                    bank, full, free = vbanks.empty()
                    dve.wait_ge(full.sem, full.due(dve))
                    dve.tensor_copy(flat(BTOK), bank[:, 0:2 * P])\
                       .then_inc(free.sem, 1)
                    dve.wait_ge(free.sem, free.due(dve))
                    dve.tensor_tensor(XDTE.rearrange("p (h c) -> p h c", h=16), XTOK[:, 0,
                        :].rearrange("p (h c) -> p h c", h=16), along(LAST, 16, 64), ALU.mult)\
                       .then_inc(state_operand.sem, 1)
                    dve.wait_ge(state_operand.sem, state_operand.due(dve))
                    for g in range(2):
                        bank, full, free = vbanks.empty()
                        dve.wait_ge(full.sem, full.due(dve))
                        dve.tensor_copy(PREV[:, g, :], bank)\
                           .then_inc(free.sem, 1)
                        dve.wait_ge(free.sem, free.due(dve))
                else:
                    for g in range(2):
                        dve.tensor_tensor(ECS[:, 8 * g:8 * g + 8, :], ECS[:, 8 * g:8 * g + 8, :],
                            over(XBC[:, 10 + g, here], 8, P), ALU.mult)\
                           .then_inc(vector_step.sem, 1)
                        dve.wait_ge(vector_step.sem, vector_step.due(dve))
                for g in range(2):
                    sig = ssd_operand if g else vector_step
                    dve.tensor_tensor(SEG[:, 8 * g:8 * g + 8, :], SEG[:, 8 * g:8 * g + 8, :],
                        over(CBM[:, g, :], 8, P), ALU.mult)\
                       .then_inc(sig.sem, 1)
                    dve.wait_ge(sig.sem, sig.due(dve))
                for k in range(0, DK, 2):
                    bank, full, free = vbanks.empty()
                    dve.wait_ge(full.sem, full.due(dve))
                    halves_v(G[:, k:k + 2, here], bank, free)
            for k in range(DK):
                dve.scalar_tensor_tensor(G[:, k, :], XBC[:, k, :], DCOL[:, k:k + 1], G[:, k, :],
                    ALU.mult, ALU.add)\
                   .then_inc(vector_step.sem, 1)
                dve.wait_ge(vector_step.sem, vector_step.due(dve))

        def ffn_v(l):
            dve.wait_ge(evicted[0].sem, halves(0, rec_out if l == 0 else att_out))
            dve.wait_ge(evicted[1].sem, halves(1, rec_out if l == 0 else att_out))
            norm_v(X, SQF, DK, lambda k: col("ffn_norm", 8 * l + k), H)
            job = ffn_up[l]
            base = job.at // 2
            with dve.Fori(0, job.n // 2) as j:
                dve.wait_ge(product[1].sem, j + (base + 1))
                dve.wait_ge(evicted[0].sem, j + (base + 1))
                dve.tensor_tensor(hidden[:, bass.ds(j * 2, 2), :], psum[1].rearrange("p (a b) -> p a b", a=2),
                                  silu_g, ALU.mult).then_inc(evicted[1].sem, 1)
            dve.wait_ge(evicted[1].sem, base + job.n // 2)
            dve.nop().then_inc(hidden_ready.sem, 1)
            evict(dve, ffn_down[l], add_to_x)

        def ffn_act(l):
            rms_act(D)
            base = ffn_up[l].at // 2
            with act.Fori(0, ffn_up[l].n // 2) as j:
                act.wait_ge(product[0].sem, j + (base + 1))
                act.wait_ge(evicted[1].sem, j + base)
                act.activation(silu_g, psum[0].rearrange("p (a b) -> p a b", a=2), ACT.Silu).then_inc(evicted[0].sem, 1)

        def attention_v():
            dve.wait_ge(evicted[0].sem, halves(0, ffn_down[0]))
            dve.wait_ge(evicted[1].sem, halves(1, ffn_down[0]))
            norm_v(X, SQA, DK, lambda k: col("att_norm", k), H)
            for x, job, gain in ((Q, att_q, "att_q_norm"), (K, att_k, "att_k_norm")):
                dve.wait_ge(evicted[0].sem, halves(0, job))
                dve.wait_ge(evicted[1].sem, halves(1, job))
                dve.tensor_tensor(SQA, x, x, ALU.mult)\
                   .then_inc(head_squares.sem, 1)
                dve.wait_ge(head_squares.sem, head_squares.due(dve))
                dve.wait_ge(head_rms.sem, head_rms.due(dve))
                dve.scalar_tensor_tensor(flat(x), flat(x), col(gain), flat(RS), ALU.mult, ALU.mult)\
                   .then_inc(head_normed.sem, 1)
                dve.wait_ge(head_normed.sem, head_normed.due(dve))
                for k in range(0, DK, 2):
                    bank, full, free = vbanks.empty()
                    dve.wait_ge(full.sem, full.due(dve))
                    dve.tensor_tensor(ROT[:, k:k + 2, :], bank.rearrange("p (a b) -> p a b", a=2),
                        over(const("att_sin"), 2, T), ALU.mult)\
                       .then_inc(free.sem, 1)
                    dve.wait_ge(free.sem, free.due(dve))
                dve.tensor_tensor(x, x, over(const("att_cos"), DK, T), ALU.mult)\
                   .then_inc(vector_step.sem, 1)
                dve.wait_ge(vector_step.sem, vector_step.due(dve))
                dve.tensor_tensor(x, x, ROT, ALU.add)\
                   .then_inc(vector_step.sem, 1)
                dve.wait_ge(vector_step.sem, vector_step.due(dve))
            kp = KP.rearrange("p (k e) t -> p k e t", e=2)
            for e in range(2):
                sig = keys_ready if e else vector_step
                dve.tensor_scalar(kp[:, :, e, :], K, half[:, e:e + 1], None, ALU.mult)\
                   .then_inc(sig.sem, 1)
                dve.wait_ge(sig.sem, sig.due(dve))

            def take(h, bank, free):
                at = slice(64 * (h % 2), 64 * (h % 2) + 64)
                dve.tensor_copy(O[at, h // 2, :], bank[at])\
                   .then_inc(free.sem, 1)
                dve.wait_ge(free.sem, free.due(dve))

            attend_v(16, 64 ** -0.5, const("windows"), SC, PR, MX, SM, take)
            dve.nop().then_inc(heads_out.sem, 1)
            evict(dve, att_out, add_to_x)

        def reduce_angle_v(src, dst, k, tmp):
            magic = float(3 << 22)
            dve.tensor_scalar(k, src, 0.15915494309189535, magic, ALU.mult, ALU.add)\
               .then_inc(vector_step.sem, 1)
            dve.wait_ge(vector_step.sem, vector_step.due(dve))
            dve.tensor_scalar(k, k, magic, None, ALU.subtract)\
               .then_inc(vector_step.sem, 1)
            dve.wait_ge(vector_step.sem, vector_step.due(dve))
            dve.scalar_tensor_tensor(dst, k, -6.28125, src, ALU.mult, ALU.add)\
               .then_inc(vector_step.sem, 1)
            dve.wait_ge(vector_step.sem, vector_step.due(dve))
            dve.scalar_tensor_tensor(dst, k, -0.0019350051879882812, dst, ALU.mult, ALU.add)\
               .then_inc(vector_step.sem, 1)
            dve.wait_ge(vector_step.sem, vector_step.due(dve))
            dve.scalar_tensor_tensor(dst, k, -3.0199159819e-07, dst, ALU.mult, ALU.add)\
               .then_inc(vector_step.sem, 1)
            dve.wait_ge(vector_step.sem, vector_step.due(dve))
            dve.tensor_scalar(dst, dst, 3.1415925, -3.1415925, ALU.min, ALU.max)\
               .then_inc(vector_step.sem, 1)
            dve.wait_ge(vector_step.sem, vector_step.due(dve))

        def angles_v():
            dve.wait_ge(positions_landed.sem, positions_landed.due(dve, 16))
            dve.tensor_copy(ANG[:, 0, :], ANG[:, 3, :].bitcast(I32))\
               .then_inc(vector_step.sem, 1)
            dve.wait_ge(vector_step.sem, vector_step.due(dve))
            dve.tensor_scalar(ANG[:, 0, :], ANG[:, 0, :], const("mla_freq"), None, ALU.mult)\
               .then_inc(vector_step.sem, 1)
            dve.wait_ge(vector_step.sem, vector_step.due(dve))
            reduce_angle_v(ANG[:, 0, :], ANG[:, 1, :], ANG[:, 2, :], None)
            dve.tensor_scalar(ANG[:, 2, :], ANG[:, 1, :], 1.5707963267948966, None, ALU.add)\
               .then_inc(vector_step.sem, 1)
            dve.wait_ge(vector_step.sem, vector_step.due(dve))
            dve.tensor_scalar(ANG[:, 3, :], ANG[:, 2, :], 3.1415927, -6.283185307179586, ALU.is_gt,
                ALU.mult)\
               .then_inc(vector_step.sem, 1)
            dve.wait_ge(vector_step.sem, vector_step.due(dve))
            dve.tensor_tensor(ANG[:, 2, :], ANG[:, 2, :], ANG[:, 3, :], ALU.add)\
               .then_inc(vector_step.sem, 1)
            dve.wait_ge(vector_step.sem, vector_step.due(dve))
            dve.tensor_scalar(ANG[:, 2, :], ANG[:, 2, :], 3.1415925, -3.1415925, ALU.min, ALU.max)\
               .then_inc(angles_ready.sem, 1)
            dve.wait_ge(angles_ready.sem, angles_ready.due(dve))
            dve.wait_ge(tables_ready.sem, tables_ready.due(dve))

        def merge_v(job, tmp, base):
            def body(i, s, rounds, turn):
                dve.wait_ge(product[s].sem, rounds + 1)
                dve.tensor_tensor(tmp[s], psum[s].rearrange("p (a b) -> p a b", a=2), two(GT, i), ALU.mult)\
                   .then_inc(evicted[s].sem, 1)
                dve.wait_ge(evicted[s].sem, rounds + 1)
                dve.tensor_tensor(two(M, i), two(M, i), tmp[s], ALU.add).then_inc(merged.sem, 1)
                dve.wait_ge(merged.sem, turn * 2 + (base + s + 1))

            job.each(dve, body)

        def mla_v(j, l):
            n2 = lambda n: f"{n}_2/{l}"
            dve.wait_ge(evicted[0].sem, halves(0, j["cq"]))
            dve.wait_ge(evicted[1].sem, halves(1, j["cq"]))
            norm_v(CQ, SQM[:, 0:4, :], 4, lambda k: col(n2("mla_q_norm"), k), CQ)
            dve.wait_ge(evicted[0].sem, halves(0, j["kr"]))
            dve.wait_ge(evicted[1].sem, halves(1, j["kr"]))
            norm_v(CKV, SQM[:, 0:2, :], 2, lambda k: col(n2("mla_kv_norm"), k), CKV)
            dve.wait_ge(evicted[0].sem, halves(0, j["uqr"]))
            dve.wait_ge(evicted[1].sem, halves(1, j["uqr"]))
            dve.wait_ge(evicted[0].sem, halves(0, j["ukv"]))
            dve.wait_ge(evicted[1].sem, halves(1, j["ukv"]))
            for x, nt in ((QR, 4), (KR, 1)):
                for k in range(0, nt, 2):
                    bank, full, free = vbanks.empty()
                    dve.wait_ge(full.sem, full.due(dve))
                    n = min(2, nt - k)
                    dve.tensor_tensor(ROTM[:, k:k + n, :], bank[:,
                        0:n * T].rearrange("p (a b) -> p a b", a=n), over(SIN, n, T), ALU.mult)\
                       .then_inc(free.sem, 1)
                    dve.wait_ge(free.sem, free.due(dve))
                dve.tensor_tensor(x, x, over(COS, nt, T), ALU.mult)\
                   .then_inc(vector_step.sem, 1)
                dve.wait_ge(vector_step.sem, vector_step.due(dve))
                dve.tensor_tensor(x, x, ROTM[:, 0:nt, :], ALU.add)\
                   .then_inc(vector_step.sem, 1)
                dve.wait_ge(vector_step.sem, vector_step.due(dve))
            for e in range(2):
                sig = keys_ready if e else vector_step
                dve.tensor_scalar(KRP[:, e, :], KR[:, 0, :], half[:, e:e + 1], None, ALU.mult)\
                   .then_inc(sig.sem, 1)
                dve.wait_ge(sig.sem, sig.due(dve))
            dve.wait_ge(evicted[0].sem, halves(0, j["mz"]))
            dve.wait_ge(evicted[1].sem, halves(1, j["mz"]))

            def take(h, bank, free):
                dve.tensor_tensor(OM[:, h, :], bank, ZM[:, h, :], ALU.mult)\
                   .then_inc(free.sem, 1)
                dve.wait_ge(free.sem, free.due(dve))

            attend_v(8, 192 ** -0.5, const("chunks"), MSC, MPR, MMX, MSM, take)
            dve.nop().then_inc(heads_out.sem, 1)
            dve.wait_ge(evicted[0].sem, halves(0, j["ga"]))
            dve.wait_ge(evicted[1].sem, halves(1, j["ga"]))
            evict(dve, j["mo"], lambda i, bank, done, rounds:
                  dve.tensor_tensor(two(M, i), bank, two(GT, i), ALU.mult).then_inc(done, 1))

        def mix_v(src, dst, nt, mu, l):
            dve.tensor_tensor(dst, src[:, :, 0:T], src[:, :, 1:T + 1], ALU.subtract)\
               .then_inc(vector_step.sem, 1)
            dve.wait_ge(vector_step.sem, vector_step.due(dve))
            for k in range(nt):
                dve.scalar_tensor_tensor(dst[:, k, :], dst[:, k, :], col(f"rwkv_mu_2/{l}", mu + k),
                    src[:, k, 1:T + 1], ALU.mult, ALU.add)\
                   .then_inc(vector_step.sem, 1)
                dve.wait_ge(vector_step.sem, vector_step.due(dve))

        KAPPA = float(np.exp(np.float64(-0.5)))

        def rwkv_v(j, l):
            n2 = lambda n: f"{n}_2/{l}"
            dve.wait_ge(evicted[0].sem, halves(0, j["gl"]))
            dve.wait_ge(evicted[1].sem, halves(1, j["gl"]))
            dve.wait_ge(evicted[0].sem, halves(0, j["mo"]))
            dve.wait_ge(evicted[1].sem, halves(1, j["mo"]))
            for x in raw:
                sig = fronts_zeroed if x is raw[2] else vector_step
                dve.memset(x[:, :, 0:1], 0.0)\
                   .then_inc(sig.sem, 1)
                dve.wait_ge(sig.sem, sig.due(dve))
            dve.memset(flat(W2), 0.0)\
               .then_inc(lora_zeroed.sem, 1)
            dve.wait_ge(lora_zeroed.sem, lora_zeroed.due(dve))
            wl = WL.rearrange("p (a b) -> p a b", a=1)
            sq1 = SQR[:, 0:1, :]
            dve.tensor_tensor(sq1, wl[:, :, 0:T], wl[:, :, 1:T + 1], ALU.subtract)\
               .then_inc(vector_step.sem, 1)
            dve.wait_ge(vector_step.sem, vector_step.due(dve))
            dve.scalar_tensor_tensor(sq1[:, 0, :], sq1[:, 0, :], col(n2("rwkv_mu"), 24), WL[:, 1:T + 1],
                ALU.mult, ALU.add)\
               .then_inc(vector_step.sem, 1)
            dve.wait_ge(vector_step.sem, vector_step.due(dve))
            dve.tensor_copy(WL[:, 1:T + 1], sq1[:, 0, :])\
               .then_inc(lora_mixed.sem, 1)
            dve.wait_ge(lora_mixed.sem, lora_mixed.due(dve))
            for x, dst, n, job in ((raw[0], R, 0, "r"), (raw[1], KR_, 1, "k"), (raw[2], V_, 2, "v")):
                dve.wait_ge(evicted[0].sem, halves(0, j[job]))
                dve.wait_ge(evicted[1].sem, halves(1, j[job]))
                mix_v(x, dst, DK, 8 * n, l)
            dve.wait_ge(lora_gates.sem, lora_gates.due(dve))
            for k in range(DK):
                dve.tensor_tensor_scan(CC[:, k, :], const("run"), SW[:, k, :], 0.0, ALU.mult, ALU.add)\
                   .then_inc(vector_step.sem, 1)
                dve.wait_ge(vector_step.sem, vector_step.due(dve))
            dve.tensor_tensor(SW, CC, SW, ALU.subtract)\
               .then_inc(cumulated.sem, 1)
            dve.wait_ge(cumulated.sem, cumulated.due(dve))
            dve.tensor_tensor(KKD, KR_, along(col(n2("rwkv_k_k"), 0, 8), DK, T), ALU.mult)\
               .then_inc(vector_step.sem, 1)
            dve.wait_ge(vector_step.sem, vector_step.due(dve))
            dve.tensor_tensor(SQR, KKD, KKD, ALU.mult)\
               .then_inc(head_squares.sem, 1)
            dve.wait_ge(head_squares.sem, head_squares.due(dve))
            dve.tensor_scalar(KAI, col(n2("rwkv_k_a"), 0, 8), -1.0, 1.0, ALU.mult, ALU.add)\
               .then_inc(vector_step.sem, 1)
            dve.wait_ge(vector_step.sem, vector_step.due(dve))
            for k in range(DK):
                dve.tensor_scalar(BDF[:, k, :], AA[:, k, :], col(n2("rwkv_k_a"), k), KAI[:, k:k + 1],
                    ALU.mult, ALU.add)\
                   .then_inc(vector_step.sem, 1)
                dve.wait_ge(vector_step.sem, vector_step.due(dve))
            dve.tensor_tensor(KR_, KR_, BDF, ALU.mult)\
               .then_inc(vector_step.sem, 1)
            dve.wait_ge(vector_step.sem, vector_step.due(dve))
            dve.wait_ge(head_rms.sem, head_rms.due(dve))
            dve.tensor_scalar(SQR, SQR, 1e-12, None, ALU.max)\
               .then_inc(vector_step.sem, 1)
            dve.wait_ge(vector_step.sem, vector_step.due(dve))
            dve.reciprocal(SQR, SQR)\
               .then_inc(vector_step.sem, 1)
            dve.wait_ge(vector_step.sem, vector_step.due(dve))
            dve.tensor_tensor(KKD, KKD, SQR, ALU.mult)\
               .then_inc(vector_step.sem, 1)
            dve.wait_ge(vector_step.sem, vector_step.due(dve))
            dve.tensor_tensor(BDF, KKD, AA, ALU.mult)\
               .then_inc(vector_step.sem, 1)
            dve.wait_ge(vector_step.sem, vector_step.due(dve))
            dve.tensor_tensor(SQR, R, KR_, ALU.mult)\
               .then_inc(vector_step.sem, 1)
            dve.wait_ge(vector_step.sem, vector_step.due(dve))
            dve.tensor_tensor(SQR, SQR, along(col(n2("rwkv_r_k"), 0, 8), DK, T), ALU.mult)\
               .then_inc(head_squares.sem, 1)
            dve.wait_ge(head_squares.sem, head_squares.due(dve))
            for k in range(0, DK, 2):
                bank, full, free = vbanks.empty()
                dve.wait_ge(full.sem, full.due(dve))
                dve.tensor_tensor(BONUS[:, k:k + 2, :], bank.rearrange("p (a b) -> p a b", a=2), V_[:,
                    k:k + 2, :], ALU.mult)\
                   .then_inc(free.sem, 1)
                dve.wait_ge(free.sem, free.due(dve))
            dve.wait_ge(decays.sem, decays.due(dve))
            dve.tensor_tensor(R, R, E1, ALU.mult)\
               .then_inc(vector_step.sem, 1)
            dve.wait_ge(vector_step.sem, vector_step.due(dve))
            dve.tensor_tensor(KKD, KKD, SW, ALU.mult)\
               .then_inc(vector_step.sem, 1)
            dve.wait_ge(vector_step.sem, vector_step.due(dve))
            dve.tensor_tensor(BDF, BDF, E2, ALU.mult)\
               .then_inc(vector_step.sem, 1)
            dve.wait_ge(vector_step.sem, vector_step.due(dve))
            dve.tensor_tensor(KR_, KR_, E2, ALU.mult)\
               .then_inc(vector_step.sem, 1)
            dve.wait_ge(vector_step.sem, vector_step.due(dve))
            dve.tensor_copy(ECEND, E1.rearrange("p k (c t) -> p k c t", t=CH)[:, :, :, CH - 1])\
               .then_inc(vector_step.sem, 1)
            dve.wait_ge(vector_step.sem, vector_step.due(dve))
            dve.memset(flat(ST[0]), 0.0)\
               .then_inc(vector_step.sem, 1)
            dve.wait_ge(vector_step.sem, vector_step.due(dve))
            for t in range(TT):
                here = slice(t * P, t * P + P)
                pad = PAD.rearrange("p (k e) t -> p k e t", e=4)
                for n, x in ((0, KKD), (2, R)):
                    for e in range(2):
                        sig = tile_operands if (n, e) == (2, 1) else vector_step
                        dve.tensor_scalar(pad[:, :, n + e, :], x[:, :, here], half[:, e:e + 1], None,
                            ALU.mult)\
                           .then_inc(sig.sem, 1)
                        dve.wait_ge(sig.sem, sig.due(dve))
                dve.tensor_copy(XT, over(ident, 16, P))\
                   .then_inc(vector_step.sem, 1)
                dve.wait_ge(vector_step.sem, vector_step.due(dve))
                for h in range(0, 16, 4):
                    bank, full, free = vbanks.empty()
                    dve.wait_ge(full.sem, full.due(dve))
                    dve.tensor_tensor(AN[:, h:h + 4, :], bank.rearrange("p (a b) -> p a b", a=4),
                        over(const("neg_strict"), 4, P), ALU.mult)\
                       .then_inc(free.sem, 1)
                    dve.wait_ge(free.sem, free.due(dve))
                dve.nop().then_inc(a_ready.sem, 1)
                for h in range(0, 16, 4):
                    bank, full, free = vbanks.empty()
                    dve.wait_ge(full.sem, full.due(dve))
                    dve.tensor_tensor(BT[:, h:h + 4, :], bank.rearrange("p (a b) -> p a b", a=4),
                        over(const("before"), 4, P), ALU.mult)\
                       .then_inc(free.sem, 1)
                    dve.wait_ge(free.sem, free.due(dve))
                for level in range(6):
                    mask = over(const(f"level{level}"), 4, P).bitcast(I32)
                    for h in range(0, 16, 4):
                        bank, full, free = vbanks.empty()
                        dve.wait_ge(full.sem, full.due(dve))
                        dve.copy_predicated(XT[:, h:h + 4, :], mask, bank.rearrange("p (a b) -> p a b",
                            a=4))\
                           .then_inc(free.sem, 1)
                        dve.wait_ge(free.sem, free.due(dve))
                        dve.nop().then_inc(inverse_ready.sem, 1)
                for h in range(0, 2):
                    bank, full, free = vbanks.empty()
                    dve.wait_ge(full.sem, full.due(dve))
                    dve.tensor_copy(BVT[:, h * 512:h * 512 + 512], bank)\
                       .then_inc(free.sem, 1)
                    dve.wait_ge(free.sem, free.due(dve))
                dve.nop().then_inc(bv_ready.sem, 1)
                for h in range(0, 4):
                    bank, full, free = vbanks.empty()
                    dve.wait_ge(full.sem, full.due(dve))
                    halves_v(WT[:, 2 * h:2 * h + 2, :], bank, free)
                for h in range(0, 2):
                    bank, full, free = vbanks.empty()
                    dve.wait_ge(full.sem, full.due(dve))
                    dve.tensor_copy(ZT[:, h * 512:h * 512 + 512], bank)\
                       .then_inc(free.sem, 1)
                    dve.wait_ge(free.sem, free.due(dve))
                for x in (XX, QQ):
                    for h in range(0, 16, 4):
                        bank, full, free = vbanks.empty()
                        dve.wait_ge(full.sem, full.due(dve))
                        dve.tensor_tensor(x[:, h:h + 4, :], bank.rearrange("p (a b) -> p a b", a=4),
                            over(const("upto"), 4, P), ALU.mult)\
                           .then_inc(free.sem, 1)
                        dve.wait_ge(free.sem, free.due(dve))
                dve.nop().then_inc(w_ready.sem, 1)
                for c in range(2):
                    dve.nop().then_inc(state_ready.sem, 1)
                    rows = slice(0, P) if c == 0 else slice(CH, P)
                    for k in range(2):
                        bank, full, free = vbanks.empty()
                        dve.wait_ge(full.sem, full.due(dve))
                        at = slice(k * 512, k * 512 + 512)
                        dve.scalar_tensor_tensor(UT[rows, at], bank[rows], -1.0, ZT[rows, at], ALU.mult,
                            ALU.subtract)\
                           .then_inc(free.sem, 1)
                        dve.wait_ge(free.sem, free.due(dve))
                    dve.nop().then_inc(u_ready.sem, 1)
                    if c == 1:
                        for k in range(0, DK, 2):
                            bank, full, free = vbanks.empty()
                            dve.wait_ge(full.sem, full.due(dve))
                            halves_v(R[:, k:k + 2, here], bank, free)
                    if (t, c) != (TT - 1, 1):
                        g = 2 * t + c
                        for k in range(0, DK, 4):
                            bank, full, free = vbanks.empty()
                            dve.wait_ge(full.sem, full.due(dve))
                            new = ST[1 - c][:, k:k + 4, :]
                            dve.tensor_tensor(new, bank.rearrange("p (a b) -> p a b", a=4), over(ones64,
                                4, P), ALU.mult)\
                               .then_inc(free.sem, 1)
                            dve.wait_ge(free.sem, free.due(dve))
                            dve.tensor_tensor(new, new, ST[c][:, k:k + 4, :], ALU.add)\
                               .then_inc(vector_step.sem, 1)
                            dve.wait_ge(vector_step.sem, vector_step.due(dve))
                            dve.tensor_tensor(new, new, ECEND[:, k:k + 4, g:g + 1].to_broadcast([P, 4,
                                P]), ALU.mult)\
                               .then_inc(vector_step.sem, 1)
                            dve.wait_ge(vector_step.sem, vector_step.due(dve))
            dve.nop().then_inc(head_squares.sem, 1)
            dve.wait_ge(head_squares.sem, head_squares.due(dve))
            for k in range(0, DK, 2):
                bank, full, free = vbanks.empty()
                dve.wait_ge(full.sem, full.due(dve))
                dve.scalar_tensor_tensor(flat(R[:, k:k + 2, :]), bank, -1.0 / 64, flat(R[:, k:k + 2,
                    :]), ALU.mult, ALU.add)\
                   .then_inc(free.sem, 1)
                dve.wait_ge(free.sem, free.due(dve))
            dve.tensor_tensor(SQT, R, R, ALU.mult)\
               .then_inc(head_squares.sem, 1)
            dve.wait_ge(head_squares.sem, head_squares.due(dve))
            dve.wait_ge(head_rms.sem, head_rms.due(dve))
            dve.tensor_tensor(R, R, RST, ALU.mult)\
               .then_inc(vector_step.sem, 1)
            dve.wait_ge(vector_step.sem, vector_step.due(dve))
            for k in range(DK):
                dve.tensor_scalar(R[:, k, :], R[:, k, :], col(n2("rwkv_ln_w"), k), col(n2("rwkv_ln_b"),
                    k), ALU.mult, ALU.add)\
                   .then_inc(vector_step.sem, 1)
                dve.wait_ge(vector_step.sem, vector_step.due(dve))
            dve.tensor_tensor(R, R, BONUS, ALU.add)\
               .then_inc(vector_step.sem, 1)
            dve.wait_ge(vector_step.sem, vector_step.due(dve))
            dve.wait_ge(evicted[0].sem, halves(0, j["rz"]))
            dve.wait_ge(evicted[1].sem, halves(1, j["rz"]))
            dve.tensor_tensor(R, R, ZR, ALU.mult)\
               .then_inc(branch_ready.sem, 1)
            dve.wait_ge(branch_ready.sem, branch_ready.due(dve))
            dve.wait_ge(evicted[0].sem, halves(0, j["gb"]))
            dve.wait_ge(evicted[1].sem, halves(1, j["gb"]))
            merge_v(j["ro"], TMP, 8 * l)
            dve.nop().then_inc(merged_rwkv.sem, 1)

        def gla_v(j, l):
            n2 = lambda n: f"{n}_2/{l}"
            dve.wait_ge(evicted[0].sem, halves(0, j["gl"]))
            dve.wait_ge(evicted[1].sem, halves(1, j["gl"]))
            for h in range(0, 4, 2):
                bank, full, free = vbanks.empty()
                dve.wait_ge(full.sem, full.due(dve))
                dve.tensor_tensor(GX[:, h:h + 2, :], bank.rearrange("p (a b) -> p a b", a=2),
                    along(col(n2("gla_b"), h, 2), 2, T), ALU.add)\
                   .then_inc(free.sem, 1)
                dve.wait_ge(free.sem, free.due(dve))
            dve.scalar_tensor_tensor(flat(GE), flat(GX), -1.0, flat(GX), ALU.mult, ALU.min)\
               .then_inc(gate_in.sem, 1)
            dve.wait_ge(gate_in.sem, gate_in.due(dve))
            dve.wait_ge(gate_out.sem, gate_out.due(dve))
            dve.scalar_tensor_tensor(GX, GX, 0.0, GE, ALU.min, ALU.subtract)\
               .then_inc(vector_step.sem, 1)
            dve.wait_ge(vector_step.sem, vector_step.due(dve))
            for h in range(4):
                dve.tensor_tensor_scan(GC[:, h, :], const("run"), GX[:, h, :], 0.0, ALU.mult, ALU.add)\
                   .then_inc(vector_step.sem, 1)
                dve.wait_ge(vector_step.sem, vector_step.due(dve))
            c4 = flat(GC).rearrange("p (c t) -> p c t", t=CH)
            dve.tensor_tensor(flat(GD).rearrange("p (c t) -> p c t", t=CH), c4[:, :,
                CH - 1:CH].to_broadcast([P, 16, CH]), c4, ALU.subtract)\
               .then_inc(gla_sums.sem, 1)
            dve.wait_ge(gla_sums.sem, gla_sums.due(dve))
            dve.wait_ge(gla_exps.sem, gla_exps.due(dve))
            dve.wait_ge(evicted[0].sem, halves(0, j["gk"]))
            dve.wait_ge(evicted[1].sem, halves(1, j["gk"]))
            dve.scalar_tensor_tensor(GX, GQ, 128 ** -0.5, GE, ALU.mult, ALU.mult)\
               .then_inc(vector_step.sem, 1)
            dve.wait_ge(vector_step.sem, vector_step.due(dve))
            dve.tensor_tensor(KINV, GK, GY, ALU.mult)\
               .then_inc(vector_step.sem, 1)
            dve.wait_ge(vector_step.sem, vector_step.due(dve))
            dve.tensor_tensor(KTE, GK, GD, ALU.mult)\
               .then_inc(gla_operands.sem, 1)
            dve.wait_ge(gla_operands.sem, gla_operands.due(dve))
            dve.wait_ge(evicted[0].sem, halves(0, j["gv"]))
            dve.wait_ge(evicted[1].sem, halves(1, j["gv"]))
            for t in range(TT):
                here = slice(t * P, t * P + P)
                bank, full, free = vbanks.empty()
                dve.wait_ge(full.sem, full.due(dve))
                dve.tensor_tensor(AT, bank.rearrange("p (a b) -> p a b", a=4), over(const("upto"), 4,
                    P), ALU.mult)\
                   .then_inc(free.sem, 1)
                dve.wait_ge(free.sem, free.due(dve))
                for c in range(2):
                    g = 2 * t + c
                    if g == 3:
                        continue
                    for h in range(0, 4, 2):
                        bank, full, free = vbanks.empty()
                        dve.wait_ge(full.sem, full.due(dve))
                        for n in range(2):
                            b = bank[:, n * T:n * T + T]
                            if g == 0:
                                sig = free if n else vector_step
                                dve.tensor_copy(GS[1][:, h + n, :], b)\
                                   .then_inc(sig.sem, 1)
                                dve.wait_ge(sig.sem, sig.due(dve))
                            else:
                                sig = free if n else vector_step
                                dve.scalar_tensor_tensor(GS[g + 1][:, h + n, :], GS[g][:, h + n, :],
                                    EL[:, (h + n) * 4 + g:(h + n) * 4 + g + 1], b, ALU.mult, ALU.add)\
                                   .then_inc(sig.sem, 1)
                                dve.wait_ge(sig.sem, sig.due(dve))
                dve.nop().then_inc(gla_states.sem, 1)
                for h in range(0, 4, 2):
                    bank, full, free = vbanks.empty()
                    dve.wait_ge(full.sem, full.due(dve))
                    dve.tensor_copy(OG[:, 2 * h:2 * h + 4, here], bank.rearrange("p (a b) -> p a b", a=4))\
                       .then_inc(free.sem, 1)
                    dve.wait_ge(free.sem, free.due(dve))
            norm_v(OG, SQG, 2, lambda k: col(n2("gla_norm"), k % 2), OG, 4)
            dve.wait_ge(evicted[0].sem, halves(0, j["gz"]))
            dve.wait_ge(evicted[1].sem, halves(1, j["gz"]))
            dve.tensor_tensor(OG, OG, GZ, ALU.mult)\
               .then_inc(branch_ready.sem, 1)
            dve.wait_ge(branch_ready.sem, branch_ready.due(dve))
            dve.wait_ge(evicted[0].sem, halves(0, j["gc"]))
            dve.wait_ge(evicted[1].sem, halves(1, j["gc"]))
            merge_v(j["go"], TMPG, 8 * l + 4)

        @block.vector
        def _(_v):
            for _, _, free in vbanks.banks:
                dve.nop().then_inc(free.sem, 1)
                free.due(dve)
            take_in_v()
            rec_v()
            ffn_v(0)
            attention_v()
            ffn_v(1)
            dve.wait_ge(evicted[0].sem, halves(0, ffn_down[1]))
            dve.wait_ge(evicted[1].sem, halves(1, ffn_down[1]))
            dve.memset(WL[:, 0:1], 0.0)\
               .then_inc(vector_step.sem, 1)
            dve.wait_ge(vector_step.sem, vector_step.due(dve))
            dve.nop().then_inc(second_begins.sem, 1)
            angles_v()
            for l in range(2):
                j = second[l]
                n2 = lambda n: f"{n}_2/{l}"
                dve.wait_ge(evicted[0].sem, halves(0, j["ada"]))
                dve.wait_ge(evicted[1].sem, halves(1, j["ada"]))
                dve.tensor_tensor(MOD, MOD, col(n2("ada_b"), 0, 24), ALU.add)\
                   .then_inc(vector_step.sem, 1)
                dve.wait_ge(vector_step.sem, vector_step.due(dve))
                dve.scalar_tensor_tensor(GPRE, MOD[:, 8:16], 1.0, col(n2("norm_pre"), 0, 8), ALU.add,
                    ALU.mult)\
                   .then_inc(vector_step.sem, 1)
                dve.wait_ge(vector_step.sem, vector_step.due(dve))
                dve.tensor_tensor(GPOST, MOD[:, 16:24], col(n2("norm_post"), 0, 8), ALU.mult)\
                   .then_inc(vector_step.sem, 1)
                dve.wait_ge(vector_step.sem, vector_step.due(dve))
                norm_v(X, SQM, DK, lambda k: GPRE[:, k:k + 1], H, shift=lambda k: MOD[:, k:k + 1])
                mla_v(j, l)
                rwkv_v(j, l)
                gla_v(j, l)
                dve.nop().then_inc(merge_ready.sem, 1)
                dve.wait_ge(evicted[0].sem, halves(0, j["out"]))
                dve.wait_ge(evicted[1].sem, halves(1, j["out"]))
                norm_v(QN, SQM, DK, lambda k: GPOST[:, k:k + 1], QN)
                sig = x_ready if l else x_added
                dve.tensor_tensor(X, X, QN, ALU.add)\
                   .then_inc(sig.sem, 1)
                dve.wait_ge(sig.sem, sig.due(dve))
            for k in range(4):
                bank, full, free = vbanks.empty()
                dve.wait_ge(full.sem, full.due(dve))
                dve.tensor_copy(flat(XIN)[:, k * 512:k * 512 + 512], bank)\
                   .then_inc(free.sem, 1)
                dve.wait_ge(free.sem, free.due(dve))
            dve.nop().then_inc(output_ready.sem, 1)

        def take_in_act():
            act.dma_start(cst, A["const"]).then_inc(inputs_landed.sem, 16)
            act.dma_start(XIN, A["x"][0].rearrange("(t p) d -> p t d", p=P)).then_inc(inputs_landed.sem, 16)
            act.wait_ge(packs_zeroed.sem, packs_zeroed.due(act))
            for name, (pack, row, n) in VEC_AT.items():
                key, _, l = name.partition("/")
                src = A[key]
                if l:
                    src = src[int(l)]
                elif key not in ("ffn_norm", "c_2"):
                    src = src[0]
                flat_src = src if len(src.shape) == 1 else src.rearrange(" ".join("abc"[:len(src.shape)]) + " -> (" + " ".join("abc"[:len(src.shape)]) + ")")
                if flat_src.shape[0] == 64:
                    for e in range(2):
                        act.dma_start(PACK[row:row + 1, pack, 64 * e:64 * e + 64], flat_src.rearrange("(a b) -> a b", a=1)).then_inc(inputs_landed.sem, 16)
                else:
                    act.dma_start(PACK[row:row + n, pack, :], flat_src.rearrange("(a b) -> a b", b=P)).then_inc(inputs_landed.sem, 16)
            for n, name in enumerate(("ssd_dt_bias", "ssd_a_log", "ssd_d")):
                act.dma_start(AROW[:, n, :], A[name][0].partition_broadcast(P)).then_inc(rows_landed.sem, 16)
            act.wait_ge(lru_weights_zeroed.sem, lru_weights_zeroed.due(act))
            for n, name in enumerate(("lru_w_r", "lru_w_i")):
                w = A[name][0].rearrange("(k e) i j -> e i k j", e=2)
                for e in range(2):
                    act.dma_start(BD[64 * e:64 * e + 64, n, :, 64 * e:64 * e + 64], w[e]).then_inc(lru_weights_landed.sem, 16)

        def rec_act():
            act.wait_ge(biases_set.sem, biases_set.due(act))
            rms_act(D)
            softplus_act(LAMA)
            act.wait_ge(rows_landed.sem, rows_landed.due(act, 48))
            act.activation(AROW[:, 1, :], AROW[:, 1, :], ACT.Exp)\
               .then_inc(a_exp.sem, 1)
            act.wait_ge(a_exp.sem, a_exp.due(act))
            evict(act, rec_dt, lambda i, bank, done, rounds:
                  act.activation(DT[:, :, 8 * i:8 * i + 8], bank[:, :, 0:8], ACT.Copy).then_inc(done, 1))
            softplus_act(flat(DTB))
            act.wait_ge(conv_fronts_zeroed.sem, conv_fronts_zeroed.due(act))
            evict(act, rec_x, keep(LX, ACT.Copy, 3))
            evict(act, rec_gate, keep(G, ACT.Gelu_apprx_tanh))
            evict(act, rec_xbc, keep(XB, ACT.Copy, 3))
            evict(act, rec_z, keep(Z, ACT.Silu))
            act.wait_ge(ssd_conv_done.sem, ssd_conv_done.due(act))
            act.activation(flat(XBC), flat(XBC), ACT.Silu)\
               .then_inc(xbc_ready.sem, 1)
            act.wait_ge(xbc_ready.sem, xbc_ready.due(act))
            for k in range(DK):
                bank, full, free = abanks.empty()
                act.wait_ge(full.sem, full.due(act))
                act.activation(RG[:, k, :], bank[:, 0:T], ACT.Sigmoid, bias=col("lru_b_r", k))\
                   .then_inc(scalar_step.sem, 1)
                act.wait_ge(scalar_step.sem, scalar_step.due(act))
                act.activation(IG[:, k, :], bank[:, T:], ACT.Sigmoid, bias=col("lru_b_i", k))\
                   .then_inc(free.sem, 1)
                act.wait_ge(free.sem, free.due(act))
            act.nop().then_inc(lru_gates.sem, 1)
            act.wait_ge(rate_ready.sem, rate_ready.due(act))
            act.activation(flat(H), flat(RG), ACT.Exp, scale=-1.0)\
               .then_inc(scalar_step.sem, 1)
            act.wait_ge(scalar_step.sem, scalar_step.due(act))
            act.activation(flat(RG), flat(RG), ACT.Tanh)\
               .then_inc(lru_functions.sem, 1)
            act.wait_ge(lru_functions.sem, lru_functions.due(act))
            act.wait_ge(lru_root_in.sem, lru_root_in.due(act))
            act.activation(flat(UU), flat(UU), ACT.Sqrt)\
               .then_inc(lru_root.sem, 1)
            act.wait_ge(lru_root.sem, lru_root.due(act))
            for t in range(TT):
                act.wait_ge(decay_in.sem, decay_in.due(act))
                act.activation(flat(SEG), flat(SEG), ACT.Exp)\
                   .then_inc(scalar_step.sem, 1)
                act.wait_ge(scalar_step.sem, scalar_step.due(act))
                if t == 0:
                    act.activation(LAST, LAST, ACT.Exp)\
                       .then_inc(decay_out.sem, 1)
                    act.wait_ge(decay_out.sem, decay_out.due(act))
                else:
                    act.activation(flat(ECS), flat(ECS), ACT.Exp)\
                       .then_inc(decay_out.sem, 1)
                    act.wait_ge(decay_out.sem, decay_out.due(act))
            rms_act(512, 2)

        def att_act():
            rms_act(D)
            evict(act, att_q, keep(Q, ACT.Copy))
            evict(act, att_k, keep(K, ACT.Copy))
            evict(act, att_v, keep_tokens(VT))
            for _ in range(2):
                for k in range(0, DK, 2):
                    bank, full, free = abanks.empty()
                    act.wait_ge(full.sem, full.due(act))
                    act.activation(flat(RS[:, k:k + 2, :]), bank, ACT.Ln, bias=biases[:, 0:1],
                        scale=1.0 / 64)\
                       .then_inc(free.sem, 1)
                    act.wait_ge(free.sem, free.due(act))
                act.activation(flat(RS), flat(RS), ACT.Exp, scale=-0.5)\
                   .then_inc(head_rms.sem, 1)
                act.wait_ge(head_rms.sem, head_rms.due(act))
                act.wait_ge(head_normed.sem, head_normed.due(act))
            attend_act(16, SC, PR, PT, MX, SM)

        def keep_one(dst):
            return lambda i, bank, done, rounds: act.activation(dst, bank[0:dst.shape[0], 0, :], ACT.Copy).then_inc(done, 1)

        def mla_act(j, l):
            evict(act, j["cq"], keep(CQ, ACT.Copy))
            evict(act, j["ckv"], keep(CKV, ACT.Copy))
            evict(act, j["kr"], keep_one(KR[:, 0, :]))
            evict(act, j["wl"], keep_one(WL[:, 1:]))
            evict(act, j["gl"], keep_one(GL[0:16, :]))
            evict(act, j["mz"], keep(ZM, ACT.Silu))
            evict(act, j["ga"], keep(GT, ACT.Sigmoid))
            rms_act(512)
            evict(act, j["uqn"], keep(QN, ACT.Copy))
            evict(act, j["uqr"], keep(QR, ACT.Copy))
            rms_act(256)
            evict(act, j["ukn"], keep(KN, ACT.Copy))
            evict(act, j["ukv"], keep_tokens(VM))
            attend_act(8, MSC, MPR, MPT, MMX, MSM)

        def rwkv_act(j, l):
            n2 = lambda n: f"{n}_2/{l}"
            act.wait_ge(lora_zeroed.sem, lora_zeroed.due(act))
            act.dma_start(flat(W2)[0:64, 0:D], A["rwkv_w2_2"][l]).then_inc(lora_weights.sem, 16)
            act.dma_start(flat(W2)[64:128, D:2 * D], A["rwkv_a2_2"][l]).then_inc(lora_weights.sem, 16)
            act.wait_ge(fronts_zeroed.sem, fronts_zeroed.due(act))
            for n, x in (("r", raw[0]), ("k", raw[1]), ("v", raw[2])):
                evict(act, j[n], keep(x, ACT.Copy, 1))
            act.wait_ge(lora_mixed.sem, lora_mixed.due(act))
            act.activation(WL[0:64, 1:], WL[0:64, 1:], ACT.Tanh)\
               .then_inc(lora_ready.sem, 1)
            act.wait_ge(lora_ready.sem, lora_ready.due(act))
            for k in range(DK):
                bank, full, free = abanks.empty()
                act.wait_ge(full.sem, full.due(act))
                act.activation(SW[:, k, :], bank[:, 0:T], ACT.Sigmoid, bias=col(n2("rwkv_w0"), k))\
                   .then_inc(scalar_step.sem, 1)
                act.wait_ge(scalar_step.sem, scalar_step.due(act))
                act.activation(AA[:, k, :], bank[:, T:], ACT.Sigmoid, bias=col(n2("rwkv_a0"), k))\
                   .then_inc(free.sem, 1)
                act.wait_ge(free.sem, free.due(act))
            act.nop().then_inc(lora_gates.sem, 1)
            for k in range(0, DK, 2):
                bank, full, free = abanks.empty()
                act.wait_ge(full.sem, full.due(act))
                act.activation(flat(SQR[:, k:k + 2, :]), bank, ACT.Sqrt)\
                   .then_inc(free.sem, 1)
                act.wait_ge(free.sem, free.due(act))
            act.nop().then_inc(head_rms.sem, 1)
            act.wait_ge(head_rms.sem, head_rms.due(act))
            act.wait_ge(cumulated.sem, cumulated.due(act))
            act.activation(flat(E1), flat(CC), ACT.Exp, scale=-KAPPA)\
               .then_inc(scalar_step.sem, 1)
            act.wait_ge(scalar_step.sem, scalar_step.due(act))
            act.activation(flat(E2), flat(CC), ACT.Exp, scale=KAPPA)\
               .then_inc(scalar_step.sem, 1)
            act.wait_ge(scalar_step.sem, scalar_step.due(act))
            act.activation(flat(SW), flat(SW), ACT.Exp, scale=-KAPPA)\
               .then_inc(decays.sem, 1)
            act.wait_ge(decays.sem, decays.due(act))
            for t in range(TT):
                for x in (VTK, KKT):
                    for n in range(2):
                        bank, full, free = abanks.empty()
                        act.wait_ge(full.sem, full.due(act))
                        act.activation(x[:, n * 512:n * 512 + 512], bank, ACT.Copy)\
                           .then_inc(free.sem, 1)
                        act.wait_ge(free.sem, free.due(act))
                for x in (KDT, BDT):
                    for n in range(2):
                        bank, full, free = abanks.empty()
                        act.wait_ge(full.sem, full.due(act))
                        for c in range(2):
                            sig = free if c else scalar_step
                            act.activation(x[c][:, n * 512:n * 512 + 512], bank, ACT.Copy, scale=half[:,
                                c:c + 1])\
                               .then_inc(sig.sem, 1)
                            act.wait_ge(sig.sem, sig.due(act))
                act.nop().then_inc(token_major.sem, 1)
                for level in range(1, 6):
                    for h in range(0, 16, 4):
                        bank, full, free = abanks.empty()
                        act.wait_ge(full.sem, full.due(act))
                        act.activation(flat(XX[:, h:h + 4, :]), bank, ACT.Copy)\
                           .then_inc(free.sem, 1)
                        act.wait_ge(free.sem, free.due(act))
                    for h in range(0, 16, 4):
                        bank, full, free = abanks.empty()
                        act.wait_ge(full.sem, full.due(act))
                        act.activation(flat(QQ[:, h:h + 4, :]), bank, ACT.Copy)\
                           .then_inc(free.sem, 1)
                        act.wait_ge(free.sem, free.due(act))
                        act.nop().then_inc(level_operands.sem, 1)
            for k in range(0, DK, 2):
                bank, full, free = abanks.empty()
                act.wait_ge(full.sem, full.due(act))
                act.activation(flat(RST[:, k:k + 2, :]), bank, ACT.Ln, bias=biases[:, 1:2],
                    scale=1.0 / 64)\
                   .then_inc(free.sem, 1)
                act.wait_ge(free.sem, free.due(act))
            act.activation(flat(RST), flat(RST), ACT.Exp, scale=-0.5)\
               .then_inc(head_rms.sem, 1)
            act.wait_ge(head_rms.sem, head_rms.due(act))
            evict(act, j["rz"], keep(ZR, ACT.Silu))
            act.wait_ge(evicted[0].sem, halves(0, j["mo"]))
            act.wait_ge(evicted[1].sem, halves(1, j["mo"]))
            evict(act, j["gb"], keep(GT, ACT.Sigmoid))

        def gla_act(j, l):
            act.wait_ge(evicted[0].sem, halves(0, j["ro"]))
            act.wait_ge(evicted[1].sem, halves(1, j["ro"]))
            act.wait_ge(merged_rwkv.sem, merged_rwkv.due(act))
            act.dma_start(G2[0:16, :], A["gla_w2_2"][l]).then_inc(lora_weights.sem, 16)
            evict(act, j["gq"], keep(GQ, ACT.Copy))
            evict(act, j["gk"], keep(GK, ACT.Copy))
            evict(act, j["gv"], keep_tokens(GV))
            act.wait_ge(gate_in.sem, gate_in.due(act))
            act.activation(flat(GE), flat(GE), ACT.Exp)\
               .then_inc(scalar_step.sem, 1)
            act.wait_ge(scalar_step.sem, scalar_step.due(act))
            act.activation(flat(GE), flat(GE), ACT.Ln, bias=biases[:, 2:3])\
               .then_inc(gate_out.sem, 1)
            act.wait_ge(gate_out.sem, gate_out.due(act))
            act.wait_ge(gla_sums.sem, gla_sums.due(act))
            act.activation(flat(GE), flat(GC), ACT.Exp, scale=1.0 / 16)\
               .then_inc(scalar_step.sem, 1)
            act.wait_ge(scalar_step.sem, scalar_step.due(act))
            act.activation(flat(GY), flat(GC), ACT.Exp, scale=-1.0 / 16)\
               .then_inc(scalar_step.sem, 1)
            act.wait_ge(scalar_step.sem, scalar_step.due(act))
            act.activation(flat(GD), flat(GD), ACT.Exp, scale=1.0 / 16)\
               .then_inc(scalar_step.sem, 1)
            act.wait_ge(scalar_step.sem, scalar_step.due(act))
            act.activation(EL, flat(GC).rearrange("p (c t) -> p c t", t=CH)[:, :, CH - 1], ACT.Exp,
                scale=1.0 / 16)\
               .then_inc(gla_exps.sem, 1)
            act.wait_ge(gla_exps.sem, gla_exps.due(act))
            for t in range(TT):
                bank, full, free = abanks.empty()
                act.wait_ge(full.sem, full.due(act))
                for c in range(2):
                    sig = free if c else scalar_step
                    act.activation(flat(KTT[c]), bank, ACT.Copy, scale=half[:, c:c + 1])\
                       .then_inc(sig.sem, 1)
                    act.wait_ge(sig.sem, sig.due(act))
                act.nop().then_inc(token_major.sem, 1)
            rms_act(256, 4)
            evict(act, j["gz"], keep(GZ, ACT.Silu))
            evict(act, j["gc"], keep(GT, ACT.Sigmoid))

        @block.scalar
        def _(_a):
            for _, _, free in abanks.banks:
                act.nop().then_inc(free.sem, 1)
                free.due(act)
            take_in_act()
            rec_act()
            ffn_act(0)
            att_act()
            ffn_act(1)
            act.wait_ge(second_begins.sem, second_begins.due(act))
            act.dma_start(ANG[:, 3, :].bitcast(I32), A["positions_2"][0].partition_broadcast(P)).then_inc(positions_landed.sem, 16)
            act.activation(CA[:, :, 0], col("c_2", 0, 8), ACT.Silu)\
               .then_inc(condition_ready.sem, 1)
            act.wait_ge(condition_ready.sem, condition_ready.due(act))
            act.wait_ge(angles_ready.sem, angles_ready.due(act))
            act.activation(SIN, ANG[:, 1, :], ACT.Sin)\
               .then_inc(scalar_step.sem, 1)
            act.wait_ge(scalar_step.sem, scalar_step.due(act))
            act.activation(COS, ANG[:, 2, :], ACT.Sin)\
               .then_inc(tables_ready.sem, 1)
            act.wait_ge(tables_ready.sem, tables_ready.due(act))
            for l in range(2):
                j = second[l]
                if l:
                    act.wait_ge(x_added.sem, x_added.due(act))
                evict(act, j["ada"], lambda i, bank, done, rounds:
                      act.activation(MOD.rearrange("p (a b) -> p a b", b=1)[:, bass.ds(i * 2, 2), :], bank[:, :, 0:1], ACT.Copy).then_inc(done, 1))
                rms_act(D)
                mla_act(j, l)
                rwkv_act(j, l)
                gla_act(j, l)
                evict(act, j["out"], keep(QN, ACT.Copy))
                rms_act(D)

        @block.sync
        def _(_s):
            for j in first_jobs:
                load(j)
            for s in range(2):
                sp.wait_ge(product[s].sem, (ffn_down[1].at + ffn_down[1].n) // 2)
            for l in range(2):
                for j in second[l].values():
                    load(j)
            sp.wait_ge(output_ready.sem, output_ready.due(sp))
            sp.dma_start(out[0].rearrange("(t p) d -> p t d", p=P), XIN).then_inc(output_written.sem, 16)
            sp.wait_ge(output_written.sem, 16)


NAMES = ["x", "rec_norm", "rec_w_in", "lru_conv_w", "lru_conv_b", "lru_w_r", "lru_b_r", "lru_w_i", "lru_b_i",
         "lru_lambda", "ssd_conv_w", "ssd_conv_b", "ssd_dt_bias", "ssd_a_log", "ssd_d", "ssd_norm", "rec_w_out",
         "att_norm", "att_w_qkv", "att_q_norm", "att_k_norm", "att_w_out", "ffn_norm", "ffn_w_gate_up",
         "ffn_w_down", "c_2", "positions_2", "ada_w_2", "ada_b_2", "norm_pre_2", "norm_post_2", "w_in_2",
         "rwkv_mu_2", "mla_q_norm_2", "mla_kv_norm_2", "mla_w_uq_2", "mla_w_ukv_2", "mla_w_o_2", "rwkv_w0_2",
         "rwkv_w2_2", "rwkv_a0_2", "rwkv_a2_2", "rwkv_k_k_2", "rwkv_k_a_2", "rwkv_r_k_2", "rwkv_ln_w_2",
         "rwkv_ln_b_2", "rwkv_w_o_2", "gla_w2_2", "gla_b_2", "gla_norm_2", "gla_w_o_2", "w_out_2"]


def kernel(**inputs):
    import numpy as _np
    import concourse.bacc as _bacc
    from concourse import mybir as _mybir
    from concourse.bass_utils import run_bass_kernel_spmd as _run

    nc = _bacc.Bacc("TRN2", target_bir_lowering=False, num_devices=1)
    arrays, args = {}, {}
    for name in NAMES + ["const"]:
        a = CONST if name == "const" else _np.ascontiguousarray(inputs[name])
        arrays[f"in_{name}"] = a
        args[name] = nc.dram_tensor(f"in_{name}", a.shape, _mybir.dt.from_np(a.dtype), kind="ExternalInput").ap()
    out = nc.dram_tensor("out_x", (1, T, D), F32, kind="ExternalOutput").ap()
    program(nc, args, out)
    r = _run(nc, [arrays], core_ids=[0])
    return r.results[0]["out_x"]
```

```python
from contextlib import ExitStack

import numpy as np

import concourse.bass as bass
from concourse import mybir

F32 = mybir.dt.float32
F32R = mybir.dt.float32r
I32 = mybir.dt.int32
ALU = mybir.AluOpType
ACT = mybir.ActivationFunctionType
AX = mybir.AxisListType.X

P = 128
T = 256
TT = T // P
D = 1024
DK = D // P
COLS = 256
EPS = 1e-6
GN_EPS = 64e-5
FFN = 2816
CH = 64



def constants():
    p = np.arange(P)
    s, t = p[:, None], p[None, :]
    same = s // CH == t // CH
    parts = {}
    parts["ident"] = np.eye(P)
    parts["ones"] = np.ones((P, P))
    parts["ones64"] = same * 1.0
    parts["tri"] = (s <= t) * 1.0
    parts["half"] = np.stack([p < 64, p >= 64], 1) * 1.0
    parts["neg_strict"] = -1.0 * (same & (t < s))
    parts["before"] = same & (s < t)
    parts["upto"] = same & (s <= t)
    for n in range(6):
        b = 1 << n
        parts[f"level{n}"] = (s // (2 * b) == t // (2 * b)) & ((s // b) % 2 == 0) & ((t // b) % 2 == 1)
    tok = np.arange(T)
    parts["run"] = np.tile((tok % CH != 0) * 1.0, (P, 1))
    q = (np.arange(TT)[None, :, None] * P + p[:, None, None])
    k = tok[None, None, :]
    count = (k <= q) * ((k >= q - 128) * 1 + ((q - k) % 4 == 0) * 1 + ((q - k) % 16 == 0) * 1)
    parts["windows"] = np.where(count > 0, np.log(np.maximum(count, 1)), -1e30).reshape(P, -1)
    parts["chunks"] = np.where(k // CH <= q // CH, 0.0, -1e30).reshape(P, -1)
    half = 8
    inv = np.float32(500000.0) ** (np.float32(-2.0) * np.arange(half, dtype=np.float32) / np.float32(16))
    ang = (tok[:, None].astype(np.float32) * inv[None, :].astype(np.float32)).astype(np.float32).T
    e = p % 64
    cos = np.ones((P, T))
    sin = np.zeros((P, T))
    for i in range(P):
        if e[i] < 16:
            cos[i], sin[i] = np.cos(ang[e[i] % 8]), np.sin(ang[e[i] % 8])
    rot = np.zeros((P, P))
    for i in range(P):
        if e[i] < 8:
            rot[i + 8, i] = -1.0
        elif e[i] < 16:
            rot[i - 8, i] = 1.0
    parts["att_cos"], parts["att_sin"], parts["att_rot"] = cos, sin, rot
    rot = np.zeros((P, P))
    for i in range(P):
        if e[i] < 32:
            rot[i + 32, i] = -1.0
        else:
            rot[i - 32, i] = 1.0
    parts["mla_rot"] = rot
    freq = np.float32(10000.0) ** (-np.arange(0, 64, 2, dtype=np.float32) / np.float32(64))
    parts["mla_freq"] = np.tile(np.concatenate([freq, freq]), 2)[:, None]
    at, n = {}, 0
    for name, a in parts.items():
        at[name] = (n, n + a.shape[1])
        n += a.shape[1]
    return np.concatenate([np.asarray(a, np.float32) for a in parts.values()], 1), at


CONST, CONST_AT = constants()



def vector_rows():
    sizes = [("rec_norm", 8), ("lru_conv_w", 32), ("lru_conv_b", 8), ("lru_b_r", 8), ("lru_b_i", 8),
             ("lru_lambda", 8), ("ssd_conv_w", 48), ("ssd_conv_b", 12), ("ssd_norm", 8), ("att_norm", 8),
             ("ffn_norm", 16), ("att_q_norm", 1), ("att_k_norm", 1), ("c_2", 8)]
    second = [(f"{n}_2", 2 * r) for n, r in (
        ("ada_b", 24), ("norm_pre", 8), ("norm_post", 8), ("rwkv_mu", 25), ("mla_q_norm", 4),
        ("mla_kv_norm", 2), ("rwkv_w0", 8), ("rwkv_a0", 8), ("rwkv_k_k", 8), ("rwkv_k_a", 8),
        ("rwkv_r_k", 8), ("rwkv_ln_w", 8), ("rwkv_ln_b", 8), ("gla_b", 4), ("gla_norm", 2))]
    at, pack, row = {}, 0, 0
    for name, n in sizes + second:
        if row + n > P or name == second[0][0]:
            pack, row = pack + 1, 0
        at[name] = (pack, row, n)
        row += n
    return at, at[second[0][0]][0], pack + 1


VEC_AT, FIRST_PACKS, PACKS = vector_rows()

SIZES = (("cq", 512), ("ckv", 256), ("kr", 64), ("mz", 1024), ("r", 1024), ("k", 1024), ("v", 1024),
         ("wl", 64), ("al", 64), ("rz", 1024), ("gq", 512), ("gk", 512), ("gv", 1024), ("gl", 16),
         ("gz", 1024), ("ga", 1024), ("gb", 1024), ("gc", 1024))
IN_AT = {}
_n = 0
for _name, _size in SIZES:
    IN_AT[_name] = _n
    _n += _size


class Count:

    def __init__(self, sem):
        self.sem, self.counts = sem, {}

    def due(self, eng, n=1):
        k = self.counts[id(eng)] = self.counts.get(id(eng), 0) + n
        return k


class Banks:

    def __init__(self, tiles, full, free):
        self.banks, self.filled, self.emptied = list(zip(tiles, full, free)), 0, 0

    def fill(self):
        tile, full, free = self.banks[self.filled % len(self.banks)]
        self.filled += 1
        return tile, free, full.sem

    def empty(self):
        self.emptied += 1
        return self.banks[(self.emptied - 1) % len(self.banks)]


def program(nc, A, out, stop=None):
    with ExitStack() as ctx:
        def sem(name):
            return Count(ctx.enter_context(nc.semaphore(name)))


        def flat(x):
            return x.rearrange("p a b -> p (a b)")

        AR = 53100
        COMMON = CONST.shape[1] + PACKS * P + 2 * DK * T + 6 * T + 4 + 56
        common = ctx.enter_context(nc.sbuf_tensor("common", [P, COMMON], F32))
        with nc.sbuf_tensor("arena", [P, AR - COMMON], F32) as arena:
            pass
        KD_ = FFN // P
        WHOLE = 2 * KD_ * COLS + 2 * 2 * T
        SPLIT_AT, SPLIT = COMMON + WHOLE, 2 * 2 * DK * COLS + 2 * DK * T + 2 * KD_ * T
        whole = ctx.enter_context(nc.sbuf_tensor("whole", [P, WHOLE], F32))
        parts = ctx.enter_context(nc.sbuf_tensor("parts", [P, SPLIT], F32R))
        psum = [ctx.enter_context(nc.psum_tensor(f"bank{i}", [P, 512], F32))[:, :] for i in range(8)]
        place = [0]

        def buf(*shape):
            n = int(np.prod(shape))
            at = place[0]
            place[0] += n
            assert place[0] <= AR, ("the arena is too small", place[0])
            v = common[:, at:at + n] if at < COMMON else arena[:, at - COMMON:at - COMMON + n]
            if len(shape) == 2:
                v = v.rearrange("p (a b) -> p a b", a=shape[0])
            if len(shape) == 3:
                v = v.rearrange("p (a b c) -> p a b c", a=shape[0], b=shape[1])
            return v

        cst = buf(CONST.shape[1])

        def const(name):
            return cst[:, CONST_AT[name][0]:CONST_AT[name][1]]

        ident, ones, ones64, half, tri = (const(n) for n in ("ident", "ones", "ones64", "half", "tri"))
        cols = buf(PACKS * P)

        def col(name, i=0, n=1):
            name, _, l = name.partition("/")
            pack, row, rows = VEC_AT[name]
            at = pack * P + row + i + (int(l) * (rows // 2) if l else 0)
            return cols[:, at:at + n]

        X = buf(DK, T)
        H = buf(DK, T)
        STAT = buf(4, T)
        biases = buf(4)
        COS, SIN = buf(T), buf(T)
        MODS, CA = [buf(24), buf(24)], buf(8)
        base = place[0]
        assert base == COMMON

        def views(kt):
            return [buf(kt, COLS), buf(kt, COLS)]

        WIDE = views(FFN // P)
        first_base = place[0]
        LX, XB = buf(DK, T + 3), buf(12, T + 3)
        G, Z, XC, RG, IG = (buf(DK, T) for _ in range(5))
        XBC, MIX = buf(12, T), buf(16, T)
        LRU_A = MIX[:, 8:16, :]
        BD = buf(2, DK, P)
        DT, DTB, DTC, DTD, DTE = (buf(TT, 16) for _ in range(5))
        AROW, CS = buf(3, 16), buf(TT, 16)
        LAM, LAMB, LAMC, LAMD, LAMX, DCOL, LAMA = (buf(8) for _ in range(7))
        LAST = buf(16)
        top_of_recurrent = place[0]
        place[0] = first_base
        spare = buf(DK * (T + 3) + 12 * (T + 3))
        XTOK = spare[:, 0:TT * D].rearrange("p (a b) -> p a b", a=TT)
        XDTE = spare[:, TT * D:TT * D + D]
        BTOK = spare[:, 3 * D:3 * D + 2 * P].rearrange("p (a b) -> p a b", a=2)
        CBM = spare[:, 3 * D + 2 * P:3 * D + 4 * P].rearrange("p (a b) -> p a b", a=2)
        PREV = spare[:, 3 * D + 4 * P:4 * D + 4 * P].rearrange("p (a b) -> p a b", a=2)
        UU = XTOK.rearrange("p a b -> p (a b)").rearrange("p (k t) -> p k t", k=DK)
        heads16 = "p (h l) -> p h l"
        ADTRI = RG.rearrange("p a b -> p (a b)").rearrange(heads16, h=16)
        SEG = IG.rearrange("p a b -> p (a b)").rearrange(heads16, h=16)
        ECS = XC.rearrange("p a b -> p (a b)").rearrange(heads16, h=16)
        place[0] = first_base
        WHOLE_W = [whole[:, n * KD_ * COLS:(n + 1) * KD_ * COLS].rearrange("p (k c) -> p k c", k=KD_) for n in range(2)]
        silu_g, hidden = (whole[:, 2 * KD_ * COLS + n * 2 * T:2 * KD_ * COLS + (n + 1) * 2 * T].rearrange("p (a b) -> p a b", a=2) for n in range(2))
        assert SPLIT_AT + SPLIT <= AR - 2 * 3 * D - (PACKS - FIRST_PACKS) * P
        slot_floats = DK * COLS
        part_slots = [[parts[:, (2 * s + e) * slot_floats:(2 * s + e + 1) * slot_floats] for e in range(2)] for s in range(2)]
        UP_W = [[x.rearrange("p (k c) -> p k c", k=DK) for x in pair] for pair in part_slots]
        DOWN_W = [[x[:, 0:KD_ // 2 * P].rearrange("p (k c) -> p k c", c=P) for x in pair] for pair in part_slots]
        H_PARTS = [parts[:, (4 + e) * slot_floats:(5 + e) * slot_floats].rearrange("p (k t) -> p k t", t=T) for e in range(2)]
        hidden_at = 6 * slot_floats
        HIDDEN_PARTS = [parts[:, hidden_at + e * KD_ * T:hidden_at + (e + 1) * KD_ * T].rearrange("p (k t) -> p k t", t=T) for e in range(2)]
        place[0] = SPLIT_AT + hidden_at
        SQF = buf(DK, T)
        place[0] = first_base
        Q, K, SQA, RS, ROT, O = (buf(DK, T) for _ in range(6))
        VT, KP = buf(TT, D), buf(16, T)
        SC, PR, PT = ([buf(TT, T) for _ in range(n)] for n in (2, 3, 2))
        MX, SM = [buf(TT) for _ in range(2)], [buf(TT) for _ in range(2)]
        place[0] = first_base
        PACK, XIN = buf(FIRST_PACKS, P), buf(TT, D)
        place[0] = AR - 2 * 3 * D - (PACKS - FIRST_PACKS) * P
        ADA_W, ADA_SUM, PACK2 = buf(2, 3 * D // 2), buf(2, 3 * D // 2), buf(PACKS - FIRST_PACKS, P)
        assert top_of_recurrent <= AR - 2 * 3 * D - (PACKS - FIRST_PACKS) * P

        place[0] = base
        SL = views(DK)
        M, GT = buf(DK, T), buf(DK, T)
        XOUT = flat(M).rearrange("p (t d) -> p t d", t=TT)
        GPRE, GPOST = buf(8), buf(8)
        WL, GL = buf(T + 1), buf(T)
        second_base = place[0]
        CQ, CKV, KR, QR, KRP = buf(4, T), buf(2, T), buf(1, T), buf(4, T), buf(2, T)
        QN, KN, ZM, OM, SQM = (buf(DK, T) for _ in range(5))
        VM = buf(TT, D)
        ROTM = buf(4, T)
        MSC, MPR, MPT = ([buf(TT, T) for _ in range(n)] for n in (2, 3, 2))
        MMX, MSM = [buf(TT) for _ in range(2)], [buf(TT) for _ in range(2)]
        ANG = buf(4, T)
        place[0] = second_base
        GQ, GK, GE, GX, GY, GC, GD, KINV, KTE = (buf(4, T) for _ in range(9))
        GV, OG, GZ, SQG = buf(TT, D), buf(DK, T), buf(DK, T), buf(DK, T)
        G2 = buf(512)
        KTT = [buf(4, P) for _ in range(2)]
        AT = buf(4, P)
        GS = [None] + [buf(4, T) for _ in range(3)]
        EL = buf(16)
        place[0] = second_base
        raw = [buf(DK, T + 1) for _ in range(3)]
        R, KR_, V_ = buf(DK, T), buf(DK, T), buf(DK, T)
        tile_base = place[0]
        BDT, KDT = [buf(D), buf(D)], [buf(D), buf(D)]
        VTK, KKT = buf(D), buf(D)
        PAD = buf(8 * 4, P)
        AN, XT, XX, QQ, BT = (buf(16, P) for _ in range(5))
        ST = [buf(8, P), KKT.rearrange("p (a b) -> p a b", a=DK)]
        ECEND = buf(DK, 4)
        KAI = buf(8)
        assert place[0] <= AR
        place[0] = tile_base
        AA, SW, CC, W2 = buf(DK, T), buf(DK, T), buf(DK, T), buf(16, P)
        E1, E2, SQR = buf(DK, T), buf(DK, T), buf(DK, T)
        assert place[0] <= AR - 2200

        KKD, BDF, BONUS = (x[:, :, 0:T] for x in raw)
        KFACTOR = flat(W2).rearrange("p (a b) -> p a b", a=DK)
        BVT = UT = flat(AN)[:, 0:D]
        WT = flat(AN)[:, D:2 * D].rearrange("p (a b) -> p a b", a=DK)
        ZT = flat(BT)[:, 0:D]
        SQT, RST = (flat(x).rearrange("p (a b) -> p a b", a=DK) for x in (XT, XX))
        ZR = flat(PAD)[:, 0:DK * T].rearrange("p (a b) -> p a b", a=DK)
        TMP = [flat(PAD)[:, DK * T + n * 512:DK * T + n * 512 + 512].rearrange("p (a b) -> p a b", a=2) for n in range(2)]
        TMPG = [flat(GE)[:, n * 512:n * 512 + 512].rearrange("p (a b) -> p a b", a=2) for n in range(2)]

        landed = [sem("weights_landed_a"), sem("weights_landed_b")]
        product = [sem("half_product_a"), sem("half_product_b")]
        evicted = [sem("half_evicted_a"), sem("half_evicted_b")]
        vector_step, scalar_step = sem("vector_step_done"), sem("scalar_step_done")
        vbanks = Banks(psum[2:5], [sem(f"full_for_vector_{i}") for i in range(3)],
                       [sem(f"vector_emptied_{i}") for i in range(3)])
        abanks = Banks(psum[5:8], [sem(f"full_for_scalar_{i}") for i in range(3)],
                       [sem(f"scalar_emptied_{i}") for i in range(3)])
        a_exp = sem("a_exp")
        a_ready = sem("a_ready")
        angles_ready = sem("angles_ready")
        biases_set = sem("biases_set")
        branch_ready = sem("branch_ready")
        bv_ready = sem("bv_ready")
        condition_ready = sem("condition_ready")
        conv_fronts_zeroed = sem("conv_fronts_zeroed")
        cumulated = sem("cumulated")
        decay_in = sem("decay_in")
        decay_out = sem("decay_out")
        decay_steps = sem("decay_steps")
        decays = sem("decays")
        fronts_zeroed = sem("fronts_zeroed")
        gate_in = sem("gate_in")
        gate_out = sem("gate_out")
        gla_exps = sem("gla_exps")
        gla_operands = sem("gla_operands")
        gla_states = sem("gla_states")
        gla_sums = sem("gla_sums")
        head_normed = sem("head_normed")
        head_rms = sem("head_rms")
        head_squares = sem("head_squares")
        heads_out = sem("heads_out")
        hidden_ready = sem("hidden_ready")
        inputs_landed = sem("inputs_landed")
        inverse_ready = sem("inverse_ready")
        keys_ready = sem("keys_ready")
        level_operands = sem("level_operands")
        lora_gates = sem("lora_gates")
        lora_mixed = sem("lora_mixed")
        lora_ready = sem("lora_ready")
        lora_weights = sem("lora_weights")
        lora_zeroed = sem("lora_zeroed")
        lru_conv_done = sem("lru_conv_done")
        lru_functions = sem("lru_functions")
        lru_gates = sem("lru_gates")
        lru_root = sem("lru_root")
        lru_root_in = sem("lru_root_in")
        lru_weights_landed = sem("lru_weights_landed")
        lru_weights_zeroed = sem("lru_weights_zeroed")
        merge_ready = sem("merge_ready")
        merged = sem("merged")
        merged_rwkv = sem("merged_rwkv")
        normed = sem("normed")
        output_ready = sem("output_ready")
        output_written = sem("output_written")
        packs_zeroed = sem("packs_zeroed")
        positions_landed = sem("positions_landed")
        probs_ready = sem("probs_ready")
        probs_scaled = sem("probs_scaled")
        probs_turned = sem("probs_turned")
        rate_ready = sem("rate_ready")
        rms_ready = sem("rms_ready")
        rows_landed = sem("rows_landed")
        scores_ready = sem("scores_ready")
        second_begins = sem("second_begins")
        softplus_exp = sem("softplus_exp")
        softplus_in = sem("softplus_in")
        squares_ready = sem("squares_ready")
        ssd_conv_done = sem("ssd_conv_done")
        ssd_operand = sem("ssd_operand")
        state_operand = sem("state_operand")
        state_ready = sem("state_ready")
        tables_ready = sem("tables_ready")
        tile_operands = sem("tile_operands")
        token_major = sem("token_major")
        u_ready = sem("u_ready")
        w_ready = sem("w_ready")
        x_ready = sem("x_ready")
        scaled = sem("scaled")
        scaled_out = sem("scaled_out")
        hi_ready = [sem("weights_hi_ready_a"), sem("weights_hi_ready_b")]
        lo_ready = [sem("weights_lo_ready_a"), sem("weights_lo_ready_b")]
        first_part_used = sem("first_part_used")
        h_ready = sem("h_ready")
        h_hi_ready = sem("h_hi_ready")
        hidden_hi_ready = sem("hidden_hi_ready")
        ada_landed = [sem("modulation_weights_landed_a"), sem("modulation_weights_landed_b")]
        ada_added = [sem("modulation_weights_added_a"), sem("modulation_weights_added_b")]
        second_rows_zeroed = sem("second_rows_zeroed")
        second_rows_landed = sem("second_rows_landed")
        modulation_products = sem("modulation_products")
        modulation_step = sem("modulation_step")
        modulation_scaled = sem("modulation_scaled")
        modulation_summed = sem("modulation_summed")
        xbc_ready = sem("xbc_ready")

        pe, dve, act, sp = nc.tensor, nc.vector, nc.scalar, nc.sync
        block = ctx.enter_context(nc.Block())

        def along(c, a, b):
            return c.unsqueeze(2).to_broadcast([P, a, b])

        def over(c, a, b):
            return c.unsqueeze(1).to_broadcast([P, a, b])

        class Job:

            def __init__(self, n, kt, rhs, loads, slots, by_token=False, width=COLS, per=1):
                self.n, self.kt, self.rhs, self.loads, self.slots = n, kt, rhs, loads, slots
                self.by_token, self.width, self.per = by_token, width, per
                self.at = None

            def each(self, eng, body):
                at = self.at
                if self.n >= 4:
                    assert at % 2 == 0 and self.n % 2 == 0 and at >= 2
                    with eng.Fori(0, self.n // 2) as j:
                        for s in range(2):
                            body(j * 2 + s, s, j + at // 2, j)
                    return
                for i in range(self.n):
                    body(i, (at + i) % 2, (at + i) // 2, i // 2)

        def load(job):
            def body(i, s, rounds, turn):
                if not isinstance(rounds, int) or rounds > 0:
                    sp.wait_ge(product[s].sem, rounds)
                for to, frm in job.loads(i, job.slots[s]):
                    sp.dma_start(to, frm).then_inc(landed[s].sem, 16)

            job.each(sp, body)

        def load_up(l):
            job, turns = ffn_up[l], turns_before[l]
            for s in range(2):
                sp.wait_ge(product[s].sem, job.at // 2)
                for to, frm in job.loads(s, WHOLE_W[s]):
                    sp.dma_start(to, frm).then_inc(landed[s].sem, 16)
            with sp.Fori(1, UPS) as j:
                for s in range(2):
                    sp.wait_ge(lo_ready[s].sem, j + turns)
                    for to, frm in job.loads(j * 2 + s, WHOLE_W[s]):
                        sp.dma_start(to, frm).then_inc(landed[s].sem, 16)

        def load_down(l):
            job, turns = ffn_down[l], turns_before[l]
            for q in range(2):
                sp.wait_ge(lo_ready[q].sem, turns + UPS)
                for to, frm in job.loads(q, WHOLE_W[q]):
                    sp.dma_start(to, frm).then_inc(landed[q].sem, 16)
            with sp.Fori(1, DK // 2) as j:
                for q in range(2):
                    sp.wait_ge(lo_ready[1].sem, j * 2 + (turns + UPS + q - 1))
                    for to, frm in job.loads(j * 2 + q, WHOLE_W[q]):
                        sp.dma_start(to, frm).then_inc(landed[q].sem, 16)

        def landed_before(job, s):
            return 16 * sum(j.per for j in all_jobs if j.at < job.at for i in range(j.n) if (j.at + i) % 2 == s)

        def multiply(job):
            n = job.rhs.shape[2]

            def body(i, s, rounds, turn):
                pe.wait_ge(landed[s].sem, turn * (16 * job.per) + (landed_before(job, s) + 16 * job.per))
                if not isinstance(rounds, int) or rounds > 0:
                    pe.wait_ge(evicted[s].sem, rounds)
                w = job.slots[s]
                bank = psum[s].rearrange("p (a b) -> p a b", a=2)
                if job.by_token:
                    for t in range(TT):
                        for k in range(job.kt):
                            last = pe.matmul(bank[:, t, 0:job.width], job.rhs[:, k, t * P:t * P + P],
                                             w[:, k, 0:job.width], start=k == 0, stop=k == job.kt - 1)
                else:
                    for m in range(-(-job.width // P)):
                        c = min(P, job.width - m * P)
                        for k in range(job.kt):
                            last = pe.matmul(bank[0:c, m, 0:n], w[:, k, m * P:m * P + c], job.rhs[:, k, :],
                                             start=k == 0, stop=k == job.kt - 1)
                last.then_inc(product[s].sem, 1)

            job.each(pe, body)

        def evict(eng, job, step):
            def body(i, s, rounds, turn):
                eng.wait_ge(product[s].sem, rounds + 1)
                step(i, psum[s].rearrange("p (a b) -> p a b", a=2), evicted[s].sem, rounds)

            job.each(eng, body)

        def halves(s, job):
            return (job.at + job.n + 1 - s) // 2

        def column_loads(w, lo, c=COLS, step=COLS):
            v = w.rearrange("(k p) n -> p k n", p=P)
            kt = v.shape[1]

            def loads(i, slot):
                frm = v[:, :, lo + i * step:lo + i * step + c] if isinstance(i, int) else v[:, :, bass.ds(i * step + lo, c)]
                return [(slot[:, 0:kt, 0:c], frm)]
            return loads

        def two(dst, i, lo=0, n=T):
            if isinstance(i, int):
                return dst[:, 2 * i:2 * i + 2, lo:lo + n]
            return dst[:, bass.ds(i * 2, 2), lo:lo + n]

        def tokens(dst, i):
            if isinstance(i, int):
                return dst[:, :, i * COLS:(i + 1) * COLS]
            return dst[:, :, bass.ds(i * COLS, COLS)]

        def keep(dst, func, lo=0):
            return lambda i, bank, done, rounds: act.activation(two(dst, i, lo), bank, func).then_inc(done, 1)

        def keep_tokens(dst):
            return lambda i, bank, done, rounds: act.activation(tokens(dst, i), bank, ACT.Copy).then_inc(done, 1)

        def add_to_x(i, bank, done, rounds):
            dve.tensor_tensor(two(X, i), bank, two(X, i), ALU.add).then_inc(done, 1)

        def sums_pe(sq, nt, groups=1):
            for g in range(groups):
                bank, free, done = abanks.fill()
                pe.wait_ge(free.sem, free.due(pe))
                for k in range(nt):
                    if k % 2 == 0:
                        pe.wait_ge(squares_ready.sem, squares_ready.due(pe))
                    last = pe.matmul(bank[:, 0:T], ones, sq[:, g * nt + k, :], start=k == 0, stop=k == nt - 1)
                last.then_inc(done, 1)

        def rms_act(n, groups=1, row=0):
            for g in range(row, row + groups):
                bank, full, free = abanks.empty()
                act.wait_ge(full.sem, full.due(act))
                act.activation(STAT[:, g, :], bank[:, 0:T], ACT.Ln, bias=biases[:, 0:1], scale=1.0 / n)\
                   .then_inc(free.sem, 1)
                act.wait_ge(free.sem, free.due(act))
            act.activation(STAT[:, row:row + groups, :], STAT[:, row:row + groups, :], ACT.Exp, scale=-0.5)\
               .then_inc(rms_ready.sem, 1)
            act.wait_ge(rms_ready.sem, rms_ready.due(act))

        def squares_v(src, sq, n):
            for k in range(0, n, 2):
                dve.tensor_tensor(sq[:, k:k + 2, :], src[:, k:k + 2, :], src[:, k:k + 2, :], ALU.mult)\
                   .then_inc(squares_ready.sem, 1)
            dve.wait_ge(squares_ready.sem, squares_ready.due(dve, n // 2))

        def norm_v(src, sq, nt, gain, dst, groups=1, shift=False, squared=False):
            if not squared:
                squares_v(src, sq, groups * nt)
            dve.wait_ge(rms_ready.sem, rms_ready.due(dve))
            n = groups * nt
            for k in range(n):
                by = scaled if shift else vector_step if k < n - 1 else normed
                dve.scalar_tensor_tensor(dst[:, k, :], src[:, k, :], gain(k), STAT[:, k // nt, :], ALU.mult, ALU.mult)\
                   .then_inc(by.sem, 1)
                by_due = by.due(dve)
            dve.wait_ge(by.sem, by_due)
            if shift:
                dve.wait_ge(normed.sem, normed.due(dve))

        def shift_act(dst, n, shift):
            for k in range(n):
                act.wait_ge(scaled.sem, scaled.due(act))
                by = normed if k == n - 1 else scalar_step
                act.activation(dst[:, k, :], dst[:, k, :], ACT.Identity, bias=shift(k)).then_inc(by.sem, 1)
                if k < n - 1:
                    by_due = by.due(act)
            act.wait_ge(scalar_step.sem, by_due)

        def head_sums_pe(sq, nt, banks, wait=True):
            if wait:
                pe.wait_ge(head_squares.sem, head_squares.due(pe))
            for k in range(0, nt, 2):
                bank, free, done = banks.fill()
                pe.wait_ge(free.sem, free.due(pe))
                pe.matmul(bank, ones64, flat(sq[:, k:k + 2, :]), start=True, stop=True).then_inc(done, 1)

        def turn_pe(pieces, banks):
            for i in range(0, len(pieces), 4):
                bank, free, done = banks.fill()
                pe.wait_ge(free.sem, free.due(pe))
                for n, x in enumerate(pieces[i:i + 4]):
                    last = pe.transpose(bank[:, n * P:n * P + P], x, ident)
                last.then_inc(done, 1)

        def softplus_v(x, a, b, c, dst):
            dve.scalar_tensor_tensor(a, x, -1.0, x, ALU.mult, ALU.min)\
               .then_inc(softplus_in.sem, 1)
            dve.wait_ge(softplus_in.sem, softplus_in.due(dve))
            dve.wait_ge(softplus_exp.sem, softplus_exp.due(dve))
            dve.tensor_scalar(b, a, 2.0, None, ALU.add)\
               .then_inc(vector_step.sem, 1)
            dve.wait_ge(vector_step.sem, vector_step.due(dve))
            dve.reciprocal(b, b)\
               .then_inc(vector_step.sem, 1)
            dve.wait_ge(vector_step.sem, vector_step.due(dve))
            dve.tensor_tensor(a, a, b, ALU.mult)\
               .then_inc(vector_step.sem, 1)
            dve.wait_ge(vector_step.sem, vector_step.due(dve))
            dve.tensor_tensor(b, a, a, ALU.mult)\
               .then_inc(vector_step.sem, 1)
            dve.wait_ge(vector_step.sem, vector_step.due(dve))
            dve.tensor_scalar(c, b, 1.0 / 17, None, ALU.mult)\
               .then_inc(vector_step.sem, 1)
            dve.wait_ge(vector_step.sem, vector_step.due(dve))
            for n in (15, 13, 11, 9, 7, 5, 3):
                dve.scalar_tensor_tensor(c, c, 1.0 / n, b, ALU.add, ALU.mult)\
                   .then_inc(vector_step.sem, 1)
                dve.wait_ge(vector_step.sem, vector_step.due(dve))
            dve.scalar_tensor_tensor(c, c, 1.0, a, ALU.add, ALU.mult)\
               .then_inc(vector_step.sem, 1)
            dve.wait_ge(vector_step.sem, vector_step.due(dve))
            dve.tensor_scalar(b, x, 0.0, None, ALU.max)\
               .then_inc(vector_step.sem, 1)
            dve.wait_ge(vector_step.sem, vector_step.due(dve))
            dve.scalar_tensor_tensor(dst, c, 2.0, b, ALU.mult, ALU.add)\
               .then_inc(vector_step.sem, 1)
            dve.wait_ge(vector_step.sem, vector_step.due(dve))

        def softplus_act(a):
            act.wait_ge(softplus_in.sem, softplus_in.due(act))
            act.activation(a, a, ACT.Exp)\
               .then_inc(softplus_exp.sem, 1)
            act.wait_ge(softplus_exp.sem, softplus_exp.due(act))

        w_in = A["rec_w_in"][0]
        dt_cols = w_in.rearrange("(k p) n -> p k n", p=P)
        rec_dt = Job(2, DK, H, lambda i, slot: [(slot[:, 0:DK, 0:8], dt_cols[:, :, 4608 + 8 * i:4616 + 8 * i])],
                     WIDE, by_token=True, width=8)
        rec_x = Job(4, DK, H, column_loads(w_in, 0), WIDE)
        rec_xbc = Job(6, DK, H, column_loads(w_in, 3 * D), WIDE)
        rec_gate = Job(4, DK, H, column_loads(w_in, D), WIDE)
        rec_z = [Job(n, DK, H, column_loads(w_in, 2 * D + i * COLS), WIDE) for i, n in ((0, 2), (2, 1), (3, 1))]
        rec_out = Job(4, 16, MIX, column_loads(A["rec_w_out"][0], 0), WIDE)
        att_q, att_k = (Job(4, DK, H, column_loads(A["att_w_qkv"][0], n * D), WIDE) for n in range(2))
        att_v = [Job(2, DK, H, column_loads(A["att_w_qkv"][0], 2 * D + n * 512), WIDE, by_token=True) for n in range(2)]
        att_out = Job(4, DK, O, column_loads(A["att_w_out"][0], 0), WIDE)

        def ffn_loads(l):
            up = A["ffn_w_gate_up"][l].rearrange("(k p) n -> p k n", p=P)

            def loads(i, slot):
                lo = 0 if slot is WHOLE_W[0] else FFN - COLS // 2
                return [(slot[:, 0:DK, :], up[:, :, bass.ds(i * (COLS // 2) + lo, COLS)])]
            return loads

        ffn_up = [Job(2 * FFN // COLS, DK, H, ffn_loads(l), WHOLE_W) for l in range(2)]
        ffn_down = [Job(DK, KD_, hidden, column_loads(A["ffn_w_down"][l], 0, P, P), WHOLE_W) for l in range(2)]
        UPS = KD_ // 2
        turns_before = [l * (UPS + DK) for l in range(2)]
        first_jobs = [rec_dt, rec_x, rec_xbc, rec_gate, *rec_z, rec_out, ffn_up[0], ffn_down[0],
                      att_q, att_k, *att_v, att_out, ffn_up[1], ffn_down[1]]

        def second_jobs(l):
            w = A["w_in_2"][l]
            wv = w.rearrange("(k p) n -> p k n", p=P)
            uq = A["mla_w_uq_2"][l].rearrange("(k p) (h c) -> p k h c", p=P, c=192)
            ukv = A["mla_w_ukv_2"][l].rearrange("(k p) (h c) -> p k h c", p=P, c=256)

            def proj(name, n, rhs=H, **kw):
                return Job(n, DK, rhs, column_loads(w, IN_AT[name]), SL, **kw)

            def part(name, i, n):
                return Job(n, DK, H, column_loads(w, IN_AT[name] + i * COLS), SL)

            def kr_loads(i, slot):
                frm = wv[:, :, IN_AT["kr"]:IN_AT["kr"] + 64]
                return [(slot[:, 0:DK, 0:64], frm), (slot[:, 0:DK, 64:128], frm)]

            def head_loads(v, kt, heads, lo, c):
                def loads(i, slot):
                    out = []
                    for k in range(kt):
                        to = slot[:, k, 0:heads * c].rearrange("p (h c) -> p h c", h=heads)
                        if isinstance(i, int):
                            out.append((to, v[:, k, i * heads:(i + 1) * heads, lo:lo + c]))
                        else:
                            out.append((to, v[:, k, bass.ds(i * heads, heads), lo:lo + c]))
                    return out
                return loads

            one = column_loads
            return {
                "cq": proj("cq", 2), "ckv": proj("ckv", 1),
                "kr": Job(1, DK, H, kr_loads, SL, width=128, per=2),
                "wl": Job(1, DK, H, one(w, IN_AT["wl"], 128), SL, width=128),
                "gl": Job(1, DK, H, one(w, IN_AT["gl"], 16), SL, width=16),
                "mz": proj("mz", 4), "ga": proj("ga", 4),
                "uqn": Job(4, 4, CQ, head_loads(uq, 4, 2, 0, 128), SL, per=4),
                "uqr": Job(2, 4, CQ, head_loads(uq, 4, 4, 128, 64), SL, per=4),
                "ukn": Job(4, 2, CKV, head_loads(ukv, 2, 2, 0, 128), SL, per=2),
                "ukv": Job(4, 2, CKV, head_loads(ukv, 2, 2, 128, 128), SL, per=2, by_token=True),
                "mo": Job(4, DK, OM, column_loads(A["mla_w_o_2"][l], 0), SL),
                "k": proj("k", 4), "r": proj("r", 4), "v": proj("v", 4),
                "gb0": part("gb", 0, 2), "gb1": part("gb", 2, 1), "gb2": part("gb", 3, 1),
                "rz0": part("rz", 0, 2), "rz1": part("rz", 2, 1), "rz2": part("rz", 3, 1),
                "gq": proj("gq", 2), "gk": proj("gk", 2),
                "ro": Job(4, DK, R, column_loads(A["rwkv_w_o_2"][l], 0), SL),
                "gv": proj("gv", 4, by_token=True),
                "gz": proj("gz", 4), "gc": proj("gc", 4),
                "go": Job(4, DK, OG, column_loads(A["gla_w_o_2"][l], 0), SL),
                "out": Job(4, DK, M, column_loads(A["w_out_2"][l], 0), SL),
            }

        second = [second_jobs(l) for l in range(2)]
        at = 0
        all_jobs = first_jobs + [j for l in range(2) for j in second[l].values()]
        for j in all_jobs:
            j.at = at
            at += j.n

        def attend_pe(heads, score, value, turned):
            for i in range(heads + 3):
                if i < heads:
                    bank, free, done = vbanks.fill()
                    pe.wait_ge(free.sem, free.due(pe))
                    score(i, bank.rearrange("p (a b) -> p a b", a=TT)).then_inc(done, 1)
                if 2 <= i <= heads + 1:
                    pe.wait_ge(probs_scaled.sem, probs_scaled.due(pe))
                    pr = turned[0][(i - 2) % 3]
                    bank, free, done = abanks.fill()
                    pe.wait_ge(free.sem, free.due(pe))
                    for s in range(TT):
                        for t in range(TT):
                            last = pe.transpose(bank[:, s * T + t * P:s * T + t * P + P], pr[:, t, s * P:s * P + P], ident)
                    last.then_inc(done, 1)
                if i >= 3:
                    pe.wait_ge(probs_turned.sem, probs_turned.due(pe))
                    bank, free, done = vbanks.fill()
                    pe.wait_ge(free.sem, free.due(pe))
                    for s in range(TT):
                        last = pe.matmul(bank[:, 0:T], value(i - 3, s), turned[1][(i - 3) % 2][:, s, :], start=s == 0, stop=s == TT - 1)
                    last.then_inc(done, 1)

        def attend_v(heads, scale, mask, sc, pr, mx, sm, take):
            for i in range(heads + 3):
                if i < heads:
                    bank, full, free = vbanks.empty()
                    dve.wait_ge(full.sem, full.due(dve))
                    dve.scalar_tensor_tensor(flat(sc[i % 2]), bank, scale, mask, ALU.mult, ALU.add)\
                       .then_inc(free.sem, 1)
                    dve.wait_ge(free.sem, free.due(dve))
                    dve.reduce_max(mx[i % 2], sc[i % 2], axis=AX)\
                       .then_inc(vector_step.sem, 1)
                    dve.wait_ge(vector_step.sem, vector_step.due(dve))
                    dve.tensor_scalar(mx[i % 2], mx[i % 2], -1.0, None, ALU.mult)\
                       .then_inc(scores_ready.sem, 1)
                    dve.wait_ge(scores_ready.sem, scores_ready.due(dve))
                if 1 <= i <= heads:
                    dve.wait_ge(probs_ready.sem, probs_ready.due(dve))
                    sums, probs = sm[(i - 1) % 2], pr[(i - 1) % 3]
                    dve.reciprocal(sums, sums)\
                       .then_inc(vector_step.sem, 1)
                    dve.wait_ge(vector_step.sem, vector_step.due(dve))
                    dve.tensor_tensor(probs, probs, along(sums, TT, T), ALU.mult)\
                       .then_inc(probs_scaled.sem, 1)
                    dve.wait_ge(probs_scaled.sem, probs_scaled.due(dve))
                if i >= 3:
                    bank, full, free = vbanks.empty()
                    dve.wait_ge(full.sem, full.due(dve))
                    take(i - 3, bank[:, 0:T], free)

        def attend_act(heads, sc, pr, pt, mx, sm):
            for i in range(heads + 2):
                if i >= 2:
                    bank, full, free = abanks.empty()
                    act.wait_ge(full.sem, full.due(act))
                    act.activation(flat(pt[(i - 2) % 2]), bank, ACT.Copy)\
                       .then_inc(free.sem, 1)
                    act.wait_ge(free.sem, free.due(act))
                    act.nop().then_inc(probs_turned.sem, 1)
                if i < heads:
                    act.wait_ge(scores_ready.sem, scores_ready.due(act))
                    n = i % 2
                    for t in range(TT):
                        sig = probs_ready if t else scalar_step
                        act.activation(pr[i % 3][:, t, :], sc[n][:, t, :], ACT.Exp, bias=mx[n][:, t:t + 1],
                            accum_out=sm[n][:, t:t + 1])\
                           .then_inc(sig.sem, 1)
                        act.wait_ge(sig.sem, sig.due(act))

        first_vectors = {name: v for name, v in VEC_AT.items() if v[0] < FIRST_PACKS}
        second_vectors = {name: v for name, v in VEC_AT.items() if v[0] >= FIRST_PACKS}
        n_inputs = 2 + len(first_vectors) + 2

        def rows_of(key):
            src = A[key] if key.endswith("_2") or key == "ffn_norm" else A[key][0]
            if len(src.shape) > 1:
                letters = "abc"[:len(src.shape)]
                src = src.rearrange(" ".join(letters) + " -> (" + " ".join(letters) + ")")
            return src

        def take_in_pe():
            pe.wait_ge(inputs_landed.sem, inputs_landed.due(pe, 16 * n_inputs))
            turn_pe([PACK[:, i, :] for i in range(FIRST_PACKS)], vbanks)
            turn_pe([XIN[:, t, k * P:k * P + P] for k in range(DK) for t in range(TT)], vbanks)

        def lru_pe():
            pe.wait_ge(lru_conv_done.sem, lru_conv_done.due(pe))
            pe.wait_ge(lru_weights_landed.sem, lru_weights_landed.due(pe, 64))
            for k in range(DK):
                bank, free, done = abanks.fill()
                pe.wait_ge(free.sem, free.due(pe))
                pe.matmul(bank[:, 0:T], BD[:, 0, k, :], XC[:, k, :], start=True, stop=True)
                pe.matmul(bank[:, T:], BD[:, 1, k, :], XC[:, k, :], start=True, stop=True).then_inc(done, 1)

        def ssd_pe():
            for t in range(TT):
                here = slice(t * P, t * P + P)
                pe.wait_ge(decay_steps.sem, decay_steps.due(pe))
                bank, free, done = vbanks.fill()
                pe.wait_ge(free.sem, free.due(pe))
                pe.matmul(bank[:, 0:16], tri, DTB[:, t, :], start=True, stop=True).then_inc(done, 1)
                for h in range(0, 16, 4):
                    bank, free, done = vbanks.fill()
                    pe.wait_ge(free.sem, free.due(pe))
                    pe.matmul(bank, ones, flat(ADTRI[:, h:h + 4, :]), start=True, stop=True).then_inc(done, 1)
                if t == 0:
                    pe.wait_ge(xbc_ready.sem, xbc_ready.due(pe))
                bank, free, done = vbanks.fill()
                pe.wait_ge(free.sem, free.due(pe))
                for g in range(2):
                    last = pe.matmul(bank[:, g * P:g * P + P], XBC[:, 8 + g, here], XBC[:, 10 + g, here], start=True, stop=True)
                last.then_inc(done, 1)
                turn_pe([XBC[:, k, here] for k in range(DK)], vbanks)
                if t == 0:
                    turn_pe([XBC[:, 8 + g, here] for g in range(2)], vbanks)
                    pe.wait_ge(state_operand.sem, state_operand.due(pe))
                    for g in range(2):
                        bank, free, done = vbanks.fill()
                        pe.wait_ge(free.sem, free.due(pe))
                        pe.matmul(bank, BTOK[:, g, :], XDTE[:, g * 512:g * 512 + 512], start=True, stop=True).then_inc(done, 1)
                multiply(rec_z[1 + t])
                pe.wait_ge(ssd_operand.sem, ssd_operand.due(pe))
                for h in range(0, 16, 4):
                    bank, free, done = vbanks.fill()
                    pe.wait_ge(free.sem, free.due(pe))
                    for n in range(4):
                        e = (h + n) // 2
                        o = bank[:, n * P:n * P + P]
                        last = pe.matmul(o, XTOK[:, t, e * P:e * P + P], SEG[:, h + n, :], start=True, stop=t == 0)
                        if t:
                            last = pe.matmul(o, PREV[:, e // 4, (e % 4) * P:(e % 4) * P + P], ECS[:, h + n, :], start=False, stop=True)
                    last.then_inc(done, 1)

        def three_passes(bank, weights, m, n, x, start, stop):
            for k in range(n):
                w_hi, w_lo = (w[:, k, m] for w in weights)
                x_hi, x_lo = (e[:, k, :] for e in x)
                pe.matmul(bank, w_hi, x_hi, start=start and k == 0, stop=False)
                pe.matmul(bank, w_hi, x_lo, start=False, stop=False)
                last = pe.matmul(bank, w_lo, x_hi, start=False, stop=stop and k == n - 1)
            return last

        def ffn_pe(l):
            sums_pe(SQF, DK)
            pe.wait_ge(normed.sem, normed.due(pe))
            up, down, turns = ffn_up[l].at // 2, ffn_down[l].at // 2, turns_before[l]
            with pe.Fori(0, UPS) as j:
                for s in range(2):
                    pe.wait_ge(lo_ready[s].sem, j + (turns + 1))
                    pe.wait_ge(evicted[s].sem, j + up)
                    for m in range(2):
                        last = three_passes(psum[s][:, m * T:m * T + T], UP_W[s], slice(m * P, m * P + P), DK, H_PARTS, True, True)
                    last.then_inc(product[s].sem, 1)
            pe.wait_ge(hidden_ready.sem, hidden_ready.due(pe, UPS))
            with pe.Fori(0, DK // 2) as j:
                for q in range(2):
                    pe.wait_ge(evicted[q].sem, j + down)
                    pe.wait_ge(lo_ready[0].sem, j * 2 + (turns + UPS + q + 1))
                    three_passes(psum[q][:, 0:T], DOWN_W[0], slice(0, P), UPS, [x[:, 0:UPS] for x in HIDDEN_PARTS], True, False)\
                        .then_inc(first_part_used.sem, 1)
                    pe.wait_ge(lo_ready[1].sem, j * 2 + (turns + UPS + q + 1))
                    three_passes(psum[q][:, 0:T], DOWN_W[1], slice(0, P), UPS, [x[:, UPS:] for x in HIDDEN_PARTS], False, True)\
                        .then_inc(product[q].sem, 1)

        def modulation_pe():
            pe.wait_ge(modulation_products.sem, modulation_products.due(pe, 2))
            bank, free, done = abanks.fill()
            pe.wait_ge(free.sem, free.due(pe))
            sums = flat(ADA_SUM)
            for m in range(24):
                last = pe.matmul(bank[:, m:m + 1], sums[:, m * P:m * P + P], ones[:, 0:1], start=True, stop=True)
            last.then_inc(done, 1)

        def att_pe():
            sums_pe(SQA, DK)
            pe.wait_ge(normed.sem, normed.due(pe))
            multiply(att_q)
            multiply(att_k)
            for n, x in enumerate((Q, K)):
                head_sums_pe(SQA, DK, abanks)
                multiply(att_v[n])
                pe.wait_ge(head_normed.sem, head_normed.due(pe))
                for k in range(0, DK, 2):
                    bank, free, done = vbanks.fill()
                    pe.wait_ge(free.sem, free.due(pe))
                    pe.matmul(bank, const("att_rot"), flat(x[:, k:k + 2, :]), start=True, stop=True).then_inc(done, 1)
            pe.wait_ge(keys_ready.sem, keys_ready.due(pe))

            def score(h, bank):
                for t in range(TT):
                    last = pe.matmul(bank[:, t, :], Q[:, h // 2, t * P:t * P + P], KP[:, h, :], start=True, stop=True)
                return last

            pe.wait_ge(evicted[0].sem, halves(0, att_v[1]))
            pe.wait_ge(evicted[1].sem, halves(1, att_v[1]))
            attend_pe(16, score, lambda h, s: VT[:, s, (h // 2) * P:(h // 2) * P + P], (PR, PT))
            pe.wait_ge(heads_out.sem, heads_out.due(pe))
            multiply(att_out)

        def mla_pe(j):
            for n in ("cq", "ckv", "kr", "wl", "gl"):
                multiply(j[n])
            sums_pe(SQM[:, 0:4], 4)
            sums_pe(SQM[:, 4:6], 2)
            multiply(j["mz"])
            bank, free, done = vbanks.fill()
            pe.wait_ge(free.sem, free.due(pe))
            pe.matmul(bank[:, 0:T], const("mla_rot"), KR[:, 0, :], start=True, stop=True).then_inc(done, 1)
            multiply(j["ga"])
            pe.wait_ge(normed.sem, normed.due(pe))
            multiply(j["uqn"])
            multiply(j["uqr"])
            pe.wait_ge(normed.sem, normed.due(pe))
            multiply(j["ukn"])
            pe.wait_ge(evicted[0].sem, halves(0, j["uqr"]))
            pe.wait_ge(evicted[1].sem, halves(1, j["uqr"]))
            for k in range(0, 4, 2):
                bank, free, done = vbanks.fill()
                pe.wait_ge(free.sem, free.due(pe))
                pe.matmul(bank, const("mla_rot"), flat(QR[:, k:k + 2, :]), start=True, stop=True).then_inc(done, 1)
            multiply(j["ukv"])
            pe.wait_ge(evicted[0].sem, halves(0, j["ukv"]))
            pe.wait_ge(evicted[1].sem, halves(1, j["ukv"]))
            pe.wait_ge(keys_ready.sem, keys_ready.due(pe))

            def score(h, bank):
                for t in range(TT):
                    here = slice(t * P, t * P + P)
                    pe.matmul(bank[:, t, :], QN[:, h, here], KN[:, h, :], start=True, stop=False)
                    last = pe.matmul(bank[:, t, :], QR[:, h // 2, here], KRP[:, h % 2, :], start=False, stop=True)
                return last

            attend_pe(8, score, lambda h, s: VM[:, s, h * P:h * P + P], (MPR, MPT))
            pe.wait_ge(heads_out.sem, heads_out.due(pe))
            multiply(j["mo"])

        def rwkv_pe(j):
            multiply(j["k"])
            pe.wait_ge(lora_ready.sem, lora_ready.due(pe))
            pe.wait_ge(lora_weights.sem, lora_weights.due(pe, 32))
            for k in range(DK):
                bank, free, done = abanks.fill()
                pe.wait_ge(free.sem, free.due(pe))
                pe.matmul(bank[:, 0:T], flat(W2)[:, k * P:k * P + P], WL[:, 1:], start=True, stop=True)
                pe.matmul(bank[:, T:], flat(W2)[:, D + k * P:D + k * P + P], WL[:, 1:], start=True, stop=True).then_inc(done, 1)
            multiply(j["r"])
            head_sums_pe(SQR, DK, abanks)
            multiply(j["v"])
            head_sums_pe(SQR, DK, vbanks)
            multiply(j["gb0"])
            for t in range(TT):
                pe.wait_ge(tile_operands.sem, tile_operands.due(pe))
                rd, kkd, kd, bd = (x[:, :, t * P:t * P + P] for x in (R, KKD, KR_, BDF))
                turn_pe([V_[:, k, t * P:t * P + P] for k in range(DK)], abanks)
                turn_pe([kkd[:, k, :] for k in range(DK)], abanks)
                turn_pe([kd[:, k, :] for k in range(DK)], abanks)
                turn_pe([bd[:, k, :] for k in range(DK)], abanks)
                for k in range(0, DK, 2):
                    bank, free, done = vbanks.fill()
                    pe.wait_ge(free.sem, free.due(pe))
                    for n in range(4):
                        last = pe.matmul(bank[:, n * P:n * P + P], PAD[:, (k + n // 2) * 4 + n % 2, :], bd[:, k + n // 2, :], start=True, stop=True)
                    last.then_inc(done, 1)
                for k in range(0, DK, 2):
                    bank, free, done = vbanks.fill()
                    pe.wait_ge(free.sem, free.due(pe))
                    for n in range(2):
                        last = pe.matmul(bank[:, n * T:n * T + T], kd[:, k + n, :], flat(PAD[:, (k + n) * 4:(k + n) * 4 + 2, :]), start=True, stop=True)
                    last.then_inc(done, 1)
                for h in range(0, 16, 4):
                    if h == 0:
                        pe.wait_ge(a_ready.sem, a_ready.due(pe))
                    turn_pe([AN[:, h + n, :] for n in range(4)], vbanks)
                for level in range(1, 6):
                    for h in range(0, 16, 4):
                        pe.wait_ge(inverse_ready.sem, inverse_ready.due(pe))
                        turn_pe([XT[:, h + n, :] for n in range(4)], abanks)
                    for h in range(0, 16, 4):
                        bank, free, done = abanks.fill()
                        pe.wait_ge(free.sem, free.due(pe))
                        for n in range(4):
                            last = pe.matmul(bank[:, n * P:n * P + P], AN[:, h + n, :], XT[:, h + n, :], start=True, stop=True)
                        last.then_inc(done, 1)
                    for h in range(0, 16, 4):
                        pe.wait_ge(level_operands.sem, level_operands.due(pe))
                        bank, free, done = vbanks.fill()
                        pe.wait_ge(free.sem, free.due(pe))
                        for n in range(4):
                            last = pe.matmul(bank[:, n * P:n * P + P], XX[:, h + n, :], QQ[:, h + n, :], start=True, stop=True)
                        last.then_inc(done, 1)
                pe.wait_ge(inverse_ready.sem, inverse_ready.due(pe, 4))
                pe.wait_ge(token_major.sem, token_major.due(pe))
                for h in range(0, 16, 8):
                    bank, free, done = vbanks.fill()
                    pe.wait_ge(free.sem, free.due(pe))
                    for n in range(8):
                        last = pe.matmul(bank[:, n * 64:n * 64 + 64], BT[:, h + n, :], VTK[:, (h + n) * 64:(h + n) * 64 + 64], start=True, stop=True)
                    last.then_inc(done, 1)
                for h in range(0, 16, 4):
                    bank, free, done = vbanks.fill()
                    pe.wait_ge(free.sem, free.due(pe))
                    for n in range(4):
                        e = (h + n) // 2
                        last = pe.matmul(bank[:, n * P:n * P + P], KKT[:, e * P:e * P + P], XT[:, h + n, :], start=True, stop=True)
                    last.then_inc(done, 1)
                pe.wait_ge(bv_ready.sem, bv_ready.due(pe))
                for h in range(0, 16, 8):
                    bank, free, done = vbanks.fill()
                    pe.wait_ge(free.sem, free.due(pe))
                    for n in range(8):
                        last = pe.matmul(bank[:, n * 64:n * 64 + 64], XT[:, h + n, :], BVT[:, (h + n) * 64:(h + n) * 64 + 64], start=True, stop=True)
                    last.then_inc(done, 1)
                for n, x in enumerate((bd, kd)):
                    for k in range(0, DK, 2):
                        bank, free, done = vbanks.fill()
                        pe.wait_ge(free.sem, free.due(pe))
                        for m in range(2):
                            last = pe.matmul(bank[:, m * T:m * T + T], x[:, k + m, :], flat(PAD[:, (k + m) * 4 + 2:(k + m) * 4 + 4, :]), start=True, stop=True)
                        last.then_inc(done, 1)
                if t == TT - 1:
                    multiply(j["rz0"])
                pe.wait_ge(w_ready.sem, w_ready.due(pe))
                for c in range(2):
                    pe.wait_ge(state_ready.sem, state_ready.due(pe))
                    for k in range(0, DK, 4):
                        bank, free, done = vbanks.fill()
                        pe.wait_ge(free.sem, free.due(pe))
                        for n in range(4):
                            last = pe.matmul(bank[:, n * P:n * P + P], WT[:, k + n, :], ST[c][:, k + n, :], start=True, stop=True)
                        last.then_inc(done, 1)
                    multiply(j[f"{'rz' if t else 'gb'}{c + 1}"])
                    pe.wait_ge(u_ready.sem, u_ready.due(pe))
                    if c == 1:
                        for h in range(0, 16, 4):
                            bank, free, done = vbanks.fill()
                            pe.wait_ge(free.sem, free.due(pe))
                            for n in range(4):
                                e, o = (h + n) // 2, bank[:, n * P:n * P + P]
                                at = slice(e * P, e * P + P)
                                pe.matmul(o, UT[:, at], XX[:, h + n, :], start=True, stop=False)
                                pe.matmul(o, VTK[:, at], QQ[:, h + n, :], start=False, stop=False)
                                pe.matmul(o[:, 0:CH], ST[0][:, e, :], rd[:, e, 0:CH], start=False, stop=False)
                                last = pe.matmul(o[:, CH:P], ST[1][:, e, :], rd[:, e, CH:P], start=False, stop=True)
                            last.then_inc(done, 1)
                    if (t, c) != (TT - 1, 1):
                        for k in range(0, DK, 4):
                            bank, free, done = vbanks.fill()
                            pe.wait_ge(free.sem, free.due(pe))
                            for n in range(4):
                                at = slice((k + n) * P, (k + n) * P + P)
                                pe.matmul(bank[:, n * P:n * P + P], BDT[c][:, at], UT[:, at], start=True, stop=False)
                                last = pe.matmul(bank[:, n * P:n * P + P], KDT[c][:, at], VTK[:, at], start=False, stop=True)
                            last.then_inc(done, 1)
            head_sums_pe(R, DK, vbanks)
            head_sums_pe(SQT, DK, abanks)
            multiply(j["gq"])
            multiply(j["gk"])
            pe.wait_ge(branch_ready.sem, branch_ready.due(pe))
            multiply(j["ro"])

        def gla_pe(j):
            pe.wait_ge(lora_weights.sem, lora_weights.due(pe, 16))
            for h in range(0, 4, 2):
                bank, free, done = vbanks.fill()
                pe.wait_ge(free.sem, free.due(pe))
                for n in range(2):
                    last = pe.matmul(bank[:, n * T:n * T + T], G2[0:16, (h + n) * P:(h + n) * P + P], GL[0:16, :], start=True, stop=True)
                last.then_inc(done, 1)
            for n in ("gv", "gz"):
                multiply(j[n])
            pe.wait_ge(evicted[0].sem, halves(0, j["gv"]))
            pe.wait_ge(evicted[1].sem, halves(1, j["gv"]))
            pe.wait_ge(gla_operands.sem, gla_operands.due(pe))
            for t in range(TT):
                here = slice(t * P, t * P + P)
                turn_pe([KTE[:, h, here] for h in range(4)], abanks)
                bank, free, done = vbanks.fill()
                pe.wait_ge(free.sem, free.due(pe))
                for h in range(4):
                    last = pe.matmul(bank[:, h * P:h * P + P], KINV[:, h, here], GX[:, h, here], start=True, stop=True)
                last.then_inc(done, 1)
                pe.wait_ge(token_major.sem, token_major.due(pe))
                for c in range(2):
                    if (t, c) != (TT - 1, 1):
                        for h in range(0, 4, 2):
                            bank, free, done = vbanks.fill()
                            pe.wait_ge(free.sem, free.due(pe))
                            for n in range(2):
                                last = pe.matmul(bank[:, n * T:n * T + T], KTT[c][:, h + n, :], GV[:, t, (h + n) * T:(h + n) * T + T], start=True, stop=True)
                            last.then_inc(done, 1)
                pe.wait_ge(gla_states.sem, gla_states.due(pe))
                for h in range(0, 4, 2):
                    bank, free, done = vbanks.fill()
                    pe.wait_ge(free.sem, free.due(pe))
                    for n in range(4):
                        hh, v = h + n // 2, n % 2
                        o = bank[:, n * P:n * P + P]
                        last = pe.matmul(o, GV[:, t, hh * T + v * P:hh * T + v * P + P], AT[:, hh, :], start=True, stop=False)
                        for c in range(2):
                            g = 2 * t + c
                            if g:
                                last = pe.matmul(o[:, c * CH:c * CH + CH], GS[g][:, hh, v * P:v * P + P],
                                                 GX[:, hh, g * CH:g * CH + CH], start=False, stop=c == 1)
                    last.then_inc(done, 1)
            sums_pe(SQG, 2, 4)
            multiply(j["gc"])
            pe.wait_ge(normed.sem, normed.due(pe))
            pe.wait_ge(branch_ready.sem, branch_ready.due(pe))
            multiply(j["go"])

        @block.tensor
        def _(_pe):
            take_in_pe()
            sums_pe(XC, DK)
            pe.wait_ge(normed.sem, normed.due(pe))
            for j in (rec_dt, rec_x, rec_xbc):
                multiply(j)
            lru_pe()
            multiply(rec_gate)
            multiply(rec_z[0])
            ssd_pe()
            sums_pe(UU, 4, 2)
            pe.wait_ge(normed.sem, normed.due(pe))
            multiply(rec_out)
            ffn_pe(0)
            pe.wait_ge(second_rows_landed.sem, second_rows_landed.due(pe, 16 * len(second_vectors)))
            turn_pe([PACK2[:, i, :] for i in range(PACKS - FIRST_PACKS)], vbanks)
            att_pe()
            modulation_pe()
            ffn_pe(1)
            modulation_pe()
            for l in range(2):
                j = second[l]
                sums_pe(SQM, DK)
                pe.wait_ge(normed.sem, normed.due(pe))
                mla_pe(j)
                rwkv_pe(j)
                gla_pe(j)
                pe.wait_ge(merge_ready.sem, merge_ready.due(pe))
                multiply(j["out"])
                sums_pe(SQM, DK)
            for k in range(0, DK, 2):
                pe.wait_ge(x_ready.sem, (DK + k) // 2 + 1)
                turn_pe([X[:, k + n, t * P:t * P + P] for t in range(TT) for n in range(2)], abanks)

        def conv_v(src, nt, w, b, dst, by):
            for k in range(nt):
                dve.tensor_scalar(dst[:, k, :], src[:, k, 0:T], col(w, k), col(b, k), ALU.mult, ALU.add)\
                   .then_inc(vector_step.sem, 1)
                dve.wait_ge(vector_step.sem, vector_step.due(dve))
                for n in range(1, 4):
                    sig = by if (k, n) == (nt - 1, 3) else vector_step
                    dve.scalar_tensor_tensor(dst[:, k, :], src[:, k, n:n + T], col(w, n * nt + k),
                        dst[:, k, :], ALU.mult, ALU.add)\
                       .then_inc(sig.sem, 1)
                    dve.wait_ge(sig.sem, sig.due(dve))

        def halves_v(dst, bank, free):
            b = bank.rearrange("p (k e t) -> p k e t", k=2, e=2)
            dve.tensor_copy(dst[0:64], b[0:64, :, 0, :])\
               .then_inc(vector_step.sem, 1)
            dve.wait_ge(vector_step.sem, vector_step.due(dve))
            dve.tensor_copy(dst[64:128], b[64:128, :, 1, :])\
               .then_inc(free.sem, 1)
            dve.wait_ge(free.sem, free.due(dve))

        def take_in_v():
            dve.memset(flat(PACK), 0.0)\
               .then_inc(packs_zeroed.sem, 1)
            dve.wait_ge(packs_zeroed.sem, packs_zeroed.due(dve))
            dve.memset(biases[:, 0:1], EPS)\
               .then_inc(vector_step.sem, 1)
            dve.wait_ge(vector_step.sem, vector_step.due(dve))
            dve.memset(biases[:, 1:2], GN_EPS)\
               .then_inc(vector_step.sem, 1)
            dve.wait_ge(vector_step.sem, vector_step.due(dve))
            dve.memset(biases[:, 2:3], 1.0)\
               .then_inc(biases_set.sem, 1)
            dve.wait_ge(biases_set.sem, biases_set.due(dve))
            bank, full, free = vbanks.empty()
            dve.wait_ge(full.sem, full.due(dve))
            dve.tensor_copy(cols[:, 0:FIRST_PACKS * P], bank[:, 0:FIRST_PACKS * P])\
               .then_inc(free.sem, 1)
            dve.wait_ge(free.sem, free.due(dve))
            for k in range(0, DK, 2):
                bank, full, free = vbanks.empty()
                dve.wait_ge(full.sem, full.due(dve))
                dve.tensor_copy(flat(X[:, k:k + 2, :]), bank)\
                   .then_inc(free.sem, 1)
                dve.wait_ge(free.sem, free.due(dve))
            dve.memset(flat(BD.rearrange("p a b c -> p (a b) c")), 0.0)\
               .then_inc(lru_weights_zeroed.sem, 1)
            dve.wait_ge(lru_weights_zeroed.sem, lru_weights_zeroed.due(dve))
            dve.memset(LX[:, :, 0:3], 0.0)\
               .then_inc(vector_step.sem, 1)
            dve.wait_ge(vector_step.sem, vector_step.due(dve))
            dve.memset(XB[:, :, 0:3], 0.0)\
               .then_inc(conv_fronts_zeroed.sem, 1)
            dve.wait_ge(conv_fronts_zeroed.sem, conv_fronts_zeroed.due(dve))

        def rec_v():
            norm_v(X, XC, DK, lambda k: col("rec_norm", k), H)
            dve.tensor_scalar(LAMX, col("lru_lambda", 0, 8), -1.0, None, ALU.mult)\
               .then_inc(vector_step.sem, 1)
            dve.wait_ge(vector_step.sem, vector_step.due(dve))
            softplus_v(LAMX, LAMA, LAMB, LAMC, LAMD)
            dve.tensor_scalar(LAMD, LAMD, 8.0, None, ALU.mult)\
               .then_inc(vector_step.sem, 1)
            dve.wait_ge(vector_step.sem, vector_step.due(dve))
            dve.wait_ge(rows_landed.sem, rows_landed.due(dve, 48))
            dve.wait_ge(evicted[0].sem, halves(0, rec_dt))
            dve.wait_ge(evicted[1].sem, halves(1, rec_dt))
            dve.tensor_tensor(DT, DT, over(AROW[:, 0, :], TT, 16), ALU.add)\
               .then_inc(vector_step.sem, 1)
            dve.wait_ge(vector_step.sem, vector_step.due(dve))
            softplus_v(flat(DT), flat(DTB), flat(DTC), flat(DTD), flat(DT))
            dve.wait_ge(a_exp.sem, a_exp.due(dve))
            dve.scalar_tensor_tensor(DTB, DT, -1.0, over(AROW[:, 1, :], TT, 16), ALU.mult, ALU.mult)\
               .then_inc(vector_step.sem, 1)
            dve.wait_ge(vector_step.sem, vector_step.due(dve))
            dve.tensor_scalar(DCOL, AROW[:, 2, 0:16:2], half[:, 0:1], None, ALU.mult)\
               .then_inc(vector_step.sem, 1)
            dve.wait_ge(vector_step.sem, vector_step.due(dve))
            dve.scalar_tensor_tensor(DCOL, AROW[:, 2, 1:16:2], half[:, 1:2], DCOL, ALU.mult, ALU.add)\
               .then_inc(vector_step.sem, 1)
            dve.wait_ge(vector_step.sem, vector_step.due(dve))
            dve.wait_ge(evicted[0].sem, halves(0, rec_x))
            dve.wait_ge(evicted[1].sem, halves(1, rec_x))
            conv_v(LX, DK, "lru_conv_w", "lru_conv_b", XC, lru_conv_done)
            dve.wait_ge(lru_gates.sem, lru_gates.due(dve))
            dve.tensor_tensor(RG, RG, along(LAMD, DK, T), ALU.mult)\
               .then_inc(rate_ready.sem, 1)
            dve.wait_ge(rate_ready.sem, rate_ready.due(dve))
            dve.tensor_tensor(IG, IG, XC, ALU.mult)\
               .then_inc(vector_step.sem, 1)
            dve.wait_ge(vector_step.sem, vector_step.due(dve))
            dve.wait_ge(lru_functions.sem, lru_functions.due(dve))
            dve.tensor_tensor(UU, LRU_A, LRU_A, ALU.mult)\
               .then_inc(vector_step.sem, 1)
            dve.wait_ge(vector_step.sem, vector_step.due(dve))
            dve.scalar_tensor_tensor(flat(UU), flat(UU), 1.0, flat(RG), ALU.add, ALU.mult)\
               .then_inc(lru_root_in.sem, 1)
            dve.wait_ge(lru_root_in.sem, lru_root_in.due(dve))
            dve.wait_ge(evicted[0].sem, halves(0, rec_xbc))
            dve.wait_ge(evicted[1].sem, halves(1, rec_xbc))
            conv_v(XB, 12, "ssd_conv_w", "ssd_conv_b", XBC, ssd_conv_done)
            dve.wait_ge(lru_root.sem, lru_root.due(dve))
            dve.tensor_tensor(UU, UU, IG, ALU.mult)\
               .then_inc(vector_step.sem, 1)
            dve.wait_ge(vector_step.sem, vector_step.due(dve))
            for k in range(DK):
                dve.tensor_tensor_scan(RG[:, k, :], LRU_A[:, k, :], UU[:, k, :], 0.0, ALU.mult, ALU.add)\
                   .then_inc(vector_step.sem, 1)
                dve.wait_ge(vector_step.sem, vector_step.due(dve))
            dve.wait_ge(evicted[0].sem, halves(0, rec_gate))
            dve.wait_ge(evicted[1].sem, halves(1, rec_gate))
            dve.tensor_tensor(MIX[:, 0:DK, :], RG, G, ALU.mult)\
               .then_inc(vector_step.sem, 1)
            dve.wait_ge(vector_step.sem, vector_step.due(dve))
            ssd_v()
            dve.wait_ge(evicted[0].sem, halves(0, rec_z[2]))
            dve.wait_ge(evicted[1].sem, halves(1, rec_z[2]))
            dve.tensor_tensor(G, G, Z, ALU.mult)\
               .then_inc(vector_step.sem, 1)
            dve.wait_ge(vector_step.sem, vector_step.due(dve))
            norm_v(G, UU, 4, lambda k: col("ssd_norm", k), MIX[:, 8:16, :], 2)
            evict(dve, rec_out, add_to_x)

        def ssd_v():
            for t in range(TT):
                here = slice(t * P, t * P + P)
                dve.tensor_tensor(ADTRI, along(DTB[:, t, :], 16, P), over(tri, 16, P), ALU.mult)\
                   .then_inc(decay_steps.sem, 1)
                dve.wait_ge(decay_steps.sem, decay_steps.due(dve))
                bank, full, free = vbanks.empty()
                dve.wait_ge(full.sem, full.due(dve))
                dve.tensor_copy(CS[:, t, :], bank[:, 0:16])\
                   .then_inc(free.sem, 1)
                dve.wait_ge(free.sem, free.due(dve))
                for h in range(0, 16, 4):
                    bank, full, free = vbanks.empty()
                    dve.wait_ge(full.sem, full.due(dve))
                    b = bank.rearrange("p (h l) -> p h l", h=4)
                    if t == 0:
                        dve.tensor_copy(LAST[:, h:h + 4], b[:, :, P - 1])\
                           .then_inc(vector_step.sem, 1)
                        dve.wait_ge(vector_step.sem, vector_step.due(dve))
                    else:
                        dve.tensor_copy(ECS[:, h:h + 4, :], b)\
                           .then_inc(vector_step.sem, 1)
                        dve.wait_ge(vector_step.sem, vector_step.due(dve))
                    for n in range(4):
                        sig = free if n == 3 else vector_step
                        dve.tensor_scalar(SEG[:, h + n, :], b[:, n, :], CS[:, t, h + n:h + n + 1], 0.0,
                            ALU.subtract, ALU.min)\
                           .then_inc(sig.sem, 1)
                        dve.wait_ge(sig.sem, sig.due(dve))
                if t == 0:
                    dve.tensor_tensor(LAST, LAST, CS[:, 0, :], ALU.subtract)\
                       .then_inc(vector_step.sem, 1)
                    dve.wait_ge(vector_step.sem, vector_step.due(dve))
                dve.nop().then_inc(decay_in.sem, 1)
                bank, full, free = vbanks.empty()
                dve.wait_ge(full.sem, full.due(dve))
                dve.tensor_tensor(CBM, bank[:, 0:2 * P].rearrange("p (g l) -> p g l", g=2), over(tri, 2,
                    P), ALU.mult)\
                   .then_inc(free.sem, 1)
                dve.wait_ge(free.sem, free.due(dve))
                for k in range(0, DK, 4):
                    bank, full, free = vbanks.empty()
                    dve.wait_ge(full.sem, full.due(dve))
                    dve.tensor_tensor(XTOK[:, t, k * P:k * P + 512].rearrange("p (h c) -> p h c", h=8),
                        bank.rearrange("p (h c) -> p h c", h=8), along(DT[:, t, 2 * k:2 * k + 8], 8, 64), ALU.mult)\
                       .then_inc(free.sem, 1)
                    dve.wait_ge(free.sem, free.due(dve))
                dve.wait_ge(decay_out.sem, decay_out.due(dve))
                if t == 0:
                    bank, full, free = vbanks.empty()
                    dve.wait_ge(full.sem, full.due(dve))
                    dve.tensor_copy(flat(BTOK), bank[:, 0:2 * P])\
                       .then_inc(free.sem, 1)
                    dve.wait_ge(free.sem, free.due(dve))
                    dve.tensor_tensor(XDTE.rearrange("p (h c) -> p h c", h=16), XTOK[:, 0,
                        :].rearrange("p (h c) -> p h c", h=16), along(LAST, 16, 64), ALU.mult)\
                       .then_inc(state_operand.sem, 1)
                    dve.wait_ge(state_operand.sem, state_operand.due(dve))
                    for g in range(2):
                        bank, full, free = vbanks.empty()
                        dve.wait_ge(full.sem, full.due(dve))
                        dve.tensor_copy(PREV[:, g, :], bank)\
                           .then_inc(free.sem, 1)
                        dve.wait_ge(free.sem, free.due(dve))
                else:
                    for g in range(2):
                        dve.tensor_tensor(ECS[:, 8 * g:8 * g + 8, :], ECS[:, 8 * g:8 * g + 8, :],
                            over(XBC[:, 10 + g, here], 8, P), ALU.mult)\
                           .then_inc(vector_step.sem, 1)
                        dve.wait_ge(vector_step.sem, vector_step.due(dve))
                for g in range(2):
                    sig = ssd_operand if g else vector_step
                    dve.tensor_tensor(SEG[:, 8 * g:8 * g + 8, :], SEG[:, 8 * g:8 * g + 8, :],
                        over(CBM[:, g, :], 8, P), ALU.mult)\
                       .then_inc(sig.sem, 1)
                    dve.wait_ge(sig.sem, sig.due(dve))
                for k in range(0, DK, 2):
                    bank, full, free = vbanks.empty()
                    dve.wait_ge(full.sem, full.due(dve))
                    halves_v(G[:, k:k + 2, here], bank, free)
            for k in range(DK):
                dve.scalar_tensor_tensor(G[:, k, :], XBC[:, k, :], DCOL[:, k:k + 1], G[:, k, :],
                    ALU.mult, ALU.add)\
                   .then_inc(vector_step.sem, 1)
                dve.wait_ge(vector_step.sem, vector_step.due(dve))

        def ffn_v(l):
            dve.wait_ge(evicted[0].sem, halves(0, rec_out if l == 0 else att_out))
            dve.wait_ge(evicted[1].sem, halves(1, rec_out if l == 0 else att_out))
            up, down, turns = ffn_up[l].at // 2, ffn_down[l].at // 2, turns_before[l]

            def split_weights(s, turn):
                dve.wait_ge(landed[s].sem, turn * 16 + (landed_before(ffn_up[l], s) + 16))
                dve.tensor_copy(UP_W[s][0], WHOLE_W[s][:, 0:DK, :])\
                   .then_inc(hi_ready[s].sem, 1)
                dve.wait_ge(hi_ready[s].sem, turn + (turns + 1))
                dve.tensor_tensor(UP_W[s][1], WHOLE_W[s][:, 0:DK, :], UP_W[s][0].bitcast(F32), ALU.subtract)\
                   .then_inc(lo_ready[s].sem, 1)

            squares_v(X, SQF, DK)
            split_weights(0, 0)
            dve.wait_ge(rms_ready.sem, rms_ready.due(dve))
            for k in range(DK):
                dve.scalar_tensor_tensor(H[:, k, :], X[:, k, :], col("ffn_norm", 8 * l + k), STAT[:, 0, :], ALU.mult, ALU.mult)\
                   .then_inc(h_ready.sem, 1)
            dve.wait_ge(h_ready.sem, h_ready.due(dve, DK))
            for k in range(0, DK, 4):
                sig = normed if k else vector_step
                dve.wait_ge(h_hi_ready.sem, h_hi_ready.due(dve))
                dve.tensor_tensor(H_PARTS[1][:, k:k + 4, :], H[:, k:k + 4, :], H_PARTS[0][:, k:k + 4, :].bitcast(F32), ALU.subtract)\
                   .then_inc(sig.sem, 1)
                dve.wait_ge(sig.sem, sig.due(dve))
            split_weights(1, 0)

            def up_turn(j, more):
                dve.wait_ge(product[0].sem, j + (up + 1))
                if more:
                    split_weights(0, j + 1)
                dve.wait_ge(product[1].sem, j + (up + 1))
                dve.wait_ge(evicted[0].sem, j + (up + 1))
                dve.tensor_tensor(hidden, psum[1].rearrange("p (a b) -> p a b", a=2), silu_g, ALU.mult)\
                   .then_inc(evicted[1].sem, 1)
                if more:
                    split_weights(1, j + 1)
                dve.wait_ge(evicted[1].sem, j + (up + 1))
                dve.tensor_copy(two(HIDDEN_PARTS[0], j), hidden)\
                   .then_inc(hidden_hi_ready.sem, 1)
                dve.wait_ge(hidden_hi_ready.sem, j + (UPS * l + 1))
                dve.tensor_tensor(two(HIDDEN_PARTS[1], j), hidden, two(HIDDEN_PARTS[0], j).bitcast(F32), ALU.subtract)\
                   .then_inc(hidden_ready.sem, 1)
                dve.wait_ge(hidden_ready.sem, j + (UPS * l + 1))

            with dve.Fori(0, UPS - 1) as j:
                up_turn(j, True)
            up_turn(UPS - 1, False)

            def down_low_parts(j, q):
                for h in range(2):
                    dve.wait_ge(hi_ready[h].sem, j * 2 + (turns + UPS + q + 1))
                    dve.tensor_tensor(DOWN_W[h][1], WHOLE_W[q][:, h * UPS:h * UPS + UPS, 0:P], DOWN_W[h][0].bitcast(F32), ALU.subtract)\
                       .then_inc(lo_ready[h].sem, 1)

            def down_add(j, q):
                dve.wait_ge(product[q].sem, j + (down + 1))
                tile = X[:, 2 * j + q, :] if isinstance(j, int) else X[:, bass.ds(j * 2 + q, 1), :].rearrange("p a b -> p (a b)")
                dve.tensor_tensor(tile, psum[q][:, 0:T], tile, ALU.add)\
                   .then_inc(evicted[q].sem, 1)

            down_low_parts(0, 0)
            with dve.Fori(0, DK // 2 - 1) as j:
                down_low_parts(j, 1)
                down_add(j, 0)
                down_low_parts(j + 1, 0)
                down_add(j, 1)
            down_low_parts(DK // 2 - 1, 1)
            down_add(DK // 2 - 1, 0)
            down_add(DK // 2 - 1, 1)

        def ffn_act(l):
            up, down, turns = ffn_up[l].at // 2, ffn_down[l].at // 2, turns_before[l]

            rms_act(D)
            for k in range(0, DK, 4):
                act.wait_ge(h_ready.sem, h_ready.due(act, 4))
                act.activation(H_PARTS[0][:, k:k + 4, :], H[:, k:k + 4, :], ACT.Copy)\
                   .then_inc(h_hi_ready.sem, 1)

            with act.Fori(0, UPS) as j:
                act.wait_ge(product[0].sem, j + (up + 1))
                act.wait_ge(evicted[1].sem, j + up)
                act.activation(silu_g, psum[0].rearrange("p (a b) -> p a b", a=2), ACT.Silu)\
                   .then_inc(evicted[0].sem, 1)

            def down_high_parts(j, q, first=False):
                act.wait_ge(landed[q].sem, j * 16 + (landed_before(ffn_down[l], q) + 16))
                for h in range(2):
                    if first:
                        act.wait_ge(product[h].sem, up + UPS)
                    elif h == 0:
                        act.wait_ge(first_part_used.sem, j * 2 + (DK * l + q))
                    elif q == 1:
                        act.wait_ge(product[0].sem, j + (down + 1))
                    else:
                        act.wait_ge(product[1].sem, j + down)
                    act.activation(DOWN_W[h][0], WHOLE_W[q][:, h * UPS:h * UPS + UPS, 0:P], ACT.Copy)\
                       .then_inc(hi_ready[h].sem, 1)

            down_high_parts(0, 0, True)
            down_high_parts(0, 1)
            with act.Fori(1, DK // 2) as j:
                for q in range(2):
                    down_high_parts(j, q)

        def attention_v():
            dve.wait_ge(evicted[0].sem, halves(0, ffn_down[0]))
            dve.wait_ge(evicted[1].sem, halves(1, ffn_down[0]))
            norm_v(X, SQA, DK, lambda k: col("att_norm", k), H)
            for x, job, gain in ((Q, att_q, "att_q_norm"), (K, att_k, "att_k_norm")):
                dve.wait_ge(evicted[0].sem, halves(0, job))
                dve.wait_ge(evicted[1].sem, halves(1, job))
                dve.tensor_tensor(SQA, x, x, ALU.mult)\
                   .then_inc(head_squares.sem, 1)
                dve.wait_ge(head_squares.sem, head_squares.due(dve))
                dve.wait_ge(head_rms.sem, head_rms.due(dve))
                dve.scalar_tensor_tensor(flat(x), flat(x), col(gain), flat(RS), ALU.mult, ALU.mult)\
                   .then_inc(head_normed.sem, 1)
                dve.wait_ge(head_normed.sem, head_normed.due(dve))
                dve.tensor_tensor(SQA, x, over(const("att_cos"), DK, T), ALU.mult)\
                   .then_inc(vector_step.sem, 1)
                dve.wait_ge(vector_step.sem, vector_step.due(dve))
                for k in range(0, DK, 2):
                    bank, full, free = vbanks.empty()
                    dve.wait_ge(full.sem, full.due(dve))
                    dve.tensor_tensor(ROT[:, k:k + 2, :], bank.rearrange("p (a b) -> p a b", a=2),
                        over(const("att_sin"), 2, T), ALU.mult)\
                       .then_inc(free.sem, 1)
                    dve.wait_ge(free.sem, free.due(dve))
                dve.tensor_tensor(x, SQA, ROT, ALU.add)\
                   .then_inc(vector_step.sem, 1)
                dve.wait_ge(vector_step.sem, vector_step.due(dve))
            kp = KP.rearrange("p (k e) t -> p k e t", e=2)
            for e in range(2):
                sig = keys_ready if e else vector_step
                dve.tensor_scalar(kp[:, :, e, :], K, half[:, e:e + 1], None, ALU.mult)\
                   .then_inc(sig.sem, 1)
                dve.wait_ge(sig.sem, sig.due(dve))

            def take(h, bank, free):
                at = slice(64 * (h % 2), 64 * (h % 2) + 64)
                dve.tensor_copy(O[at, h // 2, :], bank[at])\
                   .then_inc(free.sem, 1)
                dve.wait_ge(free.sem, free.due(dve))

            attend_v(16, 64 ** -0.5, const("windows"), SC, PR, MX, SM, take)
            dve.nop().then_inc(heads_out.sem, 1)
            evict(dve, att_out, add_to_x)

        def reduce_angle_v(src, dst, k, tmp):
            magic = float(3 << 22)
            dve.tensor_scalar(k, src, 0.15915494309189535, magic, ALU.mult, ALU.add)\
               .then_inc(vector_step.sem, 1)
            dve.wait_ge(vector_step.sem, vector_step.due(dve))
            dve.tensor_scalar(k, k, magic, None, ALU.subtract)\
               .then_inc(vector_step.sem, 1)
            dve.wait_ge(vector_step.sem, vector_step.due(dve))
            dve.scalar_tensor_tensor(dst, k, -6.28125, src, ALU.mult, ALU.add)\
               .then_inc(vector_step.sem, 1)
            dve.wait_ge(vector_step.sem, vector_step.due(dve))
            dve.scalar_tensor_tensor(dst, k, -0.0019350051879882812, dst, ALU.mult, ALU.add)\
               .then_inc(vector_step.sem, 1)
            dve.wait_ge(vector_step.sem, vector_step.due(dve))
            dve.scalar_tensor_tensor(dst, k, -3.0199159819e-07, dst, ALU.mult, ALU.add)\
               .then_inc(vector_step.sem, 1)
            dve.wait_ge(vector_step.sem, vector_step.due(dve))
            dve.tensor_scalar(dst, dst, 3.1415925, -3.1415925, ALU.min, ALU.max)\
               .then_inc(vector_step.sem, 1)
            dve.wait_ge(vector_step.sem, vector_step.due(dve))

        def angles_v():
            dve.wait_ge(positions_landed.sem, positions_landed.due(dve, 16))
            dve.tensor_copy(ANG[:, 0, :], ANG[:, 3, :].bitcast(I32))\
               .then_inc(vector_step.sem, 1)
            dve.wait_ge(vector_step.sem, vector_step.due(dve))
            dve.tensor_scalar(ANG[:, 0, :], ANG[:, 0, :], const("mla_freq"), None, ALU.mult)\
               .then_inc(vector_step.sem, 1)
            dve.wait_ge(vector_step.sem, vector_step.due(dve))
            reduce_angle_v(ANG[:, 0, :], ANG[:, 1, :], ANG[:, 2, :], None)
            dve.tensor_scalar(ANG[:, 2, :], ANG[:, 1, :], 1.5707963267948966, None, ALU.add)\
               .then_inc(vector_step.sem, 1)
            dve.wait_ge(vector_step.sem, vector_step.due(dve))
            dve.tensor_scalar(ANG[:, 3, :], ANG[:, 2, :], 3.1415927, -6.283185307179586, ALU.is_gt,
                ALU.mult)\
               .then_inc(vector_step.sem, 1)
            dve.wait_ge(vector_step.sem, vector_step.due(dve))
            dve.tensor_tensor(ANG[:, 2, :], ANG[:, 2, :], ANG[:, 3, :], ALU.add)\
               .then_inc(vector_step.sem, 1)
            dve.wait_ge(vector_step.sem, vector_step.due(dve))
            dve.tensor_scalar(ANG[:, 2, :], ANG[:, 2, :], 3.1415925, -3.1415925, ALU.min, ALU.max)\
               .then_inc(angles_ready.sem, 1)
            dve.wait_ge(angles_ready.sem, angles_ready.due(dve))
            dve.wait_ge(tables_ready.sem, tables_ready.due(dve))

        def merge_v(job, tmp, base):
            def body(i, s, rounds, turn):
                dve.wait_ge(product[s].sem, rounds + 1)
                dve.tensor_tensor(tmp[s], psum[s].rearrange("p (a b) -> p a b", a=2), two(GT, i), ALU.mult)\
                   .then_inc(evicted[s].sem, 1)
                dve.wait_ge(evicted[s].sem, rounds + 1)
                dve.tensor_tensor(two(M, i), two(M, i), tmp[s], ALU.add).then_inc(merged.sem, 1)
                dve.wait_ge(merged.sem, turn * 2 + (base + s + 1))

            job.each(dve, body)

        def mla_v(j, l):
            n2 = lambda n: f"{n}_2/{l}"
            dve.wait_ge(evicted[0].sem, halves(0, j["cq"]))
            dve.wait_ge(evicted[1].sem, halves(1, j["cq"]))
            squares_v(CQ, SQM[:, 0:4], 4)
            dve.wait_ge(evicted[0].sem, halves(0, j["kr"]))
            dve.wait_ge(evicted[1].sem, halves(1, j["kr"]))
            squares_v(CKV, SQM[:, 4:6], 2)
            for x, nt, row, gain in ((CQ, 4, 0, "mla_q_norm"), (CKV, 2, 1, "mla_kv_norm")):
                dve.wait_ge(rms_ready.sem, rms_ready.due(dve))
                for k in range(nt):
                    by = vector_step if k < nt - 1 else normed
                    dve.scalar_tensor_tensor(x[:, k, :], x[:, k, :], col(n2(gain), k), STAT[:, row, :], ALU.mult, ALU.mult)\
                       .then_inc(by.sem, 1)
                    dve.wait_ge(by.sem, by.due(dve))
            if l == 0:
                angles_v()
            for x, nt in ((KR, 1), (QR, 4)):
                if x is QR:
                    dve.wait_ge(evicted[0].sem, halves(0, j["uqr"]))
                    dve.wait_ge(evicted[1].sem, halves(1, j["uqr"]))
                for k in range(0, nt, 2):
                    bank, full, free = vbanks.empty()
                    dve.wait_ge(full.sem, full.due(dve))
                    n = min(2, nt - k)
                    dve.tensor_tensor(ROTM[:, k:k + n, :], bank[:,
                        0:n * T].rearrange("p (a b) -> p a b", a=n), over(SIN, n, T), ALU.mult)\
                       .then_inc(free.sem, 1)
                    dve.wait_ge(free.sem, free.due(dve))
                dve.tensor_tensor(x, x, over(COS, nt, T), ALU.mult)\
                   .then_inc(vector_step.sem, 1)
                dve.wait_ge(vector_step.sem, vector_step.due(dve))
                sig = keys_ready if x is QR else vector_step
                dve.tensor_tensor(x, x, ROTM[:, 0:nt, :], ALU.add)\
                   .then_inc(sig.sem, 1)
                dve.wait_ge(sig.sem, sig.due(dve))
                if x is KR:
                    for e in range(2):
                        dve.tensor_scalar(KRP[:, e, :], KR[:, 0, :], half[:, e:e + 1], None, ALU.mult)\
                           .then_inc(vector_step.sem, 1)
                        dve.wait_ge(vector_step.sem, vector_step.due(dve))
            dve.wait_ge(evicted[0].sem, halves(0, j["mz"]))
            dve.wait_ge(evicted[1].sem, halves(1, j["mz"]))

            def take(h, bank, free):
                dve.tensor_tensor(OM[:, h, :], bank, ZM[:, h, :], ALU.mult)\
                   .then_inc(free.sem, 1)
                dve.wait_ge(free.sem, free.due(dve))

            attend_v(8, 192 ** -0.5, const("chunks"), MSC, MPR, MMX, MSM, take)
            dve.nop().then_inc(heads_out.sem, 1)
            dve.wait_ge(evicted[0].sem, halves(0, j["ga"]))
            dve.wait_ge(evicted[1].sem, halves(1, j["ga"]))
            evict(dve, j["mo"], lambda i, bank, done, rounds:
                  dve.tensor_tensor(two(M, i), bank, two(GT, i), ALU.mult).then_inc(done, 1))

        def mix_v(src, dst, nt, mu, l):
            dve.tensor_tensor(dst, src[:, :, 0:T], src[:, :, 1:T + 1], ALU.subtract)\
               .then_inc(vector_step.sem, 1)
            dve.wait_ge(vector_step.sem, vector_step.due(dve))
            for k in range(nt):
                dve.scalar_tensor_tensor(dst[:, k, :], dst[:, k, :], col(f"rwkv_mu_2/{l}", mu + k),
                    src[:, k, 1:T + 1], ALU.mult, ALU.add)\
                   .then_inc(vector_step.sem, 1)
                dve.wait_ge(vector_step.sem, vector_step.due(dve))

        KAPPA = float(np.exp(np.float64(-0.5)))

        def rwkv_v(j, l):
            n2 = lambda n: f"{n}_2/{l}"
            dve.wait_ge(evicted[0].sem, halves(0, j["gl"]))
            dve.wait_ge(evicted[1].sem, halves(1, j["gl"]))
            dve.wait_ge(evicted[0].sem, halves(0, j["mo"]))
            dve.wait_ge(evicted[1].sem, halves(1, j["mo"]))
            for x in raw:
                sig = fronts_zeroed if x is raw[2] else vector_step
                dve.memset(x[:, :, 0:1], 0.0)\
                   .then_inc(sig.sem, 1)
                dve.wait_ge(sig.sem, sig.due(dve))
            dve.memset(flat(W2), 0.0)\
               .then_inc(lora_zeroed.sem, 1)
            dve.wait_ge(lora_zeroed.sem, lora_zeroed.due(dve))
            wl = WL.rearrange("p (a b) -> p a b", a=1)
            sq1 = SQR[:, 0:1, :]
            dve.tensor_tensor(sq1, wl[:, :, 0:T], wl[:, :, 1:T + 1], ALU.subtract)\
               .then_inc(vector_step.sem, 1)
            dve.wait_ge(vector_step.sem, vector_step.due(dve))
            dve.scalar_tensor_tensor(sq1[:, 0, :], sq1[:, 0, :], col(n2("rwkv_mu"), 24), WL[:, 1:T + 1],
                ALU.mult, ALU.add)\
               .then_inc(vector_step.sem, 1)
            dve.wait_ge(vector_step.sem, vector_step.due(dve))
            dve.tensor_copy(WL[:, 1:T + 1], sq1[:, 0, :])\
               .then_inc(lora_mixed.sem, 1)
            dve.wait_ge(lora_mixed.sem, lora_mixed.due(dve))
            dve.wait_ge(evicted[0].sem, halves(0, j["k"]))
            dve.wait_ge(evicted[1].sem, halves(1, j["k"]))
            mix_v(raw[0], KR_, DK, 8, l)
            dve.tensor_tensor(KKD, KR_, along(col(n2("rwkv_k_k"), 0, 8), DK, T), ALU.mult)\
               .then_inc(vector_step.sem, 1)
            dve.wait_ge(vector_step.sem, vector_step.due(dve))
            dve.tensor_tensor(SQR, KKD, KKD, ALU.mult)\
               .then_inc(head_squares.sem, 1)
            dve.wait_ge(head_squares.sem, head_squares.due(dve))
            dve.wait_ge(lora_gates.sem, lora_gates.due(dve))
            for k in range(DK):
                dve.tensor_tensor_scan(CC[:, k, :], const("run"), SW[:, k, :], 0.0, ALU.mult, ALU.add)\
                   .then_inc(vector_step.sem, 1)
                dve.wait_ge(vector_step.sem, vector_step.due(dve))
            dve.tensor_tensor(SW, CC, SW, ALU.subtract)\
               .then_inc(cumulated.sem, 1)
            dve.wait_ge(cumulated.sem, cumulated.due(dve))
            dve.tensor_scalar(KAI, col(n2("rwkv_k_a"), 0, 8), -1.0, 1.0, ALU.mult, ALU.add)\
               .then_inc(vector_step.sem, 1)
            dve.wait_ge(vector_step.sem, vector_step.due(dve))
            for k in range(DK):
                dve.tensor_scalar(KFACTOR[:, k, :], AA[:, k, :], col(n2("rwkv_k_a"), k), KAI[:, k:k + 1],
                    ALU.mult, ALU.add)\
                   .then_inc(vector_step.sem, 1)
                kfactors = vector_step.due(dve)
            dve.wait_ge(vector_step.sem, kfactors)
            dve.tensor_tensor(KR_, KR_, KFACTOR, ALU.mult)\
               .then_inc(vector_step.sem, 1)
            dve.wait_ge(vector_step.sem, vector_step.due(dve))
            dve.wait_ge(head_rms.sem, head_rms.due(dve))
            dve.tensor_scalar(SQR, SQR, 1e-12, None, ALU.max)\
               .then_inc(vector_step.sem, 1)
            dve.wait_ge(vector_step.sem, vector_step.due(dve))
            dve.reciprocal(SQR, SQR)\
               .then_inc(vector_step.sem, 1)
            dve.wait_ge(vector_step.sem, vector_step.due(dve))
            dve.tensor_tensor(KKD, KKD, SQR, ALU.mult)\
               .then_inc(vector_step.sem, 1)
            dve.wait_ge(vector_step.sem, vector_step.due(dve))
            dve.wait_ge(evicted[0].sem, halves(0, j["r"]))
            dve.wait_ge(evicted[1].sem, halves(1, j["r"]))
            mix_v(raw[1], R, DK, 0, l)
            dve.tensor_tensor(BDF, KKD, AA, ALU.mult)\
               .then_inc(vector_step.sem, 1)
            dve.wait_ge(vector_step.sem, vector_step.due(dve))
            dve.tensor_tensor(SQR, R, KR_, ALU.mult)\
               .then_inc(vector_step.sem, 1)
            dve.wait_ge(vector_step.sem, vector_step.due(dve))
            dve.tensor_tensor(SQR, SQR, along(col(n2("rwkv_r_k"), 0, 8), DK, T), ALU.mult)\
               .then_inc(head_squares.sem, 1)
            dve.wait_ge(head_squares.sem, head_squares.due(dve))
            dve.wait_ge(evicted[0].sem, halves(0, j["v"]))
            dve.wait_ge(evicted[1].sem, halves(1, j["v"]))
            mix_v(raw[2], V_, DK, 16, l)
            for k in range(0, DK, 2):
                bank, full, free = vbanks.empty()
                dve.wait_ge(full.sem, full.due(dve))
                dve.tensor_tensor(BONUS[:, k:k + 2, :], bank.rearrange("p (a b) -> p a b", a=2), V_[:,
                    k:k + 2, :], ALU.mult)\
                   .then_inc(free.sem, 1)
                dve.wait_ge(free.sem, free.due(dve))
            dve.wait_ge(decays.sem, decays.due(dve))
            dve.tensor_tensor(R, R, E1, ALU.mult)\
               .then_inc(vector_step.sem, 1)
            dve.wait_ge(vector_step.sem, vector_step.due(dve))
            dve.tensor_tensor(KKD, KKD, SW, ALU.mult)\
               .then_inc(vector_step.sem, 1)
            dve.wait_ge(vector_step.sem, vector_step.due(dve))
            dve.tensor_tensor(BDF, BDF, E2, ALU.mult)\
               .then_inc(vector_step.sem, 1)
            dve.wait_ge(vector_step.sem, vector_step.due(dve))
            dve.tensor_tensor(KR_, KR_, E2, ALU.mult)\
               .then_inc(vector_step.sem, 1)
            dve.wait_ge(vector_step.sem, vector_step.due(dve))
            dve.tensor_copy(ECEND, E1.rearrange("p k (c t) -> p k c t", t=CH)[:, :, :, CH - 1])\
               .then_inc(vector_step.sem, 1)
            dve.wait_ge(vector_step.sem, vector_step.due(dve))
            dve.memset(flat(ST[0]), 0.0)\
               .then_inc(vector_step.sem, 1)
            dve.wait_ge(vector_step.sem, vector_step.due(dve))
            for t in range(TT):
                here = slice(t * P, t * P + P)
                pad = PAD.rearrange("p (k e) t -> p k e t", e=4)
                for n, x in ((0, KKD), (2, R)):
                    for e in range(2):
                        sig = tile_operands if (n, e) == (2, 1) else vector_step
                        dve.tensor_scalar(pad[:, :, n + e, :], x[:, :, here], half[:, e:e + 1], None,
                            ALU.mult)\
                           .then_inc(sig.sem, 1)
                        dve.wait_ge(sig.sem, sig.due(dve))
                dve.tensor_copy(XT, over(ident, 16, P))\
                   .then_inc(vector_step.sem, 1)
                dve.wait_ge(vector_step.sem, vector_step.due(dve))
                for h in range(0, 16, 4):
                    bank, full, free = vbanks.empty()
                    dve.wait_ge(full.sem, full.due(dve))
                    dve.tensor_tensor(AN[:, h:h + 4, :], bank.rearrange("p (a b) -> p a b", a=4),
                        over(const("neg_strict"), 4, P), ALU.mult)\
                       .then_inc(free.sem, 1)
                    dve.wait_ge(free.sem, free.due(dve))
                dve.nop().then_inc(a_ready.sem, 1)
                for h in range(0, 16, 4):
                    bank, full, free = vbanks.empty()
                    dve.wait_ge(full.sem, full.due(dve))
                    dve.tensor_tensor(BT[:, h:h + 4, :], bank.rearrange("p (a b) -> p a b", a=4),
                        over(const("before"), 4, P), ALU.mult)\
                       .then_inc(free.sem, 1)
                    dve.wait_ge(free.sem, free.due(dve))
                for level in range(6):
                    mask = over(const(f"level{level}"), 4, P).bitcast(I32)
                    for h in range(0, 16, 4):
                        bank, full, free = vbanks.empty()
                        dve.wait_ge(full.sem, full.due(dve))
                        dve.copy_predicated(XT[:, h:h + 4, :], mask, bank.rearrange("p (a b) -> p a b",
                            a=4))\
                           .then_inc(free.sem, 1)
                        dve.wait_ge(free.sem, free.due(dve))
                        dve.nop().then_inc(inverse_ready.sem, 1)
                for h in range(0, 2):
                    bank, full, free = vbanks.empty()
                    dve.wait_ge(full.sem, full.due(dve))
                    dve.tensor_copy(BVT[:, h * 512:h * 512 + 512], bank)\
                       .then_inc(free.sem, 1)
                    dve.wait_ge(free.sem, free.due(dve))
                dve.nop().then_inc(bv_ready.sem, 1)
                for h in range(0, 4):
                    bank, full, free = vbanks.empty()
                    dve.wait_ge(full.sem, full.due(dve))
                    halves_v(WT[:, 2 * h:2 * h + 2, :], bank, free)
                for h in range(0, 2):
                    bank, full, free = vbanks.empty()
                    dve.wait_ge(full.sem, full.due(dve))
                    dve.tensor_copy(ZT[:, h * 512:h * 512 + 512], bank)\
                       .then_inc(free.sem, 1)
                    dve.wait_ge(free.sem, free.due(dve))
                for x in (XX, QQ):
                    for h in range(0, 16, 4):
                        bank, full, free = vbanks.empty()
                        dve.wait_ge(full.sem, full.due(dve))
                        dve.tensor_tensor(x[:, h:h + 4, :], bank.rearrange("p (a b) -> p a b", a=4),
                            over(const("upto"), 4, P), ALU.mult)\
                           .then_inc(free.sem, 1)
                        dve.wait_ge(free.sem, free.due(dve))
                dve.nop().then_inc(w_ready.sem, 1)
                for c in range(2):
                    dve.nop().then_inc(state_ready.sem, 1)
                    rows = slice(0, P) if c == 0 else slice(CH, P)
                    for k in range(2):
                        bank, full, free = vbanks.empty()
                        dve.wait_ge(full.sem, full.due(dve))
                        at = slice(k * 512, k * 512 + 512)
                        dve.scalar_tensor_tensor(UT[rows, at], bank[rows], -1.0, ZT[rows, at], ALU.mult,
                            ALU.subtract)\
                           .then_inc(free.sem, 1)
                        dve.wait_ge(free.sem, free.due(dve))
                    dve.nop().then_inc(u_ready.sem, 1)
                    if c == 1:
                        for k in range(0, DK, 2):
                            bank, full, free = vbanks.empty()
                            dve.wait_ge(full.sem, full.due(dve))
                            halves_v(R[:, k:k + 2, here], bank, free)
                    if (t, c) != (TT - 1, 1):
                        g = 2 * t + c
                        for k in range(0, DK, 4):
                            bank, full, free = vbanks.empty()
                            dve.wait_ge(full.sem, full.due(dve))
                            new = ST[1 - c][:, k:k + 4, :]
                            dve.tensor_tensor(new, bank.rearrange("p (a b) -> p a b", a=4), over(ones64,
                                4, P), ALU.mult)\
                               .then_inc(free.sem, 1)
                            dve.wait_ge(free.sem, free.due(dve))
                            dve.tensor_tensor(new, new, ST[c][:, k:k + 4, :], ALU.add)\
                               .then_inc(vector_step.sem, 1)
                            dve.wait_ge(vector_step.sem, vector_step.due(dve))
                            dve.tensor_tensor(new, new, ECEND[:, k:k + 4, g:g + 1].to_broadcast([P, 4,
                                P]), ALU.mult)\
                               .then_inc(vector_step.sem, 1)
                            dve.wait_ge(vector_step.sem, vector_step.due(dve))
            dve.nop().then_inc(head_squares.sem, 1)
            dve.wait_ge(head_squares.sem, head_squares.due(dve))
            for k in range(0, DK, 2):
                bank, full, free = vbanks.empty()
                dve.wait_ge(full.sem, full.due(dve))
                dve.scalar_tensor_tensor(flat(R[:, k:k + 2, :]), bank, -1.0 / 64, flat(R[:, k:k + 2,
                    :]), ALU.mult, ALU.add)\
                   .then_inc(free.sem, 1)
                dve.wait_ge(free.sem, free.due(dve))
            dve.tensor_tensor(SQT, R, R, ALU.mult)\
               .then_inc(head_squares.sem, 1)
            dve.wait_ge(head_squares.sem, head_squares.due(dve))
            dve.wait_ge(head_rms.sem, head_rms.due(dve))
            dve.tensor_tensor(R, R, RST, ALU.mult)\
               .then_inc(vector_step.sem, 1)
            dve.wait_ge(vector_step.sem, vector_step.due(dve))
            for k in range(DK):
                dve.tensor_scalar(R[:, k, :], R[:, k, :], col(n2("rwkv_ln_w"), k), col(n2("rwkv_ln_b"),
                    k), ALU.mult, ALU.add)\
                   .then_inc(vector_step.sem, 1)
                dve.wait_ge(vector_step.sem, vector_step.due(dve))
            dve.tensor_tensor(R, R, BONUS, ALU.add)\
               .then_inc(vector_step.sem, 1)
            dve.wait_ge(vector_step.sem, vector_step.due(dve))
            dve.wait_ge(evicted[0].sem, halves(0, j["rz2"]))
            dve.wait_ge(evicted[1].sem, halves(1, j["rz2"]))
            dve.tensor_tensor(R, R, ZR, ALU.mult)\
               .then_inc(branch_ready.sem, 1)
            dve.wait_ge(branch_ready.sem, branch_ready.due(dve))
            dve.wait_ge(evicted[0].sem, halves(0, j["gb2"]))
            dve.wait_ge(evicted[1].sem, halves(1, j["gb2"]))
            merge_v(j["ro"], TMP, 8 * l)
            dve.nop().then_inc(merged_rwkv.sem, 1)

        def gla_v(j, l):
            n2 = lambda n: f"{n}_2/{l}"
            dve.wait_ge(evicted[0].sem, halves(0, j["gl"]))
            dve.wait_ge(evicted[1].sem, halves(1, j["gl"]))
            for h in range(0, 4, 2):
                bank, full, free = vbanks.empty()
                dve.wait_ge(full.sem, full.due(dve))
                dve.tensor_tensor(GX[:, h:h + 2, :], bank.rearrange("p (a b) -> p a b", a=2),
                    along(col(n2("gla_b"), h, 2), 2, T), ALU.add)\
                   .then_inc(free.sem, 1)
                dve.wait_ge(free.sem, free.due(dve))
            dve.scalar_tensor_tensor(flat(GE), flat(GX), -1.0, flat(GX), ALU.mult, ALU.min)\
               .then_inc(gate_in.sem, 1)
            dve.wait_ge(gate_in.sem, gate_in.due(dve))
            dve.wait_ge(gate_out.sem, gate_out.due(dve))
            dve.scalar_tensor_tensor(GX, GX, 0.0, GE, ALU.min, ALU.subtract)\
               .then_inc(vector_step.sem, 1)
            dve.wait_ge(vector_step.sem, vector_step.due(dve))
            for h in range(4):
                dve.tensor_tensor_scan(GC[:, h, :], const("run"), GX[:, h, :], 0.0, ALU.mult, ALU.add)\
                   .then_inc(vector_step.sem, 1)
                dve.wait_ge(vector_step.sem, vector_step.due(dve))
            c4 = flat(GC).rearrange("p (c t) -> p c t", t=CH)
            dve.tensor_tensor(flat(GD).rearrange("p (c t) -> p c t", t=CH), c4[:, :,
                CH - 1:CH].to_broadcast([P, 16, CH]), c4, ALU.subtract)\
               .then_inc(gla_sums.sem, 1)
            dve.wait_ge(gla_sums.sem, gla_sums.due(dve))
            dve.wait_ge(gla_exps.sem, gla_exps.due(dve))
            dve.wait_ge(evicted[0].sem, halves(0, j["gk"]))
            dve.wait_ge(evicted[1].sem, halves(1, j["gk"]))
            dve.scalar_tensor_tensor(GX, GQ, 128 ** -0.5, GE, ALU.mult, ALU.mult)\
               .then_inc(vector_step.sem, 1)
            dve.wait_ge(vector_step.sem, vector_step.due(dve))
            dve.tensor_tensor(KINV, GK, GY, ALU.mult)\
               .then_inc(vector_step.sem, 1)
            dve.wait_ge(vector_step.sem, vector_step.due(dve))
            dve.tensor_tensor(KTE, GK, GD, ALU.mult)\
               .then_inc(gla_operands.sem, 1)
            dve.wait_ge(gla_operands.sem, gla_operands.due(dve))
            dve.wait_ge(evicted[0].sem, halves(0, j["gv"]))
            dve.wait_ge(evicted[1].sem, halves(1, j["gv"]))
            for t in range(TT):
                here = slice(t * P, t * P + P)
                bank, full, free = vbanks.empty()
                dve.wait_ge(full.sem, full.due(dve))
                dve.tensor_tensor(AT, bank.rearrange("p (a b) -> p a b", a=4), over(const("upto"), 4,
                    P), ALU.mult)\
                   .then_inc(free.sem, 1)
                dve.wait_ge(free.sem, free.due(dve))
                for c in range(2):
                    g = 2 * t + c
                    if g == 3:
                        continue
                    for h in range(0, 4, 2):
                        bank, full, free = vbanks.empty()
                        dve.wait_ge(full.sem, full.due(dve))
                        for n in range(2):
                            b = bank[:, n * T:n * T + T]
                            if g == 0:
                                sig = free if n else vector_step
                                dve.tensor_copy(GS[1][:, h + n, :], b)\
                                   .then_inc(sig.sem, 1)
                                dve.wait_ge(sig.sem, sig.due(dve))
                            else:
                                sig = free if n else vector_step
                                dve.scalar_tensor_tensor(GS[g + 1][:, h + n, :], GS[g][:, h + n, :],
                                    EL[:, (h + n) * 4 + g:(h + n) * 4 + g + 1], b, ALU.mult, ALU.add)\
                                   .then_inc(sig.sem, 1)
                                dve.wait_ge(sig.sem, sig.due(dve))
                dve.nop().then_inc(gla_states.sem, 1)
                for h in range(0, 4, 2):
                    bank, full, free = vbanks.empty()
                    dve.wait_ge(full.sem, full.due(dve))
                    dve.tensor_copy(OG[:, 2 * h:2 * h + 4, here], bank.rearrange("p (a b) -> p a b", a=4))\
                       .then_inc(free.sem, 1)
                    dve.wait_ge(free.sem, free.due(dve))
            norm_v(OG, SQG, 2, lambda k: col(n2("gla_norm"), k % 2), OG, 4)
            dve.wait_ge(evicted[0].sem, halves(0, j["gz"]))
            dve.wait_ge(evicted[1].sem, halves(1, j["gz"]))
            dve.tensor_tensor(OG, OG, GZ, ALU.mult)\
               .then_inc(branch_ready.sem, 1)
            dve.wait_ge(branch_ready.sem, branch_ready.due(dve))
            dve.wait_ge(evicted[0].sem, halves(0, j["gc"]))
            dve.wait_ge(evicted[1].sem, halves(1, j["gc"]))
            merge_v(j["go"], TMPG, 8 * l + 4)

        @block.vector
        def _(_v):
            for _, _, free in vbanks.banks:
                dve.nop().then_inc(free.sem, 1)
                free.due(dve)
            take_in_v()
            rec_v()
            ffn_v(0)
            bank, full, free = vbanks.empty()
            dve.wait_ge(full.sem, full.due(dve))
            dve.tensor_copy(cols[:, FIRST_PACKS * P:], bank[:, 0:(PACKS - FIRST_PACKS) * P])\
               .then_inc(free.sem, 1)
            dve.wait_ge(free.sem, free.due(dve))
            attention_v()
            ffn_v(1)
            dve.wait_ge(evicted[0].sem, halves(0, ffn_down[1]))
            dve.wait_ge(evicted[1].sem, halves(1, ffn_down[1]))
            dve.memset(WL[:, 0:1], 0.0)\
               .then_inc(vector_step.sem, 1)
            dve.wait_ge(vector_step.sem, vector_step.due(dve))
            dve.nop().then_inc(second_begins.sem, 1)
            for l in range(2):
                j = second[l]
                n2 = lambda n: f"{n}_2/{l}"
                MOD = MODS[l]
                dve.wait_ge(modulation_summed.sem, l + 1)
                dve.tensor_tensor(MOD, MOD, col(n2("ada_b"), 0, 24), ALU.add)\
                   .then_inc(vector_step.sem, 1)
                dve.wait_ge(vector_step.sem, vector_step.due(dve))
                dve.scalar_tensor_tensor(GPRE, MOD[:, 8:16], 1.0, col(n2("norm_pre"), 0, 8), ALU.add,
                    ALU.mult)\
                   .then_inc(vector_step.sem, 1)
                dve.wait_ge(vector_step.sem, vector_step.due(dve))
                dve.tensor_tensor(GPOST, MOD[:, 16:24], col(n2("norm_post"), 0, 8), ALU.mult)\
                   .then_inc(vector_step.sem, 1)
                dve.wait_ge(vector_step.sem, vector_step.due(dve))
                norm_v(X, SQM, DK, lambda k: GPRE[:, k:k + 1], H, shift=True, squared=l == 1)
                mla_v(j, l)
                rwkv_v(j, l)
                gla_v(j, l)
                dve.nop().then_inc(merge_ready.sem, 1)
                dve.wait_ge(evicted[0].sem, halves(0, j["out"]))
                dve.wait_ge(evicted[1].sem, halves(1, j["out"]))
                squares_v(QN, SQM, DK)
                dve.wait_ge(rms_ready.sem, rms_ready.due(dve))
                for k in range(0, DK, 2):
                    for n in range(2):
                        dve.scalar_tensor_tensor(QN[:, k + n, :], QN[:, k + n, :], GPOST[:, k + n:k + n + 1],
                            STAT[:, 0, :], ALU.mult, ALU.mult)\
                           .then_inc(scaled_out.sem, 1)
                    dve.wait_ge(scaled_out.sem, scaled_out.due(dve, 2))
                    dve.tensor_tensor(X[:, k:k + 2, :], X[:, k:k + 2, :], QN[:, k:k + 2, :], ALU.add)\
                       .then_inc(x_ready.sem, 1)
                    dve.wait_ge(x_ready.sem, x_ready.due(dve))
                    if l == 0:
                        dve.tensor_tensor(SQM[:, k:k + 2, :], X[:, k:k + 2, :], X[:, k:k + 2, :], ALU.mult)\
                           .then_inc(squares_ready.sem, 1)
                        dve.wait_ge(squares_ready.sem, squares_ready.due(dve))

        def take_in_act():
            act.dma_start(cst, A["const"]).then_inc(inputs_landed.sem, 16)
            act.dma_start(XIN, A["x"][0].rearrange("(t p) d -> p t d", p=P)).then_inc(inputs_landed.sem, 16)
            act.wait_ge(packs_zeroed.sem, packs_zeroed.due(act))
            for name, (pack, row, n) in first_vectors.items():
                src = rows_of(name)
                if src.shape[0] == 64:
                    for e in range(2):
                        act.dma_start(PACK[row:row + 1, pack, 64 * e:64 * e + 64], src.rearrange("(a b) -> a b", a=1)).then_inc(inputs_landed.sem, 16)
                else:
                    act.dma_start(PACK[row:row + n, pack, :], src.rearrange("(a b) -> a b", b=P)).then_inc(inputs_landed.sem, 16)
            for n, name in enumerate(("ssd_dt_bias", "ssd_a_log", "ssd_d")):
                act.dma_start(AROW[:, n, :], A[name][0].partition_broadcast(P)).then_inc(rows_landed.sem, 16)
            act.wait_ge(lru_weights_zeroed.sem, lru_weights_zeroed.due(act))
            for n, name in enumerate(("lru_w_r", "lru_w_i")):
                w = A[name][0].rearrange("(k e) i j -> e i k j", e=2)
                for e in range(2):
                    act.dma_start(BD[64 * e:64 * e + 64, n, :, 64 * e:64 * e + 64], w[e]).then_inc(lru_weights_landed.sem, 16)

        def rec_act():
            act.wait_ge(biases_set.sem, biases_set.due(act))
            rms_act(D)
            softplus_act(LAMA)
            act.wait_ge(rows_landed.sem, rows_landed.due(act, 48))
            act.activation(AROW[:, 1, :], AROW[:, 1, :], ACT.Exp)\
               .then_inc(a_exp.sem, 1)
            act.wait_ge(a_exp.sem, a_exp.due(act))
            evict(act, rec_dt, lambda i, bank, done, rounds:
                  act.activation(DT[:, :, 8 * i:8 * i + 8], bank[:, :, 0:8], ACT.Copy).then_inc(done, 1))
            softplus_act(flat(DTB))
            act.wait_ge(conv_fronts_zeroed.sem, conv_fronts_zeroed.due(act))
            evict(act, rec_x, keep(LX, ACT.Copy, 3))
            evict(act, rec_xbc, keep(XB, ACT.Copy, 3))
            for k in range(DK):
                bank, full, free = abanks.empty()
                act.wait_ge(full.sem, full.due(act))
                act.activation(RG[:, k, :], bank[:, 0:T], ACT.Sigmoid, bias=col("lru_b_r", k))\
                   .then_inc(scalar_step.sem, 1)
                act.wait_ge(scalar_step.sem, scalar_step.due(act))
                act.activation(IG[:, k, :], bank[:, T:], ACT.Sigmoid, bias=col("lru_b_i", k))\
                   .then_inc(free.sem, 1)
                act.wait_ge(free.sem, free.due(act))
            act.nop().then_inc(lru_gates.sem, 1)
            act.wait_ge(rate_ready.sem, rate_ready.due(act))
            act.activation(flat(LRU_A), flat(RG), ACT.Exp, scale=-1.0)\
               .then_inc(scalar_step.sem, 1)
            act.wait_ge(scalar_step.sem, scalar_step.due(act))
            act.activation(flat(RG), flat(RG), ACT.Tanh)\
               .then_inc(lru_functions.sem, 1)
            act.wait_ge(lru_functions.sem, lru_functions.due(act))
            act.wait_ge(lru_root_in.sem, lru_root_in.due(act))
            act.activation(flat(UU), flat(UU), ACT.Sqrt)\
               .then_inc(lru_root.sem, 1)
            act.wait_ge(lru_root.sem, lru_root.due(act))
            evict(act, rec_gate, keep(G, ACT.Gelu_apprx_tanh))
            act.wait_ge(ssd_conv_done.sem, ssd_conv_done.due(act))
            act.activation(flat(XBC), flat(XBC), ACT.Silu)\
               .then_inc(xbc_ready.sem, 1)
            act.wait_ge(xbc_ready.sem, xbc_ready.due(act))
            act.activation(CA, col("c_2", 0, 8), ACT.Silu)\
               .then_inc(condition_ready.sem, 1)
            act.wait_ge(condition_ready.sem, condition_ready.due(act))
            evict(act, rec_z[0], keep(Z, ACT.Silu))
            for t in range(TT):
                act.wait_ge(decay_in.sem, decay_in.due(act))
                act.activation(flat(SEG), flat(SEG), ACT.Exp)\
                   .then_inc(scalar_step.sem, 1)
                act.wait_ge(scalar_step.sem, scalar_step.due(act))
                if t == 0:
                    act.activation(LAST, LAST, ACT.Exp)\
                       .then_inc(decay_out.sem, 1)
                    act.wait_ge(decay_out.sem, decay_out.due(act))
                else:
                    act.activation(flat(ECS), flat(ECS), ACT.Exp)\
                       .then_inc(decay_out.sem, 1)
                    act.wait_ge(decay_out.sem, decay_out.due(act))
                evict(act, rec_z[1 + t], keep(Z[:, 4 + 2 * t:6 + 2 * t, :], ACT.Silu))
            rms_act(512, 2)

        def modulation_act(l):
            bank, full, free = abanks.empty()
            act.wait_ge(full.sem, full.due(act))
            act.activation(MODS[l], bank[:, 0:24], ACT.Copy)\
               .then_inc(free.sem, 1)
            act.wait_ge(free.sem, free.due(act))
            act.nop().then_inc(modulation_summed.sem, 1)

        def att_act():
            rms_act(D)
            evict(act, att_q, keep(Q, ACT.Copy))
            evict(act, att_k, keep(K, ACT.Copy))
            for part in range(2):
                for k in range(0, DK, 2):
                    bank, full, free = abanks.empty()
                    act.wait_ge(full.sem, full.due(act))
                    act.activation(flat(RS[:, k:k + 2, :]), bank, ACT.Ln, bias=biases[:, 0:1],
                        scale=1.0 / 64)\
                       .then_inc(free.sem, 1)
                    act.wait_ge(free.sem, free.due(act))
                act.activation(flat(RS), flat(RS), ACT.Exp, scale=-0.5)\
                   .then_inc(head_rms.sem, 1)
                act.wait_ge(head_rms.sem, head_rms.due(act))
                evict(act, att_v[part], keep_tokens(VT[:, :, part * 512:part * 512 + 512]))
                act.wait_ge(head_normed.sem, head_normed.due(act))
            attend_act(16, SC, PR, PT, MX, SM)

        def keep_one(dst):
            return lambda i, bank, done, rounds: act.activation(dst, bank[0:dst.shape[0], 0, :], ACT.Copy).then_inc(done, 1)

        def mla_act(j, l):
            evict(act, j["cq"], keep(CQ, ACT.Copy))
            evict(act, j["ckv"], keep(CKV, ACT.Copy))
            evict(act, j["kr"], keep_one(KR[:, 0, :]))
            evict(act, j["wl"], keep_one(WL[:, 1:]))
            evict(act, j["gl"], keep_one(GL[0:16, :]))
            rms_act(512)
            rms_act(256, row=1)
            evict(act, j["mz"], keep(ZM, ACT.Silu))
            evict(act, j["ga"], keep(GT, ACT.Sigmoid))
            if l == 0:
                act.wait_ge(angles_ready.sem, angles_ready.due(act))
                act.activation(SIN, ANG[:, 1, :], ACT.Sin)\
                   .then_inc(scalar_step.sem, 1)
                act.wait_ge(scalar_step.sem, scalar_step.due(act))
                act.activation(COS, ANG[:, 2, :], ACT.Sin)\
                   .then_inc(tables_ready.sem, 1)
                act.wait_ge(tables_ready.sem, tables_ready.due(act))
            evict(act, j["uqn"], keep(QN, ACT.Copy))
            evict(act, j["uqr"], keep(QR, ACT.Copy))
            evict(act, j["ukn"], keep(KN, ACT.Copy))
            evict(act, j["ukv"], keep_tokens(VM))
            attend_act(8, MSC, MPR, MPT, MMX, MSM)

        def rwkv_act(j, l):
            n2 = lambda n: f"{n}_2/{l}"
            act.wait_ge(lora_zeroed.sem, lora_zeroed.due(act))
            act.dma_start(flat(W2)[0:64, 0:D], A["rwkv_w2_2"][l]).then_inc(lora_weights.sem, 16)
            act.dma_start(flat(W2)[64:128, D:2 * D], A["rwkv_a2_2"][l]).then_inc(lora_weights.sem, 16)
            act.wait_ge(fronts_zeroed.sem, fronts_zeroed.due(act))
            act.wait_ge(lora_mixed.sem, lora_mixed.due(act))
            act.activation(WL[0:64, 1:], WL[0:64, 1:], ACT.Tanh)\
               .then_inc(lora_ready.sem, 1)
            act.wait_ge(lora_ready.sem, lora_ready.due(act))
            evict(act, j["k"], keep(raw[0], ACT.Copy, 1))
            for k in range(DK):
                bank, full, free = abanks.empty()
                act.wait_ge(full.sem, full.due(act))
                act.activation(SW[:, k, :], bank[:, 0:T], ACT.Sigmoid, bias=col(n2("rwkv_w0"), k))\
                   .then_inc(scalar_step.sem, 1)
                act.wait_ge(scalar_step.sem, scalar_step.due(act))
                act.activation(AA[:, k, :], bank[:, T:], ACT.Sigmoid, bias=col(n2("rwkv_a0"), k))\
                   .then_inc(free.sem, 1)
                act.wait_ge(free.sem, free.due(act))
            act.nop().then_inc(lora_gates.sem, 1)
            evict(act, j["r"], keep(raw[1], ACT.Copy, 1))
            for k in range(0, DK, 2):
                bank, full, free = abanks.empty()
                act.wait_ge(full.sem, full.due(act))
                act.activation(flat(SQR[:, k:k + 2, :]), bank, ACT.Sqrt)\
                   .then_inc(free.sem, 1)
                act.wait_ge(free.sem, free.due(act))
            act.nop().then_inc(head_rms.sem, 1)
            act.wait_ge(head_rms.sem, head_rms.due(act))
            act.wait_ge(cumulated.sem, cumulated.due(act))
            act.activation(flat(E1), flat(CC), ACT.Exp, scale=-KAPPA)\
               .then_inc(scalar_step.sem, 1)
            act.wait_ge(scalar_step.sem, scalar_step.due(act))
            act.activation(flat(E2), flat(CC), ACT.Exp, scale=KAPPA)\
               .then_inc(scalar_step.sem, 1)
            act.wait_ge(scalar_step.sem, scalar_step.due(act))
            act.activation(flat(SW), flat(SW), ACT.Exp, scale=-KAPPA)\
               .then_inc(decays.sem, 1)
            act.wait_ge(decays.sem, decays.due(act))
            evict(act, j["v"], keep(raw[2], ACT.Copy, 1))
            act.wait_ge(evicted[0].sem, halves(0, j["mo"]))
            act.wait_ge(evicted[1].sem, halves(1, j["mo"]))
            evict(act, j["gb0"], keep(GT, ACT.Sigmoid))
            for t in range(TT):
                for x in (VTK, KKT):
                    for n in range(2):
                        bank, full, free = abanks.empty()
                        act.wait_ge(full.sem, full.due(act))
                        act.activation(x[:, n * 512:n * 512 + 512], bank, ACT.Copy)\
                           .then_inc(free.sem, 1)
                        act.wait_ge(free.sem, free.due(act))
                for x in (KDT, BDT):
                    for n in range(2):
                        bank, full, free = abanks.empty()
                        act.wait_ge(full.sem, full.due(act))
                        for c in range(2):
                            sig = free if c else scalar_step
                            act.activation(x[c][:, n * 512:n * 512 + 512], bank, ACT.Copy, scale=half[:,
                                c:c + 1])\
                               .then_inc(sig.sem, 1)
                            act.wait_ge(sig.sem, sig.due(act))
                act.nop().then_inc(token_major.sem, 1)
                for level in range(1, 6):
                    for h in range(0, 16, 4):
                        bank, full, free = abanks.empty()
                        act.wait_ge(full.sem, full.due(act))
                        act.activation(flat(XX[:, h:h + 4, :]), bank, ACT.Copy)\
                           .then_inc(free.sem, 1)
                        act.wait_ge(free.sem, free.due(act))
                    for h in range(0, 16, 4):
                        bank, full, free = abanks.empty()
                        act.wait_ge(full.sem, full.due(act))
                        act.activation(flat(QQ[:, h:h + 4, :]), bank, ACT.Copy)\
                           .then_inc(free.sem, 1)
                        act.wait_ge(free.sem, free.due(act))
                        act.nop().then_inc(level_operands.sem, 1)
                if t == 0:
                    evict(act, j["gb1"], keep(GT[:, 4:], ACT.Sigmoid))
                    evict(act, j["gb2"], keep(GT[:, 6:], ACT.Sigmoid))
            for n, at in (("rz0", 0), ("rz1", 4), ("rz2", 6)):
                evict(act, j[n], keep(ZR[:, at:], ACT.Silu))
            for k in range(0, DK, 2):
                bank, full, free = abanks.empty()
                act.wait_ge(full.sem, full.due(act))
                act.activation(flat(RST[:, k:k + 2, :]), bank, ACT.Ln, bias=biases[:, 1:2],
                    scale=1.0 / 64)\
                   .then_inc(free.sem, 1)
                act.wait_ge(free.sem, free.due(act))
            act.activation(flat(RST), flat(RST), ACT.Exp, scale=-0.5)\
               .then_inc(head_rms.sem, 1)
            act.wait_ge(head_rms.sem, head_rms.due(act))

        def gla_act(j, l):
            act.dma_start(G2[0:16, :], A["gla_w2_2"][l]).then_inc(lora_weights.sem, 16)
            evict(act, j["gq"], keep(GQ, ACT.Copy))
            evict(act, j["gk"], keep(GK, ACT.Copy))
            act.wait_ge(evicted[0].sem, halves(0, j["ro"]))
            act.wait_ge(evicted[1].sem, halves(1, j["ro"]))
            act.wait_ge(merged_rwkv.sem, merged_rwkv.due(act))
            act.wait_ge(gate_in.sem, gate_in.due(act))
            act.activation(flat(GE), flat(GE), ACT.Exp)\
               .then_inc(scalar_step.sem, 1)
            act.wait_ge(scalar_step.sem, scalar_step.due(act))
            act.activation(flat(GE), flat(GE), ACT.Ln, bias=biases[:, 2:3])\
               .then_inc(gate_out.sem, 1)
            act.wait_ge(gate_out.sem, gate_out.due(act))
            act.wait_ge(gla_sums.sem, gla_sums.due(act))
            act.activation(flat(GE), flat(GC), ACT.Exp, scale=1.0 / 16)\
               .then_inc(scalar_step.sem, 1)
            act.wait_ge(scalar_step.sem, scalar_step.due(act))
            act.activation(flat(GY), flat(GC), ACT.Exp, scale=-1.0 / 16)\
               .then_inc(scalar_step.sem, 1)
            act.wait_ge(scalar_step.sem, scalar_step.due(act))
            act.activation(flat(GD), flat(GD), ACT.Exp, scale=1.0 / 16)\
               .then_inc(scalar_step.sem, 1)
            act.wait_ge(scalar_step.sem, scalar_step.due(act))
            act.activation(EL, flat(GC).rearrange("p (c t) -> p c t", t=CH)[:, :, CH - 1], ACT.Exp,
                scale=1.0 / 16)\
               .then_inc(gla_exps.sem, 1)
            act.wait_ge(gla_exps.sem, gla_exps.due(act))
            evict(act, j["gv"], keep_tokens(GV))
            evict(act, j["gz"], keep(GZ, ACT.Silu))
            for t in range(TT):
                bank, full, free = abanks.empty()
                act.wait_ge(full.sem, full.due(act))
                for c in range(2):
                    sig = free if c else scalar_step
                    act.activation(flat(KTT[c]), bank, ACT.Copy, scale=half[:, c:c + 1])\
                       .then_inc(sig.sem, 1)
                    act.wait_ge(sig.sem, sig.due(act))
                act.nop().then_inc(token_major.sem, 1)
            rms_act(256, 4)
            evict(act, j["gc"], keep(GT, ACT.Sigmoid))

        @block.scalar
        def _(_a):
            for _, _, free in abanks.banks:
                act.nop().then_inc(free.sem, 1)
                free.due(act)
            take_in_act()
            rec_act()
            ffn_act(0)
            att_act()
            modulation_act(0)
            ffn_act(1)
            modulation_act(1)
            act.wait_ge(second_begins.sem, second_begins.due(act))
            act.dma_start(ANG[:, 3, :].bitcast(I32), A["positions_2"][0].partition_broadcast(P)).then_inc(positions_landed.sem, 16)
            for l in range(2):
                j = second[l]
                rms_act(D)
                shift_act(H, DK, lambda k: MODS[l][:, k:k + 1])
                mla_act(j, l)
                rwkv_act(j, l)
                gla_act(j, l)
                evict(act, j["out"], keep(QN, ACT.Copy))
                rms_act(D)
            for k in range(0, DK, 2):
                bank, full, free = abanks.empty()
                act.wait_ge(full.sem, full.due(act))
                act.activation(XOUT[:, :, k * P:(k + 2) * P], bank.rearrange("p (t c) -> p t c", t=TT), ACT.Copy)\
                   .then_inc(free.sem, 1)
                act.wait_ge(free.sem, free.due(act))
                act.nop().then_inc(output_ready.sem, 1)

        @block.gpsimd
        def _(_p):
            gp = nc.gpsimd
            gp.memset(flat(PACK2), 0.0).then_inc(second_rows_zeroed.sem, 1)
            gp.wait_ge(second_rows_zeroed.sem, 1)
            for name, (pack, row, n) in second_vectors.items():
                gp.dma_start(PACK2[row:row + n, pack - FIRST_PACKS, :], rows_of(name).rearrange("(a b) -> a b", b=P)).then_inc(second_rows_landed.sem, 16)
            gp.wait_ge(condition_ready.sem, 1)
            for l in range(2):
                w = A["ada_w_2"][l].rearrange("(k p) n -> k p n", p=P)
                n = 3 * D // 2
                if l:
                    gp.wait_ge(modulation_summed.sem, l)
                gp.memset(flat(ADA_SUM), 0.0).then_inc(modulation_step.sem, 1)
                gp.wait_ge(modulation_step.sem, l + 1)
                for s in range(2):
                    gp.dma_start(ADA_W[:, s, :], w[0][:, s * n:s * n + n]).then_inc(ada_landed[s].sem, 16)
                for k in range(DK):
                    for s in range(2):
                        gp.wait_ge(ada_landed[s].sem, 16 * (l * DK + k + 1))
                        gp.tensor_scalar(ADA_W[:, s, :], ADA_W[:, s, :], CA[:, k:k + 1], None, ALU.mult)\
                          .then_inc(modulation_scaled.sem, 1)
                        gp.wait_ge(modulation_scaled.sem, (l * DK + k) * 2 + s + 1)
                        gp.tensor_tensor(ADA_SUM[:, s, :], ADA_SUM[:, s, :], ADA_W[:, s, :], ALU.add)\
                          .then_inc(ada_added[s].sem, 1)
                        gp.wait_ge(ada_added[s].sem, l * DK + k + 1)
                        if k < DK - 1:
                            gp.dma_start(ADA_W[:, s, :], w[k + 1][:, s * n:s * n + n]).then_inc(ada_landed[s].sem, 16)
                        else:
                            gp.nop().then_inc(modulation_products.sem, 1)

        @block.sync
        def _(_s):
            for j in first_jobs:
                if j in ffn_up:
                    load_up(ffn_up.index(j))
                elif j in ffn_down:
                    load_down(ffn_down.index(j))
                else:
                    load(j)
            for s in range(2):
                sp.wait_ge(product[s].sem, (ffn_down[1].at + ffn_down[1].n) // 2)
            for l in range(2):
                for j in second[l].values():
                    load(j)
            for n in range(2):
                here = slice(n * D // 2, (n + 1) * D // 2)
                sp.wait_ge(output_ready.sem, output_ready.due(sp, 2))
                sp.dma_start(out[0].rearrange("(t p) d -> p t d", p=P)[:, :, here], XOUT[:, :, here]).then_inc(output_written.sem, 16)
            sp.wait_ge(output_written.sem, 32)


NAMES = ["x", "rec_norm", "rec_w_in", "lru_conv_w", "lru_conv_b", "lru_w_r", "lru_b_r", "lru_w_i", "lru_b_i",
         "lru_lambda", "ssd_conv_w", "ssd_conv_b", "ssd_dt_bias", "ssd_a_log", "ssd_d", "ssd_norm", "rec_w_out",
         "att_norm", "att_w_qkv", "att_q_norm", "att_k_norm", "att_w_out", "ffn_norm", "ffn_w_gate_up",
         "ffn_w_down", "c_2", "positions_2", "ada_w_2", "ada_b_2", "norm_pre_2", "norm_post_2", "w_in_2",
         "rwkv_mu_2", "mla_q_norm_2", "mla_kv_norm_2", "mla_w_uq_2", "mla_w_ukv_2", "mla_w_o_2", "rwkv_w0_2",
         "rwkv_w2_2", "rwkv_a0_2", "rwkv_a2_2", "rwkv_k_k_2", "rwkv_k_a_2", "rwkv_r_k_2", "rwkv_ln_w_2",
         "rwkv_ln_b_2", "rwkv_w_o_2", "gla_w2_2", "gla_b_2", "gla_norm_2", "gla_w_o_2", "w_out_2"]


def kernel(**inputs):
    import numpy as _np
    import concourse.bacc as _bacc
    from concourse import mybir as _mybir
    from concourse.bass_utils import run_bass_kernel_spmd as _run

    nc = _bacc.Bacc("TRN2", target_bir_lowering=False, num_devices=1)
    arrays, args = {}, {}
    for name in NAMES + ["const"]:
        a = CONST if name == "const" else _np.ascontiguousarray(inputs[name])
        arrays[f"in_{name}"] = a
        args[name] = nc.dram_tensor(f"in_{name}", a.shape, _mybir.dt.from_np(a.dtype), kind="ExternalInput").ap()
    out = nc.dram_tensor("out_x", (1, T, D), F32, kind="ExternalOutput").ap()
    program(nc, args, out)
    r = _run(nc, [arrays], core_ids=[0])
    return r.results[0]["out_x"]
```
